# Optimizing a Trainium2 kernel written in Bass

```python
import jax, jax.numpy as jnp
from jax import lax
import numpy as np

D_MODEL = 1024
BATCH = 1
SEQ = 512
DEPTH = 1

GRID_W = 64
CTX_LEN = 256
D_FF = 2816
MACARON_WEIGHT = 0.5
S5_WIDTH = 512
S5_GROUP = 16
S5_GROUPS = S5_WIDTH // S5_GROUP
S5_STATE = 64
GLA_HEADS = 4
GLA_DK = 64
GLA_DV = 128
GLA_KEY = GLA_HEADS * GLA_DK
GLA_VAL = GLA_HEADS * GLA_DV
GLA_GATE_RANK = 16
GLA_GATE_NORM = 16.0
GLA_CHUNK = 64
N_DIR = 2
N_BRANCH = 2
N_MOD = 9
RMS_EPS = 1e-6
D_IN = S5_WIDTH + 2 * GLA_KEY + 2 * GLA_VAL + N_DIR * GLA_GATE_RANK + N_BRANCH * D_MODEL

kernel_name = 'hybrid_s5_gla_macaron_dit_layer'

f32 = jnp.float32

def rms_norm(x, g):
    xf = x.astype(f32)
    y = xf * lax.rsqrt(jnp.mean(xf * xf, axis=-1, keepdims=True) + RMS_EPS)
    return (y * g.astype(f32)).astype(x.dtype)

def modulate(h, shift, scale):
    return h * (1 + scale) + shift

def swiglu(h, w_gate, w_up, w_down):
    return (jax.nn.silu(h @ w_gate) * (h @ w_up)) @ w_down

def ffn_sublayer(t, shift, scale, gate, norm_g, w_gate, w_up, w_down):
    h = modulate(rms_norm(t, norm_g), shift, scale)
    return t + gate * (MACARON_WEIGHT * swiglu(h, w_gate, w_up, w_down))

def to_col_major(t, rows):
    b, l, ch = t.shape
    return t.reshape(b, rows, GRID_W, ch).swapaxes(1, 2).reshape(b, l, ch)

def from_col_major(t, rows):
    b, l, ch = t.shape
    return t.reshape(b, GRID_W, rows, ch).swapaxes(1, 2).reshape(b, l, ch)

def _linear_recurrence(e1, e2):
    a1, b1 = e1
    a2, b2 = e2
    return a1 * a2, a2 * b1 + b2

def s5_scan(bu, lam_bar, h0):
    bu = bu.at[:, 0].add(lam_bar * h0)
    a = jnp.broadcast_to(lam_bar, bu.shape)
    _, h = lax.associative_scan(_linear_recurrence, (a, bu), axis=1)
    return h

def s5_discretise(lam_re, lam_im, log_dt, b_re, b_im):
    lam = lax.complex(jnp.minimum(lam_re.astype(f32), -1e-4), lam_im.astype(f32))
    dt = jnp.exp(log_dt.astype(f32))[:, None]
    lam_bar = jnp.exp(lam * dt)
    b = lax.complex(b_re.astype(f32), b_im.astype(f32))
    b_bar = ((lam_bar - 1.0) / lam)[..., None] * b
    return lam_bar, b_bar

def s5_branch(u_lat, u_ctx, lam_re, lam_im, log_dt, b_re, b_im, c_re, c_im, d_skip, glu_w, glu_b, need_ctx):
    def grouped(u):
        b, l, _ = u.shape
        return u.astype(f32).reshape(b, l, S5_GROUPS, S5_GROUP)

    def finish(y, u):
        b, l = u.shape[:2]
        y = y.reshape(b, l, S5_WIDTH) + d_skip.astype(f32) * u.astype(f32)
        y = jax.nn.gelu(y)
        y = y * jax.nn.sigmoid(y @ glu_w.astype(f32) + glu_b.astype(f32))
        return y.astype(u.dtype)

    bsz = u_lat.shape[0]
    ul, uc = grouped(u_lat), grouped(u_ctx)
    y_l = jnp.zeros(ul.shape, f32)
    y_c = jnp.zeros(uc.shape, f32)
    for d in range(N_DIR):
        lam_bar, b_bar = s5_discretise(lam_re[d], lam_im[d], log_dt[d], b_re[d], b_im[d])
        c_mat = lax.complex(c_re[d].astype(f32), c_im[d].astype(f32))
        bu_l = jnp.einsum('blgc,gpc->blgp', ul.astype(jnp.complex64), b_bar)
        bu_c = jnp.einsum('blgc,gpc->blgp', uc.astype(jnp.complex64), b_bar)
        if d == 1:
            bu_l, bu_c = jnp.flip(bu_l, 1), jnp.flip(bu_c, 1)
        h_c = s5_scan(bu_c, lam_bar, jnp.zeros((bsz, S5_GROUPS, S5_STATE), jnp.complex64))
        h_l = s5_scan(bu_l, lam_bar, h_c[:, -1])
        r_l = jnp.einsum('blgp,gcp->blgc', h_l, c_mat).real
        y_l = y_l + (jnp.flip(r_l, 1) if d == 1 else r_l)
        if need_ctx:
            r_c = jnp.einsum('blgp,gcp->blgc', h_c, c_mat).real
            y_c = y_c + (jnp.flip(r_c, 1) if d == 1 else r_c)
    return finish(y_l, u_lat), (finish(y_c, u_ctx) if need_ctx else None)

def gla_chunked(q, k, v, g, s0):
    bsz, nh, l, dk = q.shape
    dv = v.shape[-1]
    n = l // GLA_CHUNK
    q, k, g = [t.reshape(bsz, nh, n, GLA_CHUNK, dk) for t in (q, k, g)]
    v = v.reshape(bsz, nh, n, GLA_CHUNK, dv)
    gc = jnp.cumsum(g, axis=3)
    g_ref = gc[:, :, :, GLA_CHUNK // 2:GLA_CHUNK // 2 + 1]
    g_last = gc[:, :, :, -1:]
    scores = jnp.einsum('bhnid,bhnjd->bhnij', q * jnp.exp(gc - g_ref), k * jnp.exp(g_ref - gc))
    upto_i = jnp.tril(jnp.ones((GLA_CHUNK, GLA_CHUNK), dtype=bool))
    scores = jnp.where(upto_i, scores, 0.0)
    o_intra = jnp.einsum('bhnij,bhnje->bhnie', scores, v)
    kv = jnp.einsum('bhnjd,bhnje->bhnde', k * jnp.exp(g_last - gc), v)
    decay = jnp.exp(g_last[:, :, :, 0])

    def step(s, inp):
        dec, kv_n = inp
        return dec[..., None] * s + kv_n, s

    s_final, s_start = lax.scan(step, s0, (jnp.moveaxis(decay, 2, 0), jnp.moveaxis(kv, 2, 0)))
    s_start = jnp.moveaxis(s_start, 0, 2)
    o_inter = jnp.einsum('bhnid,bhnde->bhnie', q * jnp.exp(gc), s_start)
    return (o_intra + o_inter).reshape(bsz, nh, l, dv), s_final

def gla_branch(q_l, k_l, v_l, r_l, glr_l, q_c, k_c, v_c, r_c, glr_c, gate_up, gate_b, norm_g, need_ctx):
    def heads(t, dh):
        b, l, _ = t.shape
        return t.astype(f32).reshape(b, l, GLA_HEADS, dh).transpose(0, 2, 1, 3)

    def log_decay(glr, d):
        z = glr[..., d * GLA_GATE_RANK:(d + 1) * GLA_GATE_RANK] @ gate_up[d] + gate_b[d]
        return heads(jax.nn.log_sigmoid(z.astype(f32)) / GLA_GATE_NORM, GLA_DK)

    def readout(o, r):
        o = o.transpose(0, 2, 1, 3)
        o = o * lax.rsqrt(jnp.mean(o * o, axis=-1, keepdims=True) + RMS_EPS)
        o = o * norm_g.astype(f32).reshape(GLA_HEADS, GLA_DV)
        b, l = o.shape[:2]
        return (o.reshape(b, l, GLA_VAL) * jax.nn.silu(r.astype(f32))).astype(r.dtype)

    scale = GLA_DK ** -0.5
    lat = (heads(q_l, GLA_DK) * scale, heads(k_l, GLA_DK), heads(v_l, GLA_DV))
    cx = (heads(q_c, GLA_DK) * scale, heads(k_c, GLA_DK), heads(v_c, GLA_DV))
    bsz = q_l.shape[0]
    o_l = jnp.zeros(lat[2].shape, f32)
    o_c = jnp.zeros(cx[2].shape, f32)
    for d in range(N_DIR):
        seq_l = lat + (log_decay(glr_l, d),)
        seq_c = cx + (log_decay(glr_c, d),)
        if d == 1:
            seq_l = tuple(jnp.flip(t, 2) for t in seq_l)
            seq_c = tuple(jnp.flip(t, 2) for t in seq_c)
        oc_d, s_ctx = gla_chunked(*seq_c, jnp.zeros((bsz, GLA_HEADS, GLA_DK, GLA_DV), f32))
        ol_d, _ = gla_chunked(*seq_l, s_ctx)
        o_l = o_l + (jnp.flip(ol_d, 2) if d == 1 else ol_d)
        if need_ctx:
            o_c = o_c + (jnp.flip(oc_d, 2) if d == 1 else oc_d)
    return readout(o_l, r_l), (readout(o_c, r_c) if need_ctx else None)

def token_mixing(h_lat, h_ctx, w_in, s5_lambda_re, s5_lambda_im, s5_log_dt, s5_b_re, s5_b_im, s5_c_re, s5_c_im,
                 s5_d, s5_glu_w, s5_glu_b, s5_out, gla_gate_up, gla_gate_b, gla_norm, gla_out, w_o, rows, need_ctx):
    sizes = (S5_WIDTH, GLA_KEY, GLA_KEY, GLA_VAL, GLA_VAL, N_DIR * GLA_GATE_RANK, D_MODEL, D_MODEL)
    points = np.cumsum(sizes)[:-1].tolist()
    u_l, q_l, k_l, v_l, r_l, glr_l, ga_l, gb_l = jnp.split(h_lat @ w_in, points, axis=-1)
    u_c, q_c, k_c, v_c, r_c, glr_c, ga_c, gb_c = jnp.split(h_ctx @ w_in, points, axis=-1)
    ya_l, ya_c = s5_branch(u_l, u_c, s5_lambda_re, s5_lambda_im, s5_log_dt, s5_b_re, s5_b_im,
                           s5_c_re, s5_c_im, s5_d, s5_glu_w, s5_glu_b, need_ctx)
    q_l, k_l, v_l, r_l, glr_l = [to_col_major(t, rows) for t in (q_l, k_l, v_l, r_l, glr_l)]
    yb_l, yb_c = gla_branch(q_l, k_l, v_l, r_l, glr_l, q_c, k_c, v_c, r_c, glr_c,
                            gla_gate_up, gla_gate_b, gla_norm, need_ctx)
    yb_l = from_col_major(yb_l, rows)

    def merge(ya, yb, ga, gb):
        return (jax.nn.sigmoid(ga) * (ya @ s5_out) + jax.nn.sigmoid(gb) * (yb @ gla_out)) @ w_o

    y_ctx = merge(ya_c, yb_c, ga_c, gb_c) if need_ctx else None
    return merge(ya_l, yb_l, ga_l, gb_l), y_ctx

def setup_inputs(seed: int = 0) -> dict:
    key = jax.random.key(seed)
    ks = iter(jax.random.split(key, 40))

    def nrm(shape, scale):
        return jax.random.normal(next(ks), shape, f32) * scale

    L, D, F = DEPTH, D_MODEL, D_FF
    G, P, C = S5_GROUPS, S5_STATE, S5_GROUP
    lam_im = jnp.broadcast_to(jnp.pi * jnp.arange(P, dtype=f32), (L, N_DIR, G, P)) + nrm((L, N_DIR, G, P), 0.01)
    log_dt = jax.random.uniform(next(ks), (L, N_DIR, G), f32, float(np.log(1e-3)), float(np.log(1e-1)))
    return {
        'x': nrm((BATCH, SEQ, D), 1.0),
        'c': nrm((BATCH, D), 1.0),
        'ctx': nrm((BATCH, CTX_LEN, D), 1.0),
        'c_ctx': nrm((D,), 1.0),
        'ada_w': nrm((L, D, N_MOD * D), D ** -0.5),
        'ada_b': nrm((L, N_MOD * D), 0.02),
        'ffn1_norm': 1.0 + nrm((L, D), 0.02),
        'ffn1_w_gate': nrm((L, D, F), D ** -0.5),
        'ffn1_w_up': nrm((L, D, F), D ** -0.5),
        'ffn1_w_down': nrm((L, F, D), F ** -0.5),
        'mix_norm': 1.0 + nrm((L, D), 0.02),
        'w_in': nrm((L, D, D_IN), D ** -0.5),
        's5_lambda_re': -0.5 + nrm((L, N_DIR, G, P), 0.01),
        's5_lambda_im': lam_im,
        's5_log_dt': log_dt,
        's5_b_re': nrm((L, N_DIR, G, P, C), (2 * C) ** -0.5),
        's5_b_im': nrm((L, N_DIR, G, P, C), (2 * C) ** -0.5),
        's5_c_re': nrm((L, N_DIR, G, C, P), (2 * P) ** -0.5),
        's5_c_im': nrm((L, N_DIR, G, C, P), (2 * P) ** -0.5),
        's5_d': nrm((L, S5_WIDTH), 1.0),
        's5_glu_w': nrm((L, S5_WIDTH, S5_WIDTH), S5_WIDTH ** -0.5),
        's5_glu_b': nrm((L, S5_WIDTH), 0.02),
        's5_out': nrm((L, S5_WIDTH, D), S5_WIDTH ** -0.5),
        'gla_gate_up': nrm((L, N_DIR, GLA_GATE_RANK, GLA_KEY), GLA_GATE_RANK ** -0.5),
        'gla_gate_b': nrm((L, N_DIR, GLA_KEY), 0.1),
        'gla_norm': 1.0 + nrm((L, GLA_VAL), 0.02),
        'gla_out': nrm((L, GLA_VAL, D), GLA_VAL ** -0.5),
        'w_o': nrm((L, D, D), D ** -0.5),
        'ffn2_norm': 1.0 + nrm((L, D), 0.02),
        'ffn2_w_gate': nrm((L, D, F), D ** -0.5),
        'ffn2_w_up': nrm((L, D, F), D ** -0.5),
        'ffn2_w_down': nrm((L, F, D), F ** -0.5),
        'final_norm': 1.0 + nrm((D,), 0.02),
    }

def reference(x, c, ctx, c_ctx, ada_w, ada_b, ffn1_norm, ffn1_w_gate, ffn1_w_up, ffn1_w_down, mix_norm, w_in,
              s5_lambda_re, s5_lambda_im, s5_log_dt, s5_b_re, s5_b_im, s5_c_re, s5_c_im, s5_d, s5_glu_w, s5_glu_b,
              s5_out, gla_gate_up, gla_gate_b, gla_norm, gla_out, w_o, ffn2_norm, ffn2_w_gate, ffn2_w_up,
              ffn2_w_down, final_norm):
    rows = x.shape[1] // GRID_W
    for i in range(DEPTH):
        last = i == DEPTH - 1
        ml = jnp.split((jax.nn.silu(c) @ ada_w[i] + ada_b[i])[:, None, :], N_MOD, axis=-1)
        mc = jnp.split((jax.nn.silu(c_ctx) @ ada_w[i] + ada_b[i])[None, None, :], N_MOD, axis=-1)
        x = ffn_sublayer(x, ml[0], ml[1], ml[2], ffn1_norm[i], ffn1_w_gate[i], ffn1_w_up[i], ffn1_w_down[i])
        ctx = ffn_sublayer(ctx, mc[0], mc[1], mc[2], ffn1_norm[i], ffn1_w_gate[i], ffn1_w_up[i], ffn1_w_down[i])
        h_lat = modulate(rms_norm(x, mix_norm[i]), ml[3], ml[4])
        h_ctx = modulate(rms_norm(ctx, mix_norm[i]), mc[3], mc[4])
        y_lat, y_ctx = token_mixing(h_lat, h_ctx, w_in[i], s5_lambda_re[i], s5_lambda_im[i], s5_log_dt[i],
                                    s5_b_re[i], s5_b_im[i], s5_c_re[i], s5_c_im[i], s5_d[i], s5_glu_w[i],
                                    s5_glu_b[i], s5_out[i], gla_gate_up[i], gla_gate_b[i], gla_norm[i],
                                    gla_out[i], w_o[i], rows, not last)
        x = x + ml[5] * y_lat
        x = ffn_sublayer(x, ml[6], ml[7], ml[8], ffn2_norm[i], ffn2_w_gate[i], ffn2_w_up[i], ffn2_w_down[i])
        if not last:
            ctx = ctx + mc[5] * y_ctx
            ctx = ffn_sublayer(ctx, mc[6], mc[7], mc[8], ffn2_norm[i], ffn2_w_gate[i], ffn2_w_up[i], ffn2_w_down[i])
    return rms_norm(x, final_norm)


_drawn_inputs = setup_inputs


def setup_inputs(seed=0):
    import zlib

    import numpy as np

    out = dict(_drawn_inputs(seed))
    spreads = {}
    factors = {'ffn1_norm': 7.55,
     'mix_norm': 5.651,
     's5_lambda_re': 64.0,
     's5_lambda_im': 26.904,
     's5_log_dt': 35.312,
     's5_b_re': 37.24,
     's5_b_im': 37.472,
     's5_c_re': 38.136,
     's5_c_im': 41.208,
     's5_glu_b': 200.0,
     'gla_gate_b': 3.466,
     'gla_norm': 27.009,
     'ffn2_norm': 25.507,
     'final_norm': 19.828,
     's5_glu_w': 2.881}
    for name, (base, spread) in spreads.items():
        noise = np.random.default_rng([zlib.crc32(name.encode()), seed]).standard_normal(out[name].shape)
        drawn = base * np.exp(spread * noise) if base else spread * noise
        out[name] = __import__('jax').numpy.asarray(drawn.astype(out[name].dtype))
    for name, factor in factors.items():
        out[name] = (out[name] * factor).astype(out[name].dtype)
    return out
```

```python
from contextlib import ExitStack
import math

import numpy as np
import concourse.bass as bass
from concourse import mybir

F32 = mybir.dt.float32
F32R = mybir.dt.float32r
I32 = mybir.dt.int32
ALU = mybir.AluOpType
ACT = mybir.ActivationFunctionType
AX = mybir.AxisListType

P = 128
D = 1024
KD = D // P
FF = 2816
NL, NC = 512, 256
NT = NL + NC
EPS = 1e-6
G, GC, SP5 = 32, 16, 64
W5 = G * GC
NDIR = 2
DG = NDIR * G
CH = 8
NCH = NT // CH
LCH = NL // CH
HEADS, DK, DV = 4, 64, 128
KEY, VAL = HEADS * DK, HEADS * DV
RANK = 16
LC = 64
GRID_W = 64
ROWS = NL // GRID_W
C_U, C_Q, C_K, C_V, C_R, C_G = 0, 512, 768, 1024, 1536, 2048
C_GA, C_GB = 2080, 3104

SEG = 4
NSEG = FF // P // SEG
TAIL = FF // P - NSEG * SEG
SLOTS = 4
FFN_UNITS = NSEG * (2 * SEG + 4) + 2 * TAIL + 4
FFN_JOBS = NSEG * (2 * SEG + KD) + 2 * TAIL + KD
ADA_JOBS = 2 * (SEG * NSEG + TAIL)

UNIT, JOB = {}, {}


def _number(table, parts):
    n = 0
    for name, count in parts:
        table[name] = n
        n += count
    table["end"] = n


_number(UNIT, [("ffn1", FFN_UNITS), ("u", 4), ("glr", 1), ("k", 2), ("q", 2), ("v", 4), ("r", 4), ("ga", 8),
               ("gb", 8), ("glu", 2), ("merge", 8), ("wo", 8), ("ffn2", FFN_UNITS)])
_number(JOB, [("vec", 1), ("lam", 1), ("ct", 2), ("x", KD), ("prep", 16), ("ada", 1), ("norm0", 1), ("ffn1", FFN_JOBS + ADA_JOBS),
              ("norm1", 1), ("u", CH), ("glr", 1), ("k", 2), ("q", 2), ("ut", 8), ("xs", 16), ("v", 4), ("vt", 6), ("r", 4),
              ("ga", 8), ("gb", 8), ("y", 8), ("yt", 4), ("glu", 4), ("gla", 32), ("ybt", 4), ("merge", 16),
              ("wo", KD), ("norm2", 1), ("ffn2", FFN_JOBS), ("norm3", 1), ("out", 4)])
NADA = 9 * KD
ADA0 = 2 * KD

TWO_PI = 2 * math.pi
PI_1 = 6.28125
PI_2 = float(np.float32(np.round((TWO_PI - PI_1) * 2**20) / 2**20))
PI_3 = float(np.float32(TWO_PI - PI_1 - PI_2))
ROUND = 12582912.0
PI_MAX = 3.1415925


def build(nc, a, out):
    b_scr = nc.dram_tensor("b_scr", [DG, P, P], F32).ap()
    c_scr = nc.dram_tensor("c_scr", [P, DG, 9, GC], F32).ap()
    k_scr = nc.dram_tensor("k_scr", [GC, G, 15, GC], F32).ap()
    x_scr = nc.dram_tensor("x_scr", [P, KD, NL], F32).ap()
    g_scr = nc.dram_tensor("g_scr", [P, 2 * KD, NL], F32).ap()

    base = (nc.sbuf_base + 63) // 64 * 64
    top = [base]

    def place(name, shape, dt, at=None):
        size = int(np.prod(shape[1:])) * 4
        off = top[0] if at is None else at
        t = nc.alloc_sbuf_tensor_at(name, shape, dt, offset=off)
        if at is None:
            top[0] += (size + 63) // 64 * 64
        assert off + size <= nc.sbuf_usable_end, (name, off + size)
        return t

    KB = 1024
    w_raw = place("w_raw", [P, SLOTS, 1024], F32)
    w_hi = place("w_hi", [P, SLOTS, 1024], F32R)
    w_lo = place("w_lo", [P, SLOTS, 1024], F32R)
    h_at = top[0]
    h_hi = place("h_hi", [P, KD, NT], F32R)
    h_lo = place("h_lo", [P, KD, NT], F32R)
    x_at = top[0]
    x = place("x", [P, KD, NT], F32)
    ident = place("ident", [P, P], F32)
    ones = place("ones", [P, P], F32)
    vecs = place("vecs", [P, P], F32)
    vt = place("vt", [P, P], F32)
    mod = place("mod", [P, NADA, 2], F32)
    amul = place("amul", [P, 3, KD, 2], F32)
    cs = place("cs", [P, KD, 2], F32)
    eps = place("eps", [P, 1], F32)
    halfpi = place("halfpi", [P, 1], F32)
    sgn = place("sgn", [P, 1], F32)
    nsgn = place("nsgn", [P, 1], F32)
    lam8 = place("lam8", [P, 2, DG], F32)
    gn_in = place("gn_in", [4, P], F32)
    gn = place("gn", [P, 4], F32)
    hb = place("hb", [P, LCH, G], F32, at=h_at + 28 * KB)
    decay = place("decay", [P, 12], F32)
    oms = place("oms", [P, 16], F32)
    scratch_at = top[0]
    act_hi = place("act_hi", [P, SEG, NT], F32R)
    act_lo = place("act_lo", [P, SEG, NT], F32R)
    silu = place("silu", [P, 2, NT], F32)
    gu = place("gu", [P, 2, NT], F32)
    ssq = place("ssq", [P, NT], F32)
    rstd = place("rstd", [P, NT], F32)
    ada_w = place("ada_w", [P, 2, 1024], F32)
    ffn_end = top[0]

    m = [scratch_at]

    def mix(name, shape, dt=F32):
        size = int(np.prod(shape[1:])) * 4
        t = place(name, shape, dt, at=m[0])
        m[0] += (size + 63) // 64 * 64
        return t

    u_at = m[0]
    u_tok = mix("u_tok", [NCH, G, CH, GC])
    ut_at = m[0]
    ut = mix("ut", [P, G, NCH])
    qt = mix("qt", [P, 2, NL])
    kt = mix("kt", [P, 2, NT])
    v_sb = mix("v_sb", [P, 6, VAL])
    r_sb = mix("r_sb", [P, 4, NL])
    glr = mix("glr", [2 * RANK, NT])
    stream_at = m[0]
    stream = mix("stream", [P, 3, 1024])
    stream2 = place("stream2", [P, 2, 3, 4, P], F32, at=m[0] - 12 * KB)
    xs_at = x_at
    xs = place("xs", [P, NCH, DG], F32, at=x_at)
    st1 = mix("st1", [P, DG])
    st2 = mix("st2", [P, DG])
    gate_buf = mix("gate_buf", [P, 2, NL])
    zmask = mix("zmask", [P, NT])
    tri = mix("tri", [P, 2, P])
    gate_up = mix("gate_up", [2 * RANK, 2, KEY])
    assert m[0] <= nc.sbuf_usable_end
    v_t = place("v_t", [P, 4, NT], F32, at=stream_at)
    y_tok = place("y_tok", [LCH, CH, W5], F32, at=u_at)
    y32 = place("y32", [P, 4, NL], F32, at=xs_at)
    y_hi = place("y_hi", [P, 4, NL], F32R, at=xs_at + 8 * KB)
    y_lo = place("y_lo", [P, 4, NL], F32R, at=xs_at + 16 * KB)
    ya_hi = place("ya_hi", [P, 4, NL], F32R, at=ut_at)
    e1q = place("e1q", [P, NL], F32, at=h_at)
    kz = place("kz", [P, 2, NL], F32, at=h_at + 2 * KB)
    qz = place("qz", [P, 2, 2, NL], F32, at=h_at + 6 * KB)
    ke = place("ke", [P, NT], F32, at=h_at + 14 * KB)
    ket = place("ket", [P, 6, P], F32, at=h_at + 17 * KB)
    at_sb = place("at_sb", [P, 2, 2, 4, P], F32, at=h_at + 20 * KB)
    g_a = place("g_a", [P, NT], F32, at=h_at + 28 * KB)
    g_b = place("g_b", [P, NT], F32, at=h_at + 31 * KB)
    g_c = place("g_c", [P, NT], F32, at=h_at + 34 * KB)
    g_d = place("g_d", [P, NT], F32, at=h_at + 37 * KB)
    s_st = place("s_st", [P, 2, 8, DV], F32, at=u_at)
    s_cur = place("s_cur", [P, 2, 2, DV], F32, at=u_at + 8 * KB)
    o_sb = place("o_sb", [P, 4, VAL], F32, at=h_at + 40 * KB)
    osq = place("osq", [P, 4, VAL], F32, at=h_at)
    yb_hi = place("yb_hi", [P, 4, NL], F32R, at=xs_at)
    yb_lo = place("yb_lo", [P, 4, NL], F32R, at=xs_at + 8 * KB)
    ya_lo = place("ya_lo", [P, 4, NL], F32R, at=xs_at + 16 * KB)
    m_hi = place("m_hi", [P, KD, NL], F32R, at=h_at)
    m_lo = place("m_lo", [P, KD, NL], F32R, at=h_at + 16 * KB)
    mt = place("mt", [P, 2, 3, NL], F32, at=h_at + 32 * KB)
    gates = place("gates", [P, 2, 2, NL], F32, at=u_at)

    pr = place("pr", [P, 9, DG], F32, at=scratch_at)
    pin = place("pin", [P, 9, DG], F32, at=scratch_at + 2304)
    pis = place("pis", [P, 9, DG], F32, at=scratch_at + 2 * 2304)
    s5t = place("s5t", [P, 16, DG], F32, at=scratch_at + 3 * 2304)
    lam_in = place("lam_in", [DG, 2, P], F32, at=scratch_at + 12 * KB)
    bm = place("bm", [P, DG, GC], F32, at=scratch_at + 13 * KB)
    bsw = place("bsw", [P, DG, GC], F32, at=scratch_at + 17 * KB)
    cm = place("cm", [P, DG, GC], F32, at=scratch_at + 21 * KB)
    csw = place("csw", [P, DG, GC], F32, at=scratch_at + 25 * KB)
    c_in = place("c_in", [P, 8, 2, SP5], F32, at=scratch_at + 29 * KB)
    bb = place("bb", [P, DG, GC], F32, at=scratch_at + 33 * KB)
    x_in = place("x_in", [P, 6, D], F32, at=h_at)
    bp = place("bp", [P, 2, 8, CH, GC], F32, at=h_at + 24 * KB)
    cp = place("cp", [P, 2, 8, 9, GC], F32, at=h_at + 32 * KB)
    ptmp = place("ptmp", [P, 8, 9, GC], F32, at=h_at + 41 * KB)
    kf = place("kf", [GC, G, 15, GC], F32, at=base + 16 * KB)
    dg5 = place("dg5", [GC, G], F32, at=scratch_at + 37 * KB)
    bt_sb = place("bt_sb", [P, 1, 8, P], F32, at=scratch_at + 38 * KB)
    out_sb = place("out_sb", [P, 2, D], F32, at=h_at)

    ps = nc.alloc_psum_tensor("ps", [P, 8, 512], F32)

    def lat(j):
        return ps[:, 2 * (j % 4), :]

    def ctx_(j):
        return ps[:, 2 * (j % 4) + 1, :]

    def both(j, n):
        return ps[:, 2 * (j % 4):2 * (j % 4) + 2, 0:n]

    def ada_cols(j, n):
        return lat(j)[:, 0:2 * n].rearrange("p (t v) -> p t v", v=2)

    class Seg:
        def __init__(self, jobs, tiles, ada):
            self.jobs, self.step = jobs, 2 if ada else 1
            self.down0 = 2 * tiles * self.step

        def gu(self, v):
            return self.jobs + v * self.step

        def ada(self, v):
            return self.jobs + v * self.step + 1

        def down(self, k):
            return self.jobs + self.down0 + k

    with ExitStack() as es:
        def sem(name):
            return es.enter_context(nc.semaphore(name))

        job_done = sem("job_done")
        slot_read = [sem(f"slot_read{s}") for s in range(4)]
        w_here = [sem(f"w_here{s}") for s in range(4)]
        w_split = sem("w_split")
        w_used = sem("w_used")
        hi_made = sem("hi_made")
        ada_here = [sem(f"ada_here{s}") for s in range(2)]
        ada_used = sem("ada_used")
        consts = sem("consts")
        small_in = sem("small_in")
        x_landed = sem("x_landed")
        silu_c = sem("silu_c")
        cols_ok = sem("cols_ok")
        act_hi_ok = sem("act_hi_ok")
        act_lo_ok = sem("act_lo_ok")
        sq_ok = sem("sq_ok")
        ssq_ok = sem("ssq_ok")
        rms_ok = sem("rms_ok")
        rstd_ok = sem("rstd_ok")
        xn_ok = sem("xn_ok")
        h_hi_ok = sem("h_hi_ok")
        h_ok = sem("h_ok")
        dve_own = sem("dve_own")
        act_own = sem("act_own")
        pool_own = sem("pool_own")
        slot_taken = sem("slot_taken")
        s5_act = sem("s5_act")
        s5_dve = sem("s5_dve")
        bp_ok = sem("bp_ok")
        bt_ok = sem("bt_ok")
        c_out = [sem("c_out0"), sem("c_out1")]
        b_out = sem("b_out")
        k_ok = sem("k_ok")
        k_out = sem("k_out")
        x_spilled = sem("x_spilled")
        x_back = sem("x_back")
        st_here = [sem(f"st_here{s}") for s in range(3)]
        st_used = sem("st_used")
        scan_step = sem("scan_step")
        states_ok = sem("states_ok")
        ytok_ok = sem("ytok_ok")
        yh_ok = sem("yh_ok")
        yl_ok = sem("yl_ok")
        glu_sig = sem("glu_sig")
        ya_ok = sem("ya_ok")
        yal_ok = sem("yal_ok")
        gate_sig = sem("gate_sig")
        gate_out = [sem("gate_out0"), sem("gate_out1")]
        gate_in = [sem(f"gate_in{s}") for s in range(2)]
        gla_c = sem("gla_c")
        masks_ok = sem("masks_ok")
        z_a = sem("z_a")
        z_d = sem("z_d")
        e_a = sem("e_a")
        e_d = sem("e_d")
        keyt_ok = sem("keyt_ok")
        s_ok = sem("s_ok")
        o_ok = sem("o_ok")
        o_rs = sem("o_rs")
        ybh_ok = sem("ybh_ok")
        yb_ok = sem("yb_ok")
        ybtok_ok = sem("ybtok_ok")
        m32_ok = sem("m32_ok")
        mh_ok = sem("mh_ok")
        m_ok = sem("m_ok")
        fin_ok = sem("fin_ok")
        outc_ok = sem("outc_ok")
        out_done = [sem("out_done0"), sem("out_done1")]

        block = es.enter_context(nc.Block())

        def wait_read(eng, j):
            if j >= 4:
                eng.wait_ge(slot_read[j % 4], j // 4)

        def was_read(eng, j):
            eng.wait_ge(slot_read[j % 4], j // 4 + 1)

        def is_done(eng, j):
            eng.wait_ge(job_done, j + 1)

        SHIFT, SCALE_, GATE = 0, 1, 2

        @block.sync
        def _(sp):
            def unit(n, src, view):
                s = n % 4 if isinstance(n, int) else None
                sp.wait_ge(w_split, n + 1)
                sp.dma_start(view, src).then_inc(w_here[s], 16)

            def raw(s, k, c):
                return w_raw[:, s, 0:k * c].rearrange("p (k c) -> p k c", k=k)

            def ada_tile(t, s):
                sp.wait_ge(ada_used, t + 1)
                sp.dma_start(ada_w[:, s, :].rearrange("p (k c) -> p k c", k=KD),
                             a["ada_w"][0].rearrange("(k p) c -> p k c", p=P)[:, :, bass.ds(t * P, P)])\
                    .then_inc(ada_here[s], 16)

            for t in range(4):
                sp.dma_start(x_in[:, t, :], a["x"][0, P * t:P * t + P, :]).then_inc(x_landed, 16)
            for t in range(2):
                sp.dma_start(x_in[:, 4 + t, :], a["ctx"][0, P * t:P * t + P, :]).then_inc(x_landed, 16)
            sp.wait_ge(k_out, 16)
            for t in range(ADA0):
                ada_tile(t, t % 2)

            def ffn(first, pre, with_ada):
                wg, wu, wd = (a[f"{pre}_{w}"][0] for w in ("w_gate", "w_up", "w_down"))
                gu_src = [w.rearrange("(k p) c -> p k c", p=P) for w in (wg, wu)]
                wd_src = wd.rearrange("(k p) c -> p k c", p=P)

                def seg(i, tiles):
                    n = first + i * (2 * SEG + 4)
                    for v in range(2 * tiles):
                        s = (first + v) % 4
                        sp.wait_ge(w_split, n + v + 1)
                        sp.dma_start(raw(s, KD, P), gu_src[v % 2][:, :, bass.ds(i * (SEG * P) + (v // 2) * P, P)])\
                            .then_inc(w_here[s], 16)
                        if with_ada:
                            if tiles == SEG:
                                ada_tile(i * 8 + (ADA0 + v), v % 2)
                            else:
                                for q in range(4):
                                    ada_tile(ADA0 + 8 * NSEG + 4 * v + q, q % 2)
                    for v in range(4):
                        s = (first + v) % 4
                        sp.wait_ge(w_split, n + 2 * tiles + v + 1)
                        sp.dma_start(raw(s, tiles, 256), wd_src[:, bass.ds(i * SEG, tiles), 256 * v:256 * v + 256])\
                            .then_inc(w_here[s], 16)

                with sp.Fori(0, NSEG) as i:
                    seg(i, SEG)
                seg(NSEG, TAIL)

            ffn(UNIT["ffn1"], "ffn1", True)

            w_in = a["w_in"][0].rearrange("(k p) c -> p k c", p=P)

            def wide(n, c0):
                for q in range(4):
                    unit(n + q, w_in[:, 2 * q:2 * q + 2, c0:c0 + 512], raw((n + q) % 4, 2, 512))

            def tall(n, count, c0, c=P):
                for q in range(count):
                    unit(n + q, w_in[:, :, c0 + q * P:c0 + q * P + c], raw((n + q) % 4, KD, c))

            sp.wait_ge(xn_ok, 2 * KD)
            sp.dma_start(x_scr, x[:, :, 0:NL]).then_inc(x_spilled, 16)
            wide(UNIT["u"], C_U)
            tall(UNIT["glr"], 1, C_G, 2 * RANK)
            tall(UNIT["k"], 2, C_K)
            tall(UNIT["q"], 2, C_Q)
            sp.wait_ge(h_ok, 2 * KD)
            for b in range(8):
                if b >= 3:
                    sp.wait_ge(st_used, b - 2)
                sp.dma_start(stream[:, b % 3, :].rearrange("p (g c) -> p g c", g=8),
                             b_scr[8 * b:8 * b + 8].rearrange("g p c -> p g c")).then_inc(st_here[b % 3], 16)
            tall(UNIT["v"], 4, C_V)
            tall(UNIT["r"], 4, C_R)
            tall(UNIT["ga"], 8, C_GA)
            tall(UNIT["gb"], 8, C_GB)
            is_done(sp, JOB["vt"] + 5)
            for b in range(8):
                if b >= 2:
                    sp.wait_ge(st_used, 8 + b - 1)
                g0 = 4 * b
                for s in range(CH):
                    sp.dma_start(stream2[GC * s:GC * s + GC, b % 2, 0, :, :].rearrange("p g (t c) -> p g t c", c=GC),
                                 k_scr[:, g0:g0 + 4, 7 - s:15 - s, :]).then_inc(st_here[b % 2], 16)
                sp.dma_start(stream2[:, b % 2, 1, :, :].rearrange("p g (t c) -> p g t c", c=GC),
                             c_scr[:, g0:g0 + 4, 1:9, :]).then_inc(st_here[b % 2], 16)
                sp.dma_start(stream2[:, b % 2, 2, :, :].rearrange("p g (t c) -> p g t c", c=GC),
                             c_scr[:, G + g0:G + g0 + 4, 0:8, :]).then_inc(st_here[b % 2], 16)
            glu_w = a["s5_glu_w"][0].rearrange("(k p) c -> p k c", p=P)
            for q in range(2):
                unit(UNIT["glu"] + q, glu_w[:, :, 256 * q:256 * q + 256], raw((UNIT["glu"] + q) % 4, 4, 256))
            outs = [a[w][0].rearrange("(k p) c -> p k c", p=P) for w in ("s5_out", "gla_out")]
            for q in range(8):
                n = UNIT["merge"] + q
                c0 = 256 * (q // 2)
                unit(n, outs[q % 2][:, :, c0:c0 + 256], raw(n % 4, 4, 256))
                if q % 2 == 0:
                    for half in range(2):
                        t = q + half
                        if t >= 2:
                            sp.wait_ge(m32_ok, t - 1)
                        else:
                            sp.wait_ge(o_ok, 8)
                        for br in range(2):
                            sp.dma_start(gates[:, t % 2, br, :], g_scr[:, KD * br + t, :]).then_inc(gate_in[t % 2], 16)
            w_o = a["w_o"][0].rearrange("(k p) c -> p k c", p=P)
            for q in range(8):
                n = UNIT["wo"] + q
                if q == 1:
                    is_done(sp, JOB["merge"] + 15)
                    sp.dma_start(x[:, :, 0:NL], x_scr).then_inc(x_back, 16)
                unit(n, w_o[:, :, P * q:P * q + P], raw(n % 4, KD, P))
            ffn(UNIT["ffn2"], "ffn2", False)
            for t in range(4):
                sp.wait_ge(outc_ok, t + 1)
                sp.dma_start(out[0, P * t:P * t + P, :], out_sb[:, t % 2, :]).then_inc(out_done[t % 2], 16)
            for s in range(2):
                sp.wait_ge(out_done[s], 32)

        @block.gpsimd
        def _(pool):
            pool.sem_inc(w_split, 4)
            pool.memset(ident[:, :], 0.0).then_inc(pool_own, 1)
            pool.memset(ones[:, :], 1.0).then_inc(consts, 1)
            pool.memset(eps[:, :], EPS).then_inc(consts, 1)
            pool.memset(halfpi[:, :], math.pi / 2).then_inc(consts, 1)
            pool.wait_ge(pool_own, 1)
            pool.affine_select(out=ident[:, :], in_=ident[:, :], compare_op=ALU.not_equal, fill=1.0, base=0,
                               pattern=[[-1, P]], channel_multiplier=1).then_inc(consts, 1)

            def split(n, s, cols):
                pool.wait_ge(w_here[s], 16 * ((s_use(n)) + 1))
                pool.wait_ge(w_used, n + 1)
                pool.tensor_scalar(w_hi[:, s, 0:cols], w_raw[:, s, 0:cols], 1.0, 1.0, ALU.mult, ALU.mult)\
                    .then_inc(hi_made, 1)
                pool.wait_ge(hi_made, n + 1)
                pool.tensor_tensor(w_lo[:, s, 0:cols], w_raw[:, s, 0:cols], w_hi[:, s, 0:cols].bitcast(F32),
                                   ALU.subtract).then_inc(w_split, 1)

            def s_use(n):
                return n // 4

            def ffn(first):
                with pool.Fori(0, (FFN_UNITS - 4) // 4) as i:
                    for v in range(4):
                        s = (first + v) % 4
                        pool.wait_ge(w_here[s], i * 16 + 16 * ((first + v) // 4 + 1))
                        pool.wait_ge(w_used, i * 4 + (first + v + 1))
                        pool.sem_inc(slot_taken, 1)
                        pool.tensor_scalar(w_hi[:, s, :], w_raw[:, s, :], 1.0, 1.0, ALU.mult, ALU.mult)\
                            .then_inc(hi_made, 1)
                        pool.wait_ge(hi_made, i * 4 + (first + v + 1))
                        pool.tensor_tensor(w_lo[:, s, :], w_raw[:, s, :], w_hi[:, s, :].bitcast(F32),
                                           ALU.subtract).then_inc(w_split, 1)
                for v in range(FFN_UNITS - 4, FFN_UNITS):
                    split(first + v, (first + v) % 4, TAIL * 256)

            pool.wait_ge(k_out, 16)
            ffn(UNIT["ffn1"])
            n = UNIT["u"]
            while n < UNIT["ffn2"]:
                split(n, n % 4, 8 * 2 * RANK if n == UNIT["glr"] else 1024)
                if n == UNIT["u"] + 3:
                    pool.wait_ge(h_ok, 2 * KD)
                    pool.memset(zmask[:, :], 1.0).then_inc(pool_own, 1)
                    pool.memset(tri[:, :, :], 1.0).then_inc(pool_own, 1)
                    pool.memset(gate_up[:, :, :], 0.0).then_inc(gla_c, 1)
                    pool.wait_ge(pool_own, 3)
                    pool.memset(zmask[:, 0:NT:LC], 0.0).then_inc(masks_ok, 1)
                    pool.affine_select(out=tri[:, 0, :], in_=tri[:, 0, :], compare_op=ALU.is_ge, fill=0.0, base=0,
                                       pattern=[[1, P]], channel_multiplier=-1).then_inc(masks_ok, 1)
                    pool.affine_select(out=tri[:, 1, :], in_=tri[:, 1, :], compare_op=ALU.is_ge, fill=0.0, base=0,
                                       pattern=[[-1, P]], channel_multiplier=1).then_inc(masks_ok, 1)
                n += 1
            ffn(UNIT["ffn2"])

        @block.tensor
        def _(pe):
            pe.sem_inc(w_used, 4)
            pe.sem_inc(ada_used, 2)

            def split_mm(terms, check=True):
                last = None
                for i, (sh, sl, moving) in enumerate(terms):
                    for q, (st, part) in enumerate(((sl, 0), (sh, 1), (sh, 0))):
                        for mv in moving:
                            last = pe.matmul(mv[2], st, mv[part], start=(i == 0 and q == 0),
                                             stop=(i == len(terms) - 1 and q == 2))
                return last

            def wv(s, k, c):
                return [w[:, s, 0:k * c].rearrange("p (k c) -> p k c", k=k) for w in (w_hi, w_lo)]

            def transpose(o, i):
                return pe.transpose(o, i, ident[0:i.shape[0], 0:i.shape[0]])

            pe.wait_ge(consts, 8)
            pe.wait_ge(small_in, 16 * 20)
            transpose(lat(JOB["vec"])[:, 0:P], vecs[:, :]).then_inc(job_done, 1)
            j = JOB["lam"]
            pe.wait_ge(small_in, 16 * 20)
            transpose(lat(j)[:, 0:DG], lam_in[:, 0, :])
            transpose(lat(j)[:, P:P + 4], gn_in[:, :])
            transpose(lat(j)[:, DG:2 * DG], lam_in[:, 1, :]).then_inc(job_done, 1)
            pe.wait_ge(small_in, 16 * 20)
            for h in range(2):
                j = JOB["ct"] + h
                for t in range(4):
                    last = transpose(lat(j)[:, P * t:P * t + P], c_in[:, 4 * h + t, :, :].rearrange("p r s -> p (r s)"))
                last.then_inc(job_done, 1)
            pe.wait_ge(x_landed, 16 * 6)
            for k in range(KD):
                j = JOB["x"] + k
                wait_read(pe, j)
                for t in range(6):
                    o = lat(j)[:, P * t:P * t + P] if t < 4 else ctx_(j)[:, P * (t - 4):P * (t - 3)]
                    last = transpose(o, x_in[:, t, P * k:P * k + P])
                last.then_inc(job_done, 1)
            for b in range(8):
                j = JOB["prep"] + 2 * b
                pe.wait_ge(bp_ok, 2 * b + 1)
                wait_read(pe, j)
                for g in range(8):
                    o = (lat if g < 4 else ctx_)(j)[:, P * (g % 4):P * (g % 4) + P]
                    last = transpose(o, bp[:, b % 2, g, :, :].rearrange("p s c -> p (s c)"))
                last.then_inc(job_done, 1)
                j += 1
                pe.wait_ge(bp_ok, 2 * b + 2)
                wait_read(pe, j)
                lag0 = 0 if b < 4 else 1
                for g in range(8):
                    o = (lat if g < 4 else ctx_)(j)[0:GC, P * (g % 4):P * (g % 4) + P]
                    last = pe.matmul(o, bb[:, 8 * b + g, :],
                                     cp[:, b % 2, g, lag0:lag0 + 8, :].rearrange("p s c -> p (s c)"),
                                     start=True, stop=True)
                last.then_inc(job_done, 1)

            def ada_tile(o, s, here):
                pe.wait_ge(ada_here[s], here)
                for k in range(KD):
                    last = pe.matmul(o, ada_w[:, s, P * k:P * k + P], cs[:, k, :],
                                     start=(k == 0), stop=(k == KD - 1))
                last.then_inc(ada_used, 1)

            pe.wait_ge(silu_c, 1)
            j = JOB["ada"]
            wait_read(pe, j)
            for t in range(ADA0):
                ada_tile(ada_cols(j, ADA0)[:, t, :], t % 2, 16 * (t // 2 + 1))
            pe.wait_ge(ada_used, 2 + ADA0)
            pe.sem_inc(job_done, 1)

            def norm_sum(j, n):
                nb = 1 if n == NL else 2
                pe.wait_ge(ssq_ok, norm_count[0] * KD + KD)
                norm_count[0] += 1
                wait_read(pe, j)
                for q in range(nb):
                    c = slice(512 * q, min(512 * q + 512, n))
                    last = pe.matmul((lat, ctx_)[q](j)[:, 0:c.stop - c.start], ones[:, :], ssq[:, c],
                                     start=True, stop=True)
                last.then_inc(job_done, 1)

            norm_count = [0]

            def ffn(units, jobs, n, h_value, with_ada, act_base):
                two = n == NT

                def seg(i, tiles):
                    un = units + i * (2 * SEG + 4)
                    js = Seg(jobs, tiles, with_ada)
                    jseg = (2 * SEG * js.step + KD)

                    def slot_free(j):
                        pe.wait_ge(slot_read[j % 4], j // 4 + i * (jseg // 4))

                    for v in range(2 * tiles):
                        s, j = (units + v) % 4, js.gu(v)
                        pe.wait_ge(w_split, un + (v + 5))
                        slot_free(j)
                        wh, wl = wv(s, KD, P)
                        terms = []
                        for k in range(KD):
                            if two:
                                mv = [(h_hi[:, k, 384 * q:384 * q + 384], h_lo[:, k, 384 * q:384 * q + 384],
                                       (lat, ctx_)[q](j)[:, 0:384]) for q in range(2)]
                            else:
                                mv = [(h_hi[:, k, 0:NL], h_lo[:, k, 0:NL], lat(j))]
                            terms.append((wh[:, k, :], wl[:, k, :], mv))
                        split_mm(terms).then_inc(job_done, 1)
                        pe.wait_ge(job_done, (j + 1) + i * jseg)
                        pe.sem_inc(w_used, 1)
                        if with_ada:
                            j = js.ada(v)
                            slot_free(j)
                            if tiles == SEG:
                                ada_tile(ada_cols(j, 1)[:, 0, :], v % 2, i * 64 + 16 * ((ADA0 + v) // 2 + 1))
                            else:
                                for q in range(4):
                                    t = ADA0 + 8 * NSEG + 4 * v + q
                                    ada_tile(ada_cols(j, 4)[:, q, :], q % 2, 16 * (t // 2 + 1))
                            done = (2 + ADA0 + v + 1 + i * 8) if tiles == SEG else 2 + ADA0 + 8 * NSEG + 4 * v + 4
                            pe.wait_ge(ada_used, done)
                            pe.sem_inc(job_done, 1)
                    for v in range(4):
                        s = (units + 2 * tiles + v) % 4
                        pe.wait_ge(w_split, un + (2 * tiles + v + 5))
                        if v == 0:
                            pe.wait_ge(act_lo_ok, act_base + tiles + i * SEG)
                        wh, wl = wv(s, tiles, 256)
                        for q in range(2):
                            j = js.down(2 * v + q)
                            slot_free(j)
                            terms = []
                            for k in range(tiles):
                                mv = [(act_hi[:, k, 0:NL], act_lo[:, k, 0:NL], lat(j))]
                                if two:
                                    mv.append((act_hi[:, k, NL:NT], act_lo[:, k, NL:NT], ctx_(j)[:, 0:NC]))
                                terms.append((wh[:, k, P * q:P * q + P], wl[:, k, P * q:P * q + P], mv))
                            split_mm(terms).then_inc(job_done, 1)
                        pe.wait_ge(job_done, (j + 1) + i * jseg)
                        pe.sem_inc(w_used, 1)

                with pe.Fori(0, NSEG) as i:
                    seg(i, SEG)
                seg(NSEG, TAIL)

            norm_sum(JOB["norm0"], NT)
            pe.wait_ge(h_ok, KD)
            ffn(UNIT["ffn1"], JOB["ffn1"], NT, None, True, 0)
            norm_sum(JOB["norm1"], NT)
            pe.wait_ge(h_ok, 2 * KD)

            def hview(t, k, cols):
                return t[:, k, :][:, cols]

            def used(n, j):
                is_done(pe, j)
                pe.sem_inc(w_used, 1)

            def wide_jobs(n, j0, count, cols, rows):
                for t in range(count):
                    j = j0 + t
                    if t == 0:
                        pe.wait_ge(w_split, n + 8)
                    wait_read(pe, j)
                    terms = []
                    for k in range(KD):
                        s = (n + k // 2) % 4
                        mv = [(w_hi[:, s, 512 * (k % 2):512 * (k % 2) + 512], w_lo[:, s, 512 * (k % 2):512 * (k % 2) + 512],
                               lat(j)[0:rows, :])]
                        terms.append((cols(h_hi, k, t), cols(h_lo, k, t), mv))
                    split_mm(terms).then_inc(job_done, 1)
                is_done(pe, j0 + count - 1)
                pe.sem_inc(w_used, 4)

            def tall_jobs(n, j0, count, toks, c=P):
                for t in range(count):
                    j = j0 + t
                    pe.wait_ge(w_split, n + t + 5)
                    wait_read(pe, j)
                    wh, wl = wv((n + t) % 4, KD, c)
                    terms = []
                    for k in range(KD):
                        mv = [(h_hi[:, k, 0:NL], h_lo[:, k, 0:NL], lat(j)[0:c, :])]
                        if toks == NT:
                            mv.append((h_hi[:, k, NL:NT], h_lo[:, k, NL:NT], ctx_(j)[0:c, 0:NC]))
                        terms.append((wh[:, k, :], wl[:, k, :], mv))
                    split_mm(terms).then_inc(job_done, 1)
                    used(n + t, j)

            wide_jobs(UNIT["u"], JOB["u"], CH, lambda h, k, t: h[:, k, t:NT:CH], NCH)
            tall_jobs(UNIT["glr"], JOB["glr"], 1, NT, 2 * RANK)
            tall_jobs(UNIT["k"], JOB["k"], 2, NT)
            tall_jobs(UNIT["q"], JOB["q"], 2, NL)
            for b in range(8):
                j = JOB["ut"] + b
                if b == 0:
                    for s in range(CH - 4, CH):
                        was_read(pe, JOB["u"] + s)
                wait_read(pe, j)
                for g in range(4):
                    last = transpose(lat(j)[:, NCH * g:NCH * g + NCH],
                                     u_tok[:, 4 * b + g, :, :].rearrange("p s c -> p (s c)"))
                last.then_inc(job_done, 1)
            for b in range(16):
                j = JOB["xs"] + b
                if b == 0:
                    for q in range(4, 8):
                        was_read(pe, JOB["ut"] + q)
                if b % 2 == 0:
                    pe.wait_ge(st_here[b // 2 % 3], 16 * (b // 6 + 1))
                wait_read(pe, j)
                for q in range(4):
                    g = (4 * b + q) % G
                    e = (4 * b + q) % 8
                    last = pe.matmul(lat(j)[:, NCH * q:NCH * q + NCH], stream[:, b // 2 % 3, P * e:P * e + P],
                                     ut[:, g, :], start=True, stop=True)
                last.then_inc(job_done, 1)
                if b % 2:
                    is_done(pe, j)
                    pe.sem_inc(st_used, 1)

            tall_jobs(UNIT["v"], JOB["v"], 4, NT)
            for t in range(6):
                j = JOB["vt"] + t
                if t == 0:
                    for q in range(4):
                        was_read(pe, JOB["v"] + q)
                wait_read(pe, j)
                for q in range(4):
                    last = transpose(lat(j)[:, P * q:P * q + P], v_t[:, q, P * t:P * t + P])
                last.then_inc(job_done, 1)
            tall_jobs(UNIT["r"], JOB["r"], 4, NL)
            tall_jobs(UNIT["ga"], JOB["ga"], 8, NL)
            tall_jobs(UNIT["gb"], JOB["gb"], 8, NL)
            pe.wait_ge(states_ok, 1)
            for b in range(8):
                j = JOB["y"] + b
                pe.wait_ge(st_here[b % 2], 16 * (3, 3)[b % 2] + 160 * (b // 2 + 1))
                wait_read(pe, j)
                for q in range(4):
                    g = 4 * b + q
                    o = lat(j)[0:LCH, P * q:P * q + P]
                    c0 = NC // CH
                    pe.matmul(o, ut[:, g, 0:LCH], stream2[:, b % 2, 0, q, :], start=True, stop=False)
                    pe.matmul(o, xs[:, c0 - 1:c0 - 1 + LCH, g], stream2[:, b % 2, 1, q, :], start=False, stop=False)
                    last = pe.matmul(o, hb[:, :, g], stream2[:, b % 2, 2, q, :],
                                     start=False, stop=True)
                last.then_inc(job_done, 1)
                is_done(pe, j)
                pe.sem_inc(st_used, 1)
            for c in range(4):
                j = JOB["yt"] + c
                if c == 0:
                    for q in range(4, 8):
                        was_read(pe, JOB["y"] + q)
                wait_read(pe, j)
                for t in range(CH):
                    last = transpose(lat(j)[:, LCH * t:LCH * t + LCH], y_tok[:, t, P * c:P * c + P])
                last.then_inc(job_done, 1)
            pe.wait_ge(yl_ok, 4)
            for q in range(2):
                n = UNIT["glu"] + q
                pe.wait_ge(w_split, n + 5)
                wh, wl = wv(n % 4, 4, 256)
                for h in range(2):
                    j = JOB["glu"] + 2 * q + h
                    wait_read(pe, j)
                    split_mm([(wh[:, k, P * h:P * h + P], wl[:, k, P * h:P * h + P],
                               [(y_hi[:, k, :], y_lo[:, k, :], lat(j))]) for k in range(4)]).then_inc(job_done, 1)
                used(n, j)
            pe.wait_ge(small_in, 16 * 22)
            j = JOB["gla"]
            for ti in range(2):
                for d in range(2):
                    p_ = 2 * ti + d
                    wait_read(pe, j)
                    for q in range(2):
                        last = pe.matmul((lat, ctx_)[q](j)[:, 0:384], gate_up[:, d, P * ti:P * ti + P],
                                         glr[:, 384 * q:384 * q + 384], start=True, stop=True)
                    last.then_inc(job_done, 1)
                    j += 1
                    pe.wait_ge(e_d, p_ + 1)
                    wait_read(pe, j)
                    for t in range(6):
                        o = lat(j)[:, P * t:P * t + P] if t < 4 else ctx_(j)[:, P * (t - 4):P * (t - 3)]
                        last = transpose(o, ke[:, P * t:P * t + P])
                    last.then_inc(job_done, 1)
                    was_j = j
                    j += 1
                    for hp in range(2):
                        wait_read(pe, j)
                        for t in range(4):
                            last = pe.matmul(lat(j)[:, P * t:P * t + P], kz[:, hp, P * t:P * t + P],
                                             e1q[:, P * t:P * t + P], start=True, stop=True)
                        last.then_inc(job_done, 1)
                        j += 1
                    was_read(pe, was_j)
                    order = (4, 5, 0, 1, 2, 3) if d == 0 else (5, 4, 3, 2, 1, 0)
                    for half in range(2):
                        wait_read(pe, j)
                        for q in range(3):
                            t = order[3 * half + q]
                            for par in range(2):
                                for hp in range(2):
                                    hd = 2 * ti + hp
                                    last = pe.matmul((lat, ctx_)[par](j)[64 * hp:64 * hp + 64, P * q:P * q + P],
                                                     ket[64 * par:64 * par + 64, t, 64 * hp:64 * hp + 64],
                                                     v_sb[64 * par:64 * par + 64, t, DV * hd:DV * hd + DV],
                                                     start=True, stop=True)
                        last.then_inc(job_done, 1)
                        j += 1
                pe.wait_ge(s_ok, 2 * ti + 2)
                for t in range(4):
                    wait_read(pe, j)
                    for hp in range(2):
                        hd = 2 * ti + hp
                        c = slice(DV * hp, DV * hp + DV)
                        for d in range(2):
                            pe.matmul(lat(j)[:, c], at_sb[:, d, hp, t, :], v_sb[:, t, DV * hd:DV * hd + DV],
                                      start=(d == 0), stop=False, skip_group_check=True)
                        for par in range(2):
                            for d in range(2):
                                last = pe.matmul(lat(j)[64 * par:64 * par + 64, c],
                                                 qz[:, d, hp, P * t + 64 * par:P * t + 64 * par + 64],
                                                 s_st[:, d, 2 * t + par, :], start=False,
                                                 stop=(par == 1 and d == 1), skip_group_check=True)
                    last.then_inc(job_done, 1)
                    j += 1
            pe.wait_ge(ybtok_ok, 1)
            for c in range(4):
                j = JOB["ybt"] + c
                wait_read(pe, j)
                for t in range(4):
                    last = transpose(lat(j)[:, P * t:P * t + P], o_sb[:, t, P * c:P * c + P])
                last.then_inc(job_done, 1)
            pe.wait_ge(yb_ok, 4)
            pe.wait_ge(yal_ok, 4)
            for q in range(8):
                n = UNIT["merge"] + q
                pe.wait_ge(w_split, n + 5)
                wh, wl = wv(n % 4, 4, 256)
                yh, yl = ((ya_hi, ya_lo), (yb_hi, yb_lo))[q % 2]
                for h in range(2):
                    j = JOB["merge"] + 2 * q + h
                    wait_read(pe, j)
                    split_mm([(wh[:, k, P * h:P * h + P], wl[:, k, P * h:P * h + P],
                               [(yh[:, k, :], yl[:, k, :], lat(j))]) for k in range(4)]).then_inc(job_done, 1)
                used(n, j)
            pe.wait_ge(m_ok, KD)
            for q in range(KD):
                n, j = UNIT["wo"] + q, JOB["wo"] + q
                pe.wait_ge(w_split, n + 5)
                wait_read(pe, j)
                wh, wl = wv(n % 4, KD, P)
                split_mm([(wh[:, k, :], wl[:, k, :], [(m_hi[:, k, :], m_lo[:, k, :], lat(j))])
                          for k in range(KD)]).then_inc(job_done, 1)
                used(n, j)
            norm_sum(JOB["norm2"], NL)
            pe.wait_ge(h_ok, 3 * KD)
            ffn(UNIT["ffn2"], JOB["ffn2"], NL, None, False, FF // P)
            norm_sum(JOB["norm3"], NL)
            pe.wait_ge(fin_ok, KD)
            for t in range(4):
                j = JOB["out"] + t
                wait_read(pe, j)
                for k in range(KD):
                    last = transpose((lat if k < 4 else ctx_)(j)[:, P * (k % 4):P * (k % 4) + P],
                                     x[:, k, P * t:P * t + P])
                last.then_inc(job_done, 1)

        @block.scalar
        def _(act):
            own = [0]

            def link(ins):
                own[0] += 1
                ins.then_inc(act_own, 1)
                act.wait_ge(act_own, own[0])

            rows = [("ada_b", 72), ("ffn1_norm", 8), ("mix_norm", 8), ("ffn2_norm", 8), ("final_norm", 8), ("c", 8),
                    ("c_ctx", 8), ("s5_glu_b", 4), ("gla_gate_b", 4)]
            r0 = 0
            for name, n in rows:
                src = a[name]
                while len(src.shape) > 1:
                    src = src.rearrange("a b -> (a b)") if len(src.shape) == 2 else src.rearrange("a b c -> (a b c)")
                act.dma_start(vecs[r0:r0 + n, :], src.rearrange("(r p) -> r p", p=P)).then_inc(small_in, 16)
                r0 += n
            for q, name in enumerate(("s5_lambda_re", "s5_lambda_im")):
                for h in range(2):
                    act.dma_start(lam_in[:, q, SP5 * h:SP5 * h + SP5], a[name][0].rearrange("d g p -> (d g) p"))\
                        .then_inc(small_in, 16)
            act.dma_start(s5t[:, 0, :], a["s5_log_dt"][0].rearrange("d g -> (d g)").partition_broadcast(P))\
                .then_inc(small_in, 16)
            for q, name in enumerate(("s5_c_re", "s5_c_im")):
                act.dma_start(c_in[:, :, q, :], a[name][0].rearrange("d g c p -> (d g c) p")
                              .rearrange("(t r) p -> r t p", r=P)).then_inc(small_in, 16)
            for q, name in enumerate(("s5_b_re", "s5_b_im")):
                act.dma_start(bm[64 * q:64 * q + 64, :, :], a[name][0].rearrange("d g p c -> p (d g) c"))\
                    .then_inc(small_in, 16)
            act.dma_start(gn_in[:, :], a["gla_norm"][0].rearrange("(r p) -> r p", p=P)).then_inc(small_in, 16)
            act.dma_start(dg5[:, :], a["s5_d"][0].rearrange("(g c) -> c g", c=GC),
                          allow_slow_non_contiguous=True).then_inc(small_in, 16)

            j = JOB["vec"]
            is_done(act, j)
            act.activation(vt[:, :], lat(j)[:, 0:P], ACT.Copy).then_inc(slot_read[j % 4], 1)
            was_read(act, j)
            for v, row in enumerate((104, 112)):
                ins = act.activation(cs[:, :, v], vt[:, row:row + 8], ACT.Silu)
            ins.then_inc(silu_c, 1)
            act.wait_ge(small_in, 16 * 20)
            act.activation(s5t[:, 1, :], s5t[:, 0, :], ACT.Exp).then_inc(s5_act, 1)
            act.wait_ge(consts, 8)
            for h in range(2):
                j = JOB["ct"] + h
                is_done(act, j)
                act.activation(cm[:, 32 * h:32 * h + 32, :].rearrange("p g c -> p (g c)"), lat(j), ACT.Copy,
                               scale=1.0).then_inc(s5_act, 1)
            act.wait_ge(s5_dve, 1)
            act.activation(s5t[:, 8, :], s5t[:, 4, :], ACT.Exp).then_inc(s5_act, 1)
            act.activation(s5t[:, 9, :], s5t[:, 6, :], ACT.Sin).then_inc(s5_act, 1)
            link(act.activation(s5t[:, 10, :], s5t[:, 6, :], ACT.Abs))
            act.activation(s5t[:, 11, :], s5t[:, 10, :], ACT.Sin, bias=halfpi[:, :], scale=-1.0).then_inc(s5_act, 1)
            for k in range(KD):
                j = JOB["x"] + k
                is_done(act, j)
                act.activation(x[:, k, 0:NL], lat(j), ACT.Copy)
                act.activation(x[:, k, NL:NT], ctx_(j)[:, 0:NC], ACT.Copy).then_inc(slot_read[j % 4], 1)
            for b in range(8):
                j = JOB["prep"] + 2 * b
                is_done(act, j)
                if b:
                    act.wait_ge(b_out, 16 * b)
                act.activation(bt_sb[:, 0, :, :].rearrange("p (h g) c -> p h (g c)", h=2), both(j, 512), ACT.Copy)\
                    .then_inc(slot_read[j % 4], 1)
                was_read(act, j)
                act.dma_start(b_scr[8 * b:8 * b + 8].rearrange("g p c -> p g c"), bt_sb[:, 0, :, :]).then_inc(b_out, 16)
                act.wait_ge(bp_ok, 2 * b + 2)
                act.dma_start(c_scr[:, 8 * b:8 * b + 8, :, :], cp[:, b % 2, :, :, :]).then_inc(c_out[b % 2], 16)
            act.wait_ge(k_ok, 1)
            act.dma_start(k_scr, kf[:, :, :, :]).then_inc(k_out, 16)
            act.wait_ge(b_out, 128)
            for s in range(2):
                act.wait_ge(c_out[s], 64)
            act.wait_ge(k_out, 16)

            def norm(q, j, n):
                for k in range(KD):
                    if q == 0:
                        was_read(act, JOB["x"] + k)
                    else:
                        was_read(act, (JOB["ffn1"] + FFN_JOBS + ADA_JOBS - KD, JOB["wo"], JOB["ffn2"] + FFN_JOBS - KD)[q - 1] + k)
                    if k >= 2 or q:
                        act.wait_ge(ssq_ok, KD * q + k - 1)
                    act.activation(silu[:, k % 2, 0:n], x[:, k, 0:n], ACT.Square).then_inc(sq_ok, 1)
                is_done(act, j)
                if n == NT:
                    act.activation(rstd[:, 0:NL], lat(j), ACT.Sqrt, bias=eps[:, :], scale=1.0 / D)
                    act.activation(rstd[:, NL:NT], ctx_(j)[:, 0:NC], ACT.Sqrt, bias=eps[:, :], scale=1.0 / D)\
                        .then_inc(slot_read[j % 4], 1)
                else:
                    act.activation(rstd[:, 0:NL], lat(j), ACT.Sqrt, bias=eps[:, :], scale=1.0 / D)\
                        .then_inc(slot_read[j % 4], 1)
                if q == 3:
                    return
                for k in range(KD):
                    act.wait_ge(xn_ok, KD * q + k + 1)
                    parts = [(slice(0, NL), 0)] + ([(slice(NL, NT), 1)] if n == NT else [])
                    for c, v in parts:
                        ins = act.activation(h_hi[:, k, c], gu[:, k % 2, c], ACT.Identity,
                                             bias=mod[:, 24 * q + k, v:v + 1], scale=amul[:, q, k, v:v + 1])
                    ins.then_inc(h_hi_ok, 1)

            def ffn(jobs, n, ada):
                def seg(i, tiles):
                    js = Seg(jobs, tiles, ada)
                    jseg = 2 * SEG * js.step + KD
                    for f in range(tiles):
                        jg, ju = js.gu(2 * f), js.gu(2 * f + 1)
                        dst, src = silu[:, f % 2, 0:n], lat(jg)
                        if n == NT:
                            dst, src = dst.rearrange("p (b c) -> p b c", b=2), both(jg, 384)
                        act.wait_ge(job_done, (jg + 1) + i * jseg)
                        act.activation(dst, src, ACT.Silu).then_inc(slot_read[jg % 4], 1)
                        act.wait_ge(slot_read[ju % 4], (ju // 4 + 1) + i * (jseg // 4))
                        act.activation(act_hi[:, f, 0:n], gu[:, f % 2, 0:n], ACT.Copy).then_inc(act_hi_ok, 1)

                with act.Fori(0, NSEG) as i:
                    seg(i, SEG)
                seg(NSEG, TAIL)

            act.wait_ge(cols_ok, 1)
            norm(0, JOB["norm0"], NT)
            ffn(JOB["ffn1"], NT, True)
            act.wait_ge(cols_ok, 2)
            norm(1, JOB["norm1"], NT)

            act.wait_ge(h_ok, 2 * KD)
            for s in range(CH):
                j = JOB["u"] + s
                is_done(act, j)
                act.activation(u_tok[:, :, s, :], lat(j)[0:NCH, :].rearrange("p (g c) -> p g c", c=GC), ACT.Copy)\
                    .then_inc(slot_read[j % 4], 1)
            act.wait_ge(gla_c, 1)
            for d in range(2):
                act.dma_start(gate_up[RANK * d:RANK * d + RANK, d, :], a["gla_gate_up"][0, d]).then_inc(small_in, 16)

            def w_major(t):
                return t.rearrange("p (w r) -> p r w", r=ROWS)

            def row_major(t):
                return t.rearrange("p (r w) -> p r w", w=GRID_W)

            def evac_tokens(j, dst, n, rows, scale=1.0):
                is_done(act, j)
                ins = act.activation(w_major(dst[:, 0:NL]), row_major(lat(j)[0:rows, :]), ACT.Copy, scale=scale)
                if n == NT:
                    ins = act.activation(dst[:, NL:NT], ctx_(j)[0:rows, 0:NC], ACT.Copy)
                ins.then_inc(slot_read[j % 4], 1)

            evac_tokens(JOB["glr"], glr[:, :], NT, 2 * RANK)
            for q in range(2):
                evac_tokens(JOB["k"] + q, kt[:, q, :], NT, P)
            for q in range(2):
                evac_tokens(JOB["q"] + q, qt[:, q, :], NL, P, DK ** -0.5)
            for b in range(8):
                j = JOB["ut"] + b
                is_done(act, j)
                act.activation(ut[:, 4 * b:4 * b + 4, :], lat(j)[:, 0:4 * NCH].rearrange("p (g c) -> p g c", g=4),
                               ACT.Copy).then_inc(slot_read[j % 4], 1)
            act.wait_ge(x_spilled, 16)
            nctx = NC // CH
            for b in range(16):
                j = JOB["xs"] + b
                is_done(act, j)
                src = lat(j)[:, 0:4 * NCH].rearrange("p (g c) -> p c g", g=4)
                dgs = slice(4 * b, 4 * b + 4)
                lats, ctxs = src[:, 0:LCH, :], src[:, LCH:NCH, :]
                if b >= 8:
                    lats, ctxs = lats[:, ::-1, :], ctxs[:, ::-1, :]
                act.activation(xs[:, nctx:NCH, dgs], lats, ACT.Copy)
                act.activation(xs[:, 0:nctx, dgs], ctxs, ACT.Copy).then_inc(slot_read[j % 4], 1)
            for q in range(4):
                evac_tokens(JOB["v"] + q, v_t[:, q, :], NT, P)
            for t in range(6):
                j = JOB["vt"] + t
                is_done(act, j)
                act.activation(v_sb[:, t, :], lat(j), ACT.Copy).then_inc(slot_read[j % 4], 1)
            for t in range(4):
                j = JOB["r"] + t
                is_done(act, j)
                act.activation(r_sb[:, t, :], lat(j), ACT.Silu).then_inc(slot_read[j % 4], 1)
            for t in range(16):
                j = JOB["ga"] + t
                is_done(act, j)
                if t >= 2:
                    act.wait_ge(gate_out[t % 2], 16 * (t // 2))
                act.activation(gate_buf[:, t % 2, :], lat(j), ACT.Sigmoid).then_inc(slot_read[j % 4], 1)
                was_read(act, j)
                act.dma_start(g_scr[:, t, :], gate_buf[:, t % 2, :]).then_inc(gate_out[t % 2], 16)
            for b in range(8):
                j = JOB["y"] + b
                is_done(act, j)
                act.activation(y_tok[:, :, 64 * b:64 * b + 64].rearrange("p t (g c) -> p t g c", c=GC),
                               lat(j)[0:LCH, :].rearrange("p (g t c) -> p t g c", g=4, c=GC), ACT.Gelu_apprx_tanh)\
                    .then_inc(slot_read[j % 4], 1)


            def token_order(t):
                return t.rearrange("p (k t) -> p t k", t=CH)

            for c in range(4):
                j = JOB["yt"] + c
                is_done(act, j)
                src = lat(j).rearrange("p (t k) -> p t k", t=CH)
                act.activation(token_order(y32[:, c, :]), src, ACT.Copy)
                act.activation(token_order(y_hi[:, c, :]), src, ACT.Copy).then_inc(yh_ok, 1)
            for c in range(4):
                j = JOB["glu"] + c
                is_done(act, j)
                if c < 2:
                    act.wait_ge(gate_out[c], 128)
                act.activation(gate_buf[:, c % 2, :], lat(j), ACT.Sigmoid, bias=vt[:, 120 + c:121 + c])\
                    .then_inc(slot_read[j % 4], 1)
                act.wait_ge(ya_ok, c + 1)
                if c == 3:
                    for e in range(4):
                        act.activation(ya_hi[:, e, :], y32[:, e, :], ACT.Copy).then_inc(glu_sig, 1)
            j = JOB["gla"]
            for ti in range(2):
                for d in range(2):
                    p_ = 2 * ti + d
                    gb_col = vt[:, 124 + 2 * d + ti:125 + 2 * d + ti]
                    is_done(act, j)
                    dst = g_a[:, :].rearrange("p (b c) -> p b c", b=2)
                    if p_ == 0:
                        pass
                    else:
                        act.wait_ge(e_d, p_)
                    link(act.activation(dst, both(j, 384), ACT.Abs, bias=gb_col))
                    link(act.activation(g_a[:, :], g_a[:, :], ACT.Exp, scale=-1.0))
                    act.activation(g_a[:, :], g_a[:, :], ACT.Ln, bias=ones[:, 0:1]).then_inc(z_a, 1)
                    j += 1
                    act.wait_ge(z_d, 2 * p_ + 1)
                    act.activation(g_a[:, 0:NL], g_b[:, 0:NL], ACT.Exp, scale=1.0 / 16).then_inc(e_a, 1)
                    act.wait_ge(z_d, 2 * p_ + 2)
                    act.activation(g_a[:, 0:NL], g_b[:, 0:NL], ACT.Exp, scale=-1.0 / 16).then_inc(e_a, 1)
                    gv = g_c[:, :].rearrange("p (c t) -> p c t", t=LC)
                    own[0] += 1
                    act.activation(decay[:, :], gv[:, :, (LC - 1 if d == 0 else 0)], ACT.Exp, scale=1.0 / 16)\
                        .then_inc(act_own, 1)
                    act.activation(g_d[:, :], g_d[:, :], ACT.Exp, scale=1.0 / 16).then_inc(e_a, 1)
                    act.wait_ge(act_own, own[0])
                    act.activation(g_c[:, 0:NL], g_c[:, 0:NL], ACT.Exp, scale=1.0 / 16).then_inc(e_a, 1)
                    is_done(act, j)
                    act.activation(ket[:, 0:4, :].rearrange("p t c -> p (t c)"), lat(j), ACT.Copy)
                    act.activation(ket[:, 4:6, :].rearrange("p t c -> p (t c)"), ctx_(j)[:, 0:2 * P], ACT.Copy)\
                        .then_inc(slot_read[j % 4], 1)
                    j += 1
                    j += 4
                for t in range(4):
                    is_done(act, j)
                    act.activation(o_sb[:, t, 2 * DV * ti:2 * DV * ti + 2 * DV], lat(j)[:, 0:2 * DV], ACT.Copy)\
                        .then_inc(slot_read[j % 4], 1)
                    was_read(act, j)
                    act.sem_inc(o_ok, 1)
                    j += 1
            act.wait_ge(o_rs, 1)
            act.activation(oms[:, :], oms[:, :], ACT.Sqrt, bias=eps[:, :], scale=1.0 / DV).then_inc(o_rs, 1)
            for c in range(4):
                j = JOB["ybt"] + c
                was_read(act, j)
                act.activation(yb_hi[:, c, :], r_sb[:, c, :], ACT.Copy).then_inc(ybh_ok, 1)
            for t in range(KD):
                act.wait_ge(m32_ok, t + 1)
                act.activation(m_hi[:, t, :], mt[:, t % 2, 2, :], ACT.Copy).then_inc(mh_ok, 1)
            norm(2, JOB["norm2"], NL)
            ffn(JOB["ffn2"], NL, False)
            norm(3, JOB["norm3"], NL)
            for t in range(4):
                j = JOB["out"] + t
                is_done(act, j)
                if t >= 2:
                    act.wait_ge(out_done[t % 2], 16)
                act.activation(out_sb[:, t % 2, :].rearrange("p (b c) -> p b c", b=2), both(j, 512), ACT.Copy)\
                    .then_inc(slot_read[j % 4], 1)
                was_read(act, j)
                act.sem_inc(outc_ok, 1)

        @block.vector
        def _(dve):
            own = [0]

            def link(ins):
                own[0] += 1
                ins.then_inc(dve_own, 1)
                dve.wait_ge(dve_own, own[0])

            TT, TS, STT = dve.tensor_tensor, dve.tensor_scalar, dve.scalar_tensor_tensor
            dve.memset(sgn[0:64, :], -1.0).then_inc(consts, 1)
            dve.memset(sgn[64:128, :], 1.0).then_inc(consts, 1)
            dve.memset(nsgn[0:64, :], 1.0).then_inc(consts, 1)
            dve.memset(nsgn[64:128, :], -1.0).then_inc(consts, 1)
            f = [s5t[:, q, :] for q in range(16)]
            dt, lr, li, th = f[1], f[2], f[3], f[6]
            j = JOB["lam"]
            is_done(dve, j)
            dve.tensor_copy(li, lat(j)[:, DG:2 * DG])
            dve.tensor_copy(gn[:, :], lat(j)[:, P:P + 4])
            TS(lr, lat(j)[:, 0:DG], -1e-4, None, ALU.min).then_inc(slot_read[j % 4], 1)
            was_read(dve, j)
            dve.wait_ge(s5_act, 1)
            TT(f[4], lr, dt, ALU.mult)
            link(TT(f[5], li, dt, ALU.mult))
            link(TS(f[7], f[5], 1.0 / TWO_PI, ROUND, ALU.mult, ALU.add))
            link(TS(f[7], f[7], -ROUND, None, ALU.add))
            link(STT(f[6], f[7], -PI_1, f[5], ALU.mult, ALU.add))
            link(STT(f[6], f[7], -PI_2, f[6], ALU.mult, ALU.add))
            link(STT(f[6], f[7], -PI_3, f[6], ALU.mult, ALU.add))
            TS(th, f[6], PI_MAX, -PI_MAX, ALU.min, ALU.max).then_inc(s5_dve, 1)
            link(TT(f[12], lr, lr, ALU.mult))
            link(TT(f[13], li, li, ALU.mult))
            link(TT(f[12], f[12], f[13], ALU.add))
            link(dve.reciprocal(f[12], f[12]))
            dve.wait_ge(s5_act, 6)
            dve.wait_ge(consts, 8)
            dve.memset(pr[:, 0, :], 1.0)
            dve.memset(pin[:, 0, :], 0.0)
            TT(pr[:, 1, :], f[8], f[11], ALU.mult)
            link(TT(f[9], f[8], f[9], ALU.mult))
            link(TS(f[13], pr[:, 1, :], -1.0, None, ALU.add))
            link(TT(f[14], f[13], lr, ALU.mult))
            link(TT(f[15], f[9], li, ALU.mult))
            link(TT(f[14], f[14], f[15], ALU.add))
            link(TT(f[14], f[14], f[12], ALU.mult))
            link(TT(f[15], f[13], li, ALU.mult))
            link(TT(f[13], f[9], lr, ALU.mult))
            link(TT(f[15], f[13], f[15], ALU.subtract))
            link(TT(f[15], f[15], f[12], ALU.mult))
            link(TS(f[15], f[15], sgn[:, 0:1], None, ALU.mult))
            dve.tensor_copy(pin[:, 1, :], f[9])
            for q in range(2, 9):
                link(TT(f[0], pr[:, q - 1, :], pr[:, 1, :], ALU.mult))
                link(TT(f[10], pin[:, q - 1, :], f[9], ALU.mult))
                link(TT(pr[:, q, :], f[0], f[10], ALU.subtract))
                link(TT(f[0], pr[:, q - 1, :], f[9], ALU.mult))
                link(TT(f[10], pin[:, q - 1, :], pr[:, 1, :], ALU.mult))
                link(TT(pin[:, q, :], f[0], f[10], ALU.add))
            link(TS(pis[:, :, :], pin[:, :, :], sgn[:, 0:1], None, ALU.mult))
            link(TS(pin[:, :, :], pin[:, :, :], nsgn[:, 0:1], None, ALU.mult))
            dve.tensor_copy(lam8[:, 0, :], pr[:, 8, :])
            dve.tensor_copy(lam8[:, 1, :], pin[:, 8, :])
            dve.wait_ge(small_in, 16 * 20)
            dve.tensor_copy(bsw[0:64, :, :], bm[64:128, :, :])
            link(dve.tensor_copy(bsw[64:128, :, :], bm[0:64, :, :]))

            def over_c(t, n=GC):
                return t.unsqueeze(2).to_broadcast([P, DG, n])

            link(TT(bb[:, :, :], bm[:, :, :], over_c(f[14]), ALU.mult))
            link(TT(bm[:, :, :], bsw[:, :, :], over_c(f[15]), ALU.mult))
            link(TT(bb[:, :, :], bb[:, :, :], bm[:, :, :], ALU.add))
            dve.tensor_copy(bsw[0:64, :, :], bb[64:128, :, :])
            link(dve.tensor_copy(bsw[64:128, :, :], bb[0:64, :, :]))
            dve.wait_ge(s5_act, 3)
            link(TS(cm[:, :, :], cm[:, :, :], nsgn[:, 0:1], None, ALU.mult))
            dve.tensor_copy(csw[0:64, :, :], cm[64:128, :, :])
            link(dve.tensor_copy(csw[64:128, :, :], cm[0:64, :, :]))
            for h in range(2):
                dve.sem_inc(slot_read[(JOB["ct"] + h) % 4], 1)

            for b in range(8):
                gs = slice(8 * b, 8 * b + 8)
                fwd = b < 4

                def power(t, n, rev):
                    w = t[:, 0:n, gs]
                    if rev:
                        w = w[:, ::-1, :]
                    return w.rearrange("p s g -> p g s").unsqueeze(3).to_broadcast([P, 8, n, GC])

                def matrix(t, n):
                    return t[:, gs, :].unsqueeze(2).to_broadcast([P, 8, n, GC])

                if b >= 2:
                    is_done(dve, JOB["prep"] + 2 * (b - 2) + 1)
                    dve.wait_ge(c_out[b % 2], 16 * (b // 2))
                o = bp[:, b % 2, :, :, :]
                tmp = ptmp[:, :, 0:CH, :]
                link(TT(o, power(pr, CH, fwd), matrix(bb, CH), ALU.mult))
                link(TT(tmp, power(pis, CH, fwd), matrix(bsw, CH), ALU.mult))
                link(TT(o, o, tmp, ALU.add))
                dve.sem_inc(bp_ok, 1)
                o = cp[:, b % 2, :, :, :]
                tmp = ptmp[:, :, :, :]
                link(TT(o, power(pr, 9, not fwd), matrix(cm, 9), ALU.mult))
                link(TT(tmp, power(pin, 9, not fwd), matrix(csw, 9), ALU.mult))
                link(TT(o, o, tmp, ALU.add))
                dve.sem_inc(bp_ok, 1)
                j = JOB["prep"] + 2 * b + 1
                is_done(dve, j)
                g0 = 8 * (b % 4)
                for half in range(2):
                    gh = slice(g0 + 4 * half, g0 + 4 * half + 4)
                    src = (lat, ctx_)[half](j)[0:GC, :].rearrange("p (g t c) -> p g t c", g=4, c=GC)
                    if fwd:
                        ins = dve.tensor_copy(kf[:, gh, 7:15, :], src)
                    else:
                        dve.tensor_copy(kf[:, gh, 0:7, :], src[:, :, 0:7, :])
                        ins = TT(kf[:, gh, 7, :], src[:, :, 7, :], kf[:, gh, 7, :], ALU.add)
                ins.then_inc(slot_read[j % 4], 1)
                was_read(dve, j)
            tmp = ptmp[0:GC, :, :, :].rearrange("p a b c -> p (a b c)")[:, 0:G * GC].rearrange("p (g c) -> p g c", g=G)
            link(TT(tmp, dg5[:, :].unsqueeze(2).to_broadcast([GC, G, GC]),
                    ident[0:GC, 0:GC].unsqueeze(1).to_broadcast([GC, G, GC]), ALU.mult))
            TT(kf[:, :, 7, :], kf[:, :, 7, :], tmp, ALU.add).then_inc(k_ok, 1)

            def ada_batch(j, dst, nt, b_cols):
                TT(dst, ada_cols(j, nt), b_cols.unsqueeze(2).to_broadcast([P, nt, 2]), ALU.add)\
                    .then_inc(slot_read[j % 4], 1)

            def scale_cols(q, g_row):
                STT(amul[:, q, :, :], mod[:, 24 * q + 8:24 * q + 16, :], 1.0,
                    vt[:, g_row:g_row + 8].unsqueeze(2).to_broadcast([P, 8, 2]), ALU.add, ALU.mult).then_inc(cols_ok, 1)

            dve.wait_ge(silu_c, 1)
            is_done(dve, JOB["ada"])
            ada_batch(JOB["ada"], mod[:, 0:ADA0, :], ADA0, vt[:, 0:ADA0])
            was_read(dve, JOB["ada"])
            scale_cols(0, 72)

            def norm(q, j, n):
                for k in range(KD):
                    dve.wait_ge(sq_ok, KD * q + k + 1)
                    if k == 0:
                        dve.tensor_copy(ssq[:, 0:n], silu[:, 0, 0:n]).then_inc(ssq_ok, 1)
                    else:
                        dve.wait_ge(ssq_ok, KD * q + k)
                        TT(ssq[:, 0:n], ssq[:, 0:n], silu[:, k % 2, 0:n], ALU.add).then_inc(ssq_ok, 1)
                was_read(dve, j)
                link(dve.reciprocal(rstd[:, 0:n], rstd[:, 0:n]))
                if q == 3:
                    for k in range(KD):
                        STT(x[:, k, 0:n], x[:, k, 0:n], vt[:, 96 + k:97 + k], rstd[:, 0:n], ALU.mult, ALU.mult)\
                            .then_inc(fin_ok, 1)
                    return
                parts = [(slice(0, NL), 0)] + ([(slice(NL, NT), 1)] if n == NT else [])

                def xn(k):
                    if k >= 2:
                        dve.wait_ge(h_hi_ok, KD * q + k - 1)
                    TT(gu[:, k % 2, 0:n], x[:, k, 0:n], rstd[:, 0:n], ALU.mult).then_inc(xn_ok, 1)

                for k in range(KD):
                    xn(k)
                    dve.wait_ge(xn_ok, KD * q + k + 1)
                    for c, v in parts:
                        ins = TS(silu[:, k % 2, c], gu[:, k % 2, c], amul[:, q, k, v:v + 1],
                                 mod[:, 24 * q + k, v:v + 1], ALU.mult, ALU.add)
                    link(ins)
                    dve.wait_ge(h_hi_ok, KD * q + k + 1)
                    TT(h_lo[:, k, 0:n], silu[:, k % 2, 0:n], h_hi[:, k, 0:n].bitcast(F32), ALU.subtract)\
                        .then_inc(h_ok, 1)

            def ffn(jobs, n, q, act_base):
                def seg(i, tiles):
                    js = Seg(jobs, tiles, q == 0)
                    jseg = 2 * SEG * js.step + KD

                    def done(j):
                        dve.wait_ge(job_done, (j + 1) + i * jseg)

                    def read(j):
                        dve.wait_ge(slot_read[j % 4], (j // 4 + 1) + i * (jseg // 4))

                    def modulation(v):
                        j = js.ada(v)
                        done(j)
                        if tiles == SEG:
                            t = bass.ds(i * 8 + (ADA0 + v), 1)
                            ada_batch(j, mod[:, t, :], 1, vt[:, t])
                        else:
                            t = ADA0 + 8 * NSEG + 4 * v
                            ada_batch(j, mod[:, t:t + 4, :], 4, vt[:, t:t + 4])

                    for f_ in range(tiles):
                        jg, ju = js.gu(2 * f_), js.gu(2 * f_ + 1)
                        if q == 0:
                            modulation(2 * f_)
                        read(jg)
                        done(ju)
                        if n == NT:
                            dst, sl = (t[:, f_ % 2, :].rearrange("p (b c) -> p b c", b=2) for t in (gu, silu))
                            src = both(ju, 384)
                        else:
                            dst, src, sl = gu[:, f_ % 2, 0:n], lat(ju), silu[:, f_ % 2, 0:n]
                        STT(dst, src, 0.5, sl, ALU.mult, ALU.mult).then_inc(slot_read[ju % 4], 1)
                        read(ju)
                        dve.wait_ge(act_hi_ok, (act_base + f_ + 1) + i * SEG)
                        TT(act_lo[:, f_, 0:n], gu[:, f_ % 2, 0:n], act_hi[:, f_, 0:n].bitcast(F32), ALU.subtract)\
                            .then_inc(act_lo_ok, 1)
                        if q == 0:
                            modulation(2 * f_ + 1)
                    if q == 0:
                        for v in range(2 * tiles - 2, 2 * tiles):
                            read(js.ada(v))
                    for k in range(KD):
                        j = js.down(k)
                        done(j)
                        g = 24 * q + 16 + k
                        ins = STT(x[:, k, 0:NL], lat(j), mod[:, g, 0:1], x[:, k, 0:NL], ALU.mult, ALU.add)
                        if n == NT:
                            ins = STT(x[:, k, NL:NT], ctx_(j)[:, 0:NC], mod[:, g, 1:2], x[:, k, NL:NT],
                                      ALU.mult, ALU.add)
                        ins.then_inc(slot_read[j % 4], 1)
                    read(js.down(KD - 1))

                with dve.Fori(0, NSEG) as i:
                    seg(i, SEG)
                seg(NSEG, TAIL)

            norm(0, JOB["norm0"], NT)
            ffn(JOB["ffn1"], NT, 0, 0)
            scale_cols(1, 80)
            scale_cols(2, 88)
            norm(1, JOB["norm1"], NT)

            for q in range(4):
                was_read(dve, JOB["xs"] + 12 + q)

            def step(jj, count, first=False):
                prev, cur = xs[:, jj - 1, :], xs[:, jj, :]
                if isinstance(jj, int) is False:
                    prev = xs[:, bass.ds(jj - 1, 1), :].rearrange("p a g -> p (a g)")
                    cur = xs[:, bass.ds(jj, 1), :].rearrange("p a g -> p (a g)")
                if not first:
                    dve.wait_ge(scan_step, count)
                TT(st1[:, :], prev, lam8[:, 0, :], ALU.mult).then_inc(scan_step, 1)
                TT(st2[0:64, :], prev[64:128, :], lam8[64:128, 1, :], ALU.mult).then_inc(scan_step, 1)
                TT(st2[64:128, :], prev[0:64, :], lam8[0:64, 1, :], ALU.mult).then_inc(scan_step, 1)
                dve.wait_ge(scan_step, count + 1)
                TT(cur, cur, st1[:, :], ALU.add).then_inc(scan_step, 1)
                dve.wait_ge(scan_step, count + 4)
                TT(cur, cur, st2[:, :], ALU.add).then_inc(scan_step, 1)

            step(1, 0, first=True)
            with dve.Fori(0, 31) as i:
                for q in range(3):
                    jj = i * 3 + (2 + q)
                    count = i * 15 + (5 + 5 * q)
                    prev = xs[:, bass.ds(i * 3 + (1 + q), 1), :].rearrange("p a g -> p (a g)")
                    cur = xs[:, bass.ds(i * 3 + (2 + q), 1), :].rearrange("p a g -> p (a g)")
                    dve.wait_ge(scan_step, count)
                    TT(st1[:, :], prev, lam8[:, 0, :], ALU.mult).then_inc(scan_step, 1)
                    TT(st2[0:64, :], prev[64:128, :], lam8[64:128, 1, :], ALU.mult).then_inc(scan_step, 1)
                    TT(st2[64:128, :], prev[0:64, :], lam8[0:64, 1, :], ALU.mult).then_inc(scan_step, 1)
                    dve.wait_ge(scan_step, i * 15 + (5 + 5 * q + 1))
                    TT(cur, cur, st1[:, :], ALU.add).then_inc(scan_step, 1)
                    dve.wait_ge(scan_step, i * 15 + (5 + 5 * q + 4))
                    TT(cur, cur, st2[:, :], ALU.add).then_inc(scan_step, 1)
            dve.wait_ge(scan_step, 5 * 94)
            is_done(dve, JOB["gb"] + 7)
            dve.tensor_copy(hb[:, :, :], xs[:, NC // CH - 1:NC // CH - 1 + LCH, G:DG][:, ::-1, :]).then_inc(states_ok, 1)
            for c in range(4):
                j = JOB["yt"] + c
                dve.wait_ge(yh_ok, c + 1)
                TT(y_lo[:, c, :], y32[:, c, :], y_hi[:, c, :].bitcast(F32), ALU.subtract).then_inc(yl_ok, 1)
                dve.sem_inc(slot_read[j % 4], 1)
            for c in range(4):
                was_read(dve, JOB["glu"] + c)
                TT(y32[:, c, :], y32[:, c, :], gate_buf[:, c % 2, :], ALU.mult).then_inc(ya_ok, 1)
            for c in range(4):
                dve.wait_ge(glu_sig, c + 1)
                dve.wait_ge(ya_ok, 4)
                TT(ya_lo[:, c, :], y32[:, c, :], ya_hi[:, c, :].bitcast(F32), ALU.subtract).then_inc(yal_ok, 1)

            dve.wait_ge(masks_ok, 3)
            is_done(dve, JOB["gb"] + 7)
            for t in (tri[0:64, 0, 64:128], tri[64:128, 1, 0:64], kz[:, :, :], qz[:, :, :, :], at_sb[:, :, :, :, :]):
                link(dve.memset(t, 0.0))
            j = JOB["gla"]
            for ti in range(2):
                for d in range(2):
                    p_ = 2 * ti + d
                    gb_col = vt[:, 124 + 2 * d + ti:125 + 2 * d + ti]
                    is_done(dve, j)
                    dve.wait_ge(z_a, p_ + 1)
                    link(TS(g_b[:, :].rearrange("p (b c) -> p b c", b=2), both(j, 384), gb_col, 0.0, ALU.add, ALU.min))
                    dve.sem_inc(slot_read[j % 4], 1)
                    j += 1
                    link(TT(g_b[:, :], g_b[:, :], g_a[:, :], ALU.subtract))
                    if d == 0:
                        link(dve.tensor_tensor_scan(g_c[:, :], zmask[:, :], g_b[:, :], 0.0, ALU.mult, ALU.add))
                    else:
                        link(dve.tensor_tensor_scan(g_c[:, ::-1], zmask[:, :], g_b[:, ::-1], 0.0, ALU.mult, ALU.add))
                    gv = g_c[:, :].rearrange("p (c t) -> p c t", t=LC)
                    ref, last = (LC // 2, LC - 1) if d == 0 else (LC // 2 - 1, 0)
                    TT(g_b[:, 0:NL].rearrange("p (c t) -> p c t", t=LC), gv[:, 0:8, :],
                       gv[:, 0:8, ref:ref + 1].to_broadcast([P, 8, LC]), ALU.subtract)
                    TT(g_d[:, :].rearrange("p (c t) -> p c t", t=LC), gv[:, :, last:last + 1].to_broadcast([P, 12, LC]),
                       gv, ALU.subtract).then_inc(z_d, 1)
                    dve.wait_ge(e_a, 4 * p_ + 1)
                    TT(e1q[:, :], qt[:, ti, :], g_a[:, 0:NL], ALU.mult).then_inc(z_d, 1)
                    dve.wait_ge(e_a, 4 * p_ + 2)
                    for hp in range(2):
                        r = slice(64 * hp, 64 * hp + 64)
                        TT(kz[r, hp, :], kt[r, ti, 0:NL], g_a[r, 0:NL], ALU.mult)
                    dve.wait_ge(e_a, 4 * p_ + 4)
                    for hp in range(2):
                        r = slice(64 * hp, 64 * hp + 64)
                        TT(qz[r, d, hp, :], qt[r, ti, :], g_c[r, 0:NL], ALU.mult)
                    TT(ke[:, :], kt[:, ti, :], g_d[:, :], ALU.mult).then_inc(e_d, 1)
                    j += 1
                    for hp in range(2):
                        is_done(dve, j)
                        dve.copy_predicated(at_sb[:, d, hp, :, :],
                                            tri[:, d, :].unsqueeze(1).to_broadcast([P, 4, P]).bitcast(I32),
                                            lat(j).rearrange("p (t c) -> p t c", t=4)).then_inc(slot_read[j % 4], 1)
                        j += 1
                    order = (4, 5, 0, 1, 2, 3) if d == 0 else (5, 4, 3, 2, 1, 0)
                    nth = 0
                    prev = None
                    for half in range(2):
                        is_done(dve, j)
                        for q in range(3):
                            t = order[3 * half + q]
                            for par in ((0, 1) if d == 0 else (1, 0)):
                                c = 2 * t + par
                                kv = (lat, ctx_)[par](j)[:, P * q:P * q + P]
                                if nth < 3:
                                    nxt = s_cur[:, d, nth % 2, :]
                                elif nth < 11:
                                    nc_ = nth - 3
                                    nxt = s_st[:, d, nc_ if d == 0 else 7 - nc_, :]
                                else:
                                    nxt = None
                                if nth == 0:
                                    link(dve.tensor_copy(nxt, kv))
                                elif nxt is not None:
                                    link(STT(nxt, prev, decay[:, c:c + 1], kv, ALU.mult, ALU.add))
                                prev = nxt
                                nth += 1
                        dve.sem_inc(slot_read[j % 4], 1)
                        j += 1
                    dve.sem_inc(s_ok, 1)
                j += 4
            dve.wait_ge(o_ok, 8)
            ov = o_sb[:, :, :].rearrange("p t (h e) -> p (t h) e", h=HEADS)
            link(TT(osq[:, :, :], o_sb[:, :, :], o_sb[:, :, :], ALU.mult))
            dve.tensor_reduce(oms[:, :], osq[:, :, :].rearrange("p t (h e) -> p (t h) e", h=HEADS), AX.X, ALU.add)\
                .then_inc(o_rs, 1)
            dve.wait_ge(o_rs, 2)
            link(dve.reciprocal(oms[:, :], oms[:, :]))
            TT(ov, ov, oms[:, :].unsqueeze(2).to_broadcast([P, 16, DV]), ALU.mult).then_inc(ybtok_ok, 1)
            for c in range(4):
                j = JOB["ybt"] + c
                is_done(dve, j)
                STT(r_sb[:, c, :].rearrange("p (r w) -> p r w", w=GRID_W), lat(j).rearrange("p (w r) -> p r w", r=ROWS),
                    gn[:, c:c + 1], r_sb[:, c, :].rearrange("p (r w) -> p r w", w=GRID_W), ALU.mult, ALU.mult)\
                    .then_inc(slot_read[j % 4], 1)
            for c in range(4):
                dve.wait_ge(ybh_ok, c + 1)
                TT(yb_lo[:, c, :], r_sb[:, c, :], yb_hi[:, c, :].bitcast(F32), ALU.subtract).then_inc(yb_ok, 1)
            for t in range(KD):
                ja = JOB["merge"] + 4 * (t // 2) + t % 2
                jb = ja + 2
                dve.wait_ge(gate_in[t % 2], 32 * (t // 2 + 1))
                if t >= 2:
                    dve.wait_ge(mh_ok, t - 1)
                is_done(dve, ja)
                TT(mt[:, t % 2, 0, :], lat(ja), gates[:, t % 2, 0, :], ALU.mult).then_inc(slot_read[ja % 4], 1)
                is_done(dve, jb)
                TT(mt[:, t % 2, 1, :], lat(jb), gates[:, t % 2, 1, :], ALU.mult).then_inc(slot_read[jb % 4], 1)
                was_read(dve, ja)
                was_read(dve, jb)
                TT(mt[:, t % 2, 2, :], mt[:, t % 2, 0, :], mt[:, t % 2, 1, :], ALU.add).then_inc(m32_ok, 1)
                dve.wait_ge(m32_ok, t + 1)
                dve.wait_ge(mh_ok, t + 1)
                TT(m_lo[:, t, :], mt[:, t % 2, 2, :], m_hi[:, t, :].bitcast(F32), ALU.subtract).then_inc(m_ok, 1)
            dve.wait_ge(x_back, 16)
            for k in range(KD):
                j = JOB["wo"] + k
                is_done(dve, j)
                STT(x[:, k, 0:NL], lat(j), mod[:, 40 + k, 0:1], x[:, k, 0:NL], ALU.mult, ALU.add)\
                    .then_inc(slot_read[j % 4], 1)
            norm(2, JOB["norm2"], NL)
            ffn(JOB["ffn2"], NL, 2, FF // P)
            norm(3, JOB["norm3"], NL)


_INS = ['x', 'c', 'ctx', 'c_ctx', 'ada_w', 'ada_b', 'ffn1_norm', 'ffn1_w_gate', 'ffn1_w_up', 'ffn1_w_down', 'mix_norm',
        'w_in', 's5_lambda_re', 's5_lambda_im', 's5_log_dt', 's5_b_re', 's5_b_im', 's5_c_re', 's5_c_im', 's5_d',
        's5_glu_w', 's5_glu_b', 's5_out', 'gla_gate_up', 'gla_gate_b', 'gla_norm', 'gla_out', 'w_o', 'ffn2_norm',
        'ffn2_w_gate', 'ffn2_w_up', 'ffn2_w_down', 'final_norm']


def kernel(**inputs):
    import numpy as _np
    import concourse.bacc as _bacc
    from concourse import mybir as _mybir
    from concourse.bass_utils import run_bass_kernel_spmd as _run

    nc = _bacc.Bacc("TRN2", target_bir_lowering=False, num_devices=1)
    arrays, args = {}, {}
    for name in _INS:
        v = _np.ascontiguousarray(inputs[name])
        arrays[f"in_{name}_dram"] = v
        args[name] = nc.dram_tensor(f"in_{name}_dram", v.shape, _mybir.dt.from_np(v.dtype), kind="ExternalInput").ap()
    out = nc.dram_tensor("out_0_dram", (1, NL, D), _mybir.dt.float32, kind="ExternalOutput").ap()
    build(nc, args, out)
    r = _run(nc, [arrays], core_ids=[0])
    return r.results[0]["out_0_dram"]
```

```python
from contextlib import ExitStack
import math

import numpy as np
import concourse.bass as bass
from concourse import mybir

F32 = mybir.dt.float32
F32R = mybir.dt.float32r
I32 = mybir.dt.int32
ALU = mybir.AluOpType
ACT = mybir.ActivationFunctionType
AX = mybir.AxisListType

P = 128
D = 1024
KD = D // P
FF = 2816
NL, NC = 512, 256
NT = NL + NC
EPS = 1e-6
G, GC, SP5 = 32, 16, 64
W5 = G * GC
NDIR = 2
DG = NDIR * G
CH = 8
NCH = NT // CH
LCH = NL // CH
HEADS, DK, DV = 4, 64, 128
KEY, VAL = HEADS * DK, HEADS * DV
RANK = 16
LC = 64
GRID_W = 64
ROWS = NL // GRID_W
C_U, C_Q, C_K, C_V, C_R, C_G = 0, 512, 768, 1024, 1536, 2048
C_GA, C_GB = 2080, 3104

SEG = 4
NSEG = FF // P // SEG
TAIL = FF // P - NSEG * SEG
SLOTS = 4
USEG = 2 * SEG + 4
FFN_UNITS = NSEG * USEG + 2 * TAIL + 4


class Seg:
    def __init__(self, jobs, tiles, side):
        self.jobs, self.step = jobs, 2 if side else 1
        self.down0 = 2 * tiles * self.step
        self.count = self.down0 + KD

    def gu(self, v):
        return self.jobs + v * self.step

    def side(self, v):
        return self.jobs + v * self.step + 1

    def down(self, k):
        return self.jobs + self.down0 + k


class Part:
    def __init__(self, reps, tiles, side, segs, units, jobs):
        self.reps, self.tiles, self.side, self.segs, self.units, self.jobs = reps, tiles, side, segs, units, jobs
        self.useg = 2 * tiles + 4
        self.jseg = Seg(0, tiles, side).count


def _parts(spec):
    parts, segs, units, jobs = [], 0, 0, 0
    for reps, tiles, side in spec:
        p = Part(reps, tiles, side, segs, units, jobs)
        parts.append(p)
        segs, units, jobs = segs + reps, units + reps * p.useg, jobs + reps * p.jseg
    return parts, jobs


BATCHES = G // 8
assert BATCHES == NSEG - 1
PARTS1, FFN1_JOBS = _parts([(1, SEG, False), (NSEG - 1, SEG, True), (1, TAIL, False)])
PARTS2, FFN2_JOBS = _parts([(NSEG, SEG, False), (1, TAIL, False)])

ADA_START = 2
ADA_RING0, ADA_RING = 6, 2
ADA_LAST = ADA_START + NSEG + 1

UNIT, JOB = {}, {}


def _number(table, parts):
    n = 0
    for name, count in parts:
        table[name] = n
        n += count
    table["end"] = n


_number(UNIT, [("ffn1", FFN_UNITS), ("u", 4), ("glr", 1), ("k", 2), ("q", 2), ("v", 4), ("r", 4), ("ga", 8),
               ("gb", 8), ("glu", 2), ("merge", 8), ("wo", 8), ("ffn2", FFN_UNITS)])
_number(JOB, [("x", KD), ("vec", 1), ("lam", 1), ("norm0", 1), ("ada", ADA_START), ("ffn1", FFN1_JOBS), ("norm1", 1),
              ("u", CH), ("glr", 1), ("k", 2), ("q", 2), ("ada8", 1), ("ut", 8), ("xs", 16), ("v", 4), ("vt", 6), ("r", 4),
              ("ga", 8), ("gb", 8), ("z0", 1), ("y", 8), ("yt", 4), ("glu", 4), ("gla", 31), ("ybt", 4), ("merge", 16),
              ("wo", KD), ("norm2", 1), ("ffn2", FFN2_JOBS), ("norm3", 1), ("out", 4)])
NADA = 9 * KD

GJ = {("z", 0): JOB["z0"]}


def _gla_jobs():
    n = JOB["gla"]
    for p in range(4):
        for name, count in (("z", int(p < 3)), ("ket", 1), ("sc", 2), ("kv", 2), ("out", 4 * (p % 2))):
            if count:
                GJ[(name, p + 1 if name == "z" else p)] = n
            n += count
    assert n == JOB["ybt"]


_gla_jobs()


def last_user(n):
    for name in ("glr", "k", "q", "v", "r", "ga", "gb", "wo"):
        if UNIT[name] <= n < UNIT[name] + {"glr": 1, "k": 2, "q": 2, "v": 4, "r": 4}.get(name, 8):
            return JOB[name] + n - UNIT[name]
    for name in ("glu", "merge"):
        if UNIT[name] <= n < UNIT[name] + {"glu": 2, "merge": 8}[name]:
            return JOB[name] + 2 * (n - UNIT[name]) + 1
    if UNIT["u"] <= n < UNIT["u"] + 4:
        return JOB["u"] + CH - 1
    v = n - (UNIT["u"] - 4)
    if 0 <= v < 4:
        return JOB["norm1"] - KD + 2 * v + 1
    raise ValueError(n)

TWO_PI = 2 * math.pi
PI_1 = 6.28125
PI_2 = float(np.float32(np.round((TWO_PI - PI_1) * 2**20) / 2**20))
PI_3 = float(np.float32(TWO_PI - PI_1 - PI_2))
ROUND = 12582912.0
PI_MAX = 3.1415925


def build(nc, a, out):
    b_scr = nc.dram_tensor("b_scr", [DG, P, P], F32).ap()
    c_scr = nc.dram_tensor("c_scr", [P, DG, 9, GC], F32).ap()
    k_scr = nc.dram_tensor("k_scr", [GC, G, 15, GC], F32).ap()
    x_scr = nc.dram_tensor("x_scr", [P, KD, NL], F32).ap()
    g_scr = nc.dram_tensor("g_scr", [P, 2 * KD, NL], F32).ap()

    base = (nc.sbuf_base + 63) // 64 * 64
    top = [base]

    def place(name, shape, dt, at=None):
        size = int(np.prod(shape[1:])) * 4
        off = top[0] if at is None else at
        t = nc.alloc_sbuf_tensor_at(name, shape, dt, offset=off)
        if at is None:
            top[0] += (size + 63) // 64 * 64
        assert off + size <= nc.sbuf_usable_end, (name, off + size)
        return t

    KB = 1024
    w_raw = place("w_raw", [P, SLOTS, 1024], F32)
    w_hi = place("w_hi", [P, SLOTS, 1024], F32R)
    w_lo = place("w_lo", [P, SLOTS, 1024], F32R)
    h_at = top[0]
    h_hi = place("h_hi", [P, KD, NT], F32R)
    h_lo = place("h_lo", [P, KD, NT], F32R)
    x_at = top[0]
    x = place("x", [P, KD, NT], F32)
    ident = place("ident", [P, P], F32)
    ones = place("ones", [P, P], F32)
    vt = place("vt", [P, P], F32)
    mod = place("mod", [P, NADA, 2], F32)
    amul = place("amul", [P, 3, KD, 2], F32)
    cs = place("cs", [P, KD, 2], F32)
    eps = place("eps", [P, 1], F32)
    halfpi = place("halfpi", [P, 1], F32)
    sgn = place("sgn", [P, 1], F32)
    nsgn = place("nsgn", [P, 1], F32)
    lam8 = place("lam8", [P, 2, DG], F32)
    gn_in = place("gn_in", [4, P], F32)
    gn = place("gn", [P, 4], F32)
    hb = place("hb", [P, LCH, G], F32, at=h_at + 40 * KB)
    dg5 = place("dg5", [GC, G], F32)
    decay = place("decay", [P, 2, 12], F32)
    oms = place("oms", [P, 16], F32)
    scratch_at = top[0]
    vecs = place("vecs", [P, P], F32, at=scratch_at)
    act_hi = place("act_hi", [P, SEG, NT], F32R)
    act_lo = place("act_lo", [P, SEG, NT], F32R)
    silu = place("silu", [P, 2, NT], F32)
    gu = place("gu", [P, 2, NT], F32)
    ssq = place("ssq", [P, NT], F32)
    rstd = place("rstd", [P, NT], F32)
    s5_at = top[0] - 2 * NT * 4
    ada_at = (nc.sbuf_usable_end - 4 * (ADA_RING + 2) * D) // 64 * 64
    ada_w = place("ada_w", [P, ADA_RING, D], F32, at=ada_at)
    ada_acc = place("ada_acc", [P, 2, D], F32, at=ada_at + 4 * ADA_RING * D)

    m = [scratch_at]

    def mix(name, shape, dt=F32):
        size = int(np.prod(shape[1:])) * 4
        t = place(name, shape, dt, at=m[0])
        m[0] += (size + 63) // 64 * 64
        return t

    u_at = m[0]
    u_tok = mix("u_tok", [NCH, G, CH, GC])
    ut_at = m[0]
    ut = mix("ut", [P, G, NCH])
    qt = mix("qt", [P, 2, NL])
    kt = mix("kt", [P, 2, NT])
    v_sb = mix("v_sb", [P, 6, VAL])
    r_sb = mix("r_sb", [P, 4, NL])
    glr = mix("glr", [2 * RANK, NT])
    zmask = mix("zmask", [P, NT])
    tri = mix("tri", [P, 2, P])
    gate_up = mix("gate_up", [2 * RANK, 2, KEY])
    stream_at = m[0]
    stream = mix("stream", [P, 3, 1024])
    stream2 = place("stream2", [P, 2, 3, 4, P], F32, at=stream_at)
    xs_at = x_at
    xs = place("xs", [P, NCH, DG], F32, at=x_at)
    st1 = mix("st1", [P, DG])
    st2 = mix("st2", [P, DG])
    gate_buf = mix("gate_buf", [P, 2, NL])
    assert m[0] <= nc.sbuf_usable_end
    v_t = place("v_t", [P, 4, NT], F32, at=stream_at)
    y_tok = place("y_tok", [LCH, CH, W5], F32, at=u_at)
    y32 = place("y32", [P, 4, NL], F32, at=xs_at)
    y_hi = place("y_hi", [P, 4, NL], F32R, at=xs_at + 8 * KB)
    y_lo = place("y_lo", [P, 4, NL], F32R, at=xs_at + 16 * KB)
    ya_hi = place("ya_hi", [P, 4, NL], F32R, at=ut_at)
    e1q = place("e1q", [P, NL], F32, at=h_at)
    kz = place("kz", [P, 2, NL], F32, at=h_at + 2 * KB)
    qz = place("qz", [P, 2, 2, NL], F32, at=h_at + 6 * KB)
    ke = place("ke", [P, NT], F32, at=h_at + 14 * KB)
    ket = place("ket", [P, 6, P], F32, at=h_at + 17 * KB)
    at_sb = place("at_sb", [P, 2, 2, 4, P], F32, at=h_at + 20 * KB)
    g_a = [place("g_a0", [P, NT], F32, at=h_at + 28 * KB), place("g_a1", [P, NT], F32, at=u_at + 12 * KB)]
    g_b = place("g_b", [P, NT], F32, at=h_at + 31 * KB)
    g_c = place("g_c", [P, NT], F32, at=h_at + 34 * KB)
    g_d = place("g_d", [P, NT], F32, at=h_at + 37 * KB)
    s_st = place("s_st", [P, 2, 8, DV], F32, at=u_at)
    s_cur = place("s_cur", [P, 2, 2, DV], F32, at=u_at + 8 * KB)
    o_sb = place("o_sb", [P, 4, VAL], F32, at=h_at + 40 * KB)
    osq = place("osq", [P, 4, VAL], F32, at=h_at)
    yb_hi = place("yb_hi", [P, 4, NL], F32R, at=xs_at)
    yb_lo = place("yb_lo", [P, 4, NL], F32R, at=xs_at + 8 * KB)
    ya_lo = place("ya_lo", [P, 4, NL], F32R, at=xs_at + 16 * KB)
    m_hi = place("m_hi", [P, KD, NL], F32R, at=h_at)
    m_lo = place("m_lo", [P, KD, NL], F32R, at=h_at + 16 * KB)
    mt = place("mt", [P, 2, 3, NL], F32, at=h_at + 32 * KB)
    gates = place("gates", [P, 2, 2, NL], F32, at=u_at)

    x_in = place("x_in", [P, 6, D], F32, at=h_at)
    ada_w0 = place("ada_w0", [P, ADA_RING0, D], F32, at=h_at + 24 * KB)

    s5p = [s5_at]

    def prep(name, shape):
        t = place(name, shape, F32, at=s5p[0])
        s5p[0] += (int(np.prod(shape[1:])) * 4 + 63) // 64 * 64
        assert s5p[0] <= ada_at, name
        return t

    bm = prep("bm", [P, NDIR, 8, GC])
    bms = prep("bms", [P, NDIR, 8, GC])
    c_in = prep("c_in", [P, NDIR, 3, SP5])
    bb_t = prep("bb_t", [P, NDIR, 8, GC])
    kf = prep("kf", [GC, 4, 15, GC])
    powers = prep("powers", [P, 2, 9, DG])
    pr, pis = powers[:, 0, :, :], powers[:, 1, :, :]
    pw = prep("pw", [P, 2, 9, 4])
    coef = prep("coef", [P, 2, DG])
    bb = prep("bb", [P, NDIR, 8, GC])
    bbs = prep("bbs", [P, NDIR, 8, GC])
    cm = prep("cm", [P, NDIR, 8, GC])
    cms = prep("cms", [P, NDIR, 8, GC])
    s5t_at = s5p[0]
    bp = prep("bp", [P, 4, CH, GC])
    cp = prep("cp", [P, 2, 4, 9, GC])
    ptmp = prep("ptmp", [P, 4, 9, GC])
    bt_sb = prep("bt_sb", [P, 4, P])
    s5t = place("s5t", [P, 16, DG], F32, at=s5t_at)
    lam_in = place("lam_in", [DG, 2, P], F32, at=s5t_at + 4 * KB)
    out_sb = place("out_sb", [P, 2, D], F32, at=h_at)

    ps = nc.alloc_psum_tensor("ps", [P, 8, 512], F32)

    def lat(j):
        return ps[:, 2 * (j % 4), :]

    def ctx_(j):
        return ps[:, 2 * (j % 4) + 1, :]

    def both(j, n):
        return ps[:, 2 * (j % 4):2 * (j % 4) + 2, 0:n]

    def ada_cols(j, c0=0):
        return lat(j)[:, c0:c0 + 2 * KD].rearrange("p (t v) -> p t v", v=2)

    ADA_COL = 384

    with ExitStack() as es:
        def sem(name):
            return es.enter_context(nc.semaphore(name))

        job_done = sem("job_done")
        slot_read = [sem(f"slot_read{s}") for s in range(4)]
        w_here = [sem(f"w_here{s}") for s in range(4)]
        w_split = sem("w_split")
        hi_made = sem("hi_made")
        ada_here0 = [sem(f"ada_first{s}") for s in range(ADA_RING0)]
        ada_here = [sem(f"ada_here{s}") for s in range(ADA_RING)]
        acc_ok = sem("acc_ok")
        consts = sem("consts")
        small_in = sem("small_in")
        vec_in = sem("vec_in")
        s5_in = sem("s5_in")
        s5_own = sem("s5_own")
        s5_in_used = sem("s5_in_used")
        x_landed = sem("x_landed")
        silu_c = sem("silu_c")
        cols_ok = sem("cols_ok")
        act_hi_ok = sem("act_hi_ok")
        act_lo_ok = sem("act_lo_ok")
        sq_ok = sem("sq_ok")
        ssq_ok = sem("ssq_ok")
        rms_ok = sem("rms_ok")
        rstd_ok = sem("rstd_ok")
        xn_ok = sem("xn_ok")
        h_hi_ok = sem("h_hi_ok")
        h_ok = sem("h_ok")
        dve_own = sem("dve_own")
        act_own = sem("act_own")
        pool_own = sem("pool_own")
        slot_taken = sem("slot_taken")
        s5_act = sem("s5_act")
        s5_dve = sem("s5_dve")
        bp_ok = sem("bp_ok")
        bt_ok = sem("bt_ok")
        c_out = [sem("c_out0"), sem("c_out1")]
        b_out = sem("b_out")
        k_ok = sem("k_ok")
        k_out = sem("k_out")
        x_spilled = sem("x_spilled")
        x_back = sem("x_back")
        st_here = [sem(f"st_here{s}") for s in range(3)]
        st_used = sem("st_used")
        scan_step = sem("scan_step")
        states_ok = sem("states_ok")
        ytok_ok = sem("ytok_ok")
        yh_ok = sem("yh_ok")
        yl_ok = sem("yl_ok")
        glu_sig = sem("glu_sig")
        ya_ok = sem("ya_ok")
        yal_ok = sem("yal_ok")
        gate_sig = sem("gate_sig")
        gate_out = [sem("gate_out0"), sem("gate_out1")]
        gate_in = [sem(f"gate_in{s}") for s in range(2)]
        gla_c = sem("gla_c")
        masks_ok = sem("masks_ok")
        z_a = sem("z_a")
        z_d = sem("z_d")
        e_a = sem("e_a")
        e_d = sem("e_d")
        keyt_ok = sem("keyt_ok")
        s_ok = sem("s_ok")
        o_ok = sem("o_ok")
        o_rs = sem("o_rs")
        ybh_ok = sem("ybh_ok")
        yb_ok = sem("yb_ok")
        ybtok_ok = sem("ybtok_ok")
        m32_ok = sem("m32_ok")
        mh_ok = sem("mh_ok")
        m_ok = sem("m_ok")
        fin_ok = sem("fin_ok")
        outc_ok = sem("outc_ok")
        out_done = [sem("out_done0"), sem("out_done1")]

        block = es.enter_context(nc.Block())

        def wait_read(eng, j):
            if j >= 4:
                eng.wait_ge(slot_read[j % 4], j // 4)

        def was_read(eng, j):
            eng.wait_ge(slot_read[j % 4], j // 4 + 1)

        def is_done(eng, j):
            eng.wait_ge(job_done, j + 1)

        S5_LINKS = 4 + 12 + 2
        SMALL = 7

        @block.sync
        def _(sp):
            def unit(n, src, view):
                s = n % 4 if isinstance(n, int) else None
                sp.wait_ge(w_split, n + 1)
                sp.dma_start(view, src).then_inc(w_here[s], 16)

            def raw(s, k, c):
                return w_raw[:, s, 0:k * c].rearrange("p (k c) -> p k c", k=k)

            def ada_src(g, k):
                return a["ada_w"][0][P * k:P * k + P, bass.ds(g * D, D)]

            def ada_tile(g, k, first=False):
                s = k % ADA_RING
                if not first:
                    sp.wait_ge(acc_ok, g * 16 + (2 * (k - ADA_RING) + 2))
                sp.dma_start(ada_w[:, s, :], ada_src(g, k)).then_inc(ada_here[s], 16)

            for t in range(4):
                sp.dma_start(x_in[:, t, :], a["x"][0, P * t:P * t + P, :]).then_inc(x_landed, 16)
            for t in range(2):
                sp.dma_start(x_in[:, 4 + t, :], a["ctx"][0, P * t:P * t + P, :]).then_inc(x_landed, 16)
            for t in range(ADA_START * KD):
                s = t % ADA_RING0
                if t >= ADA_RING0:
                    sp.wait_ge(acc_ok, 2 * (t - ADA_RING0) + 2)
                sp.dma_start(ada_w0[:, s, :], ada_src(t // KD, t % KD)).then_inc(ada_here0[s], 16)

            def s5_batch(i):
                sp.wait_ge(s5_in_used, i + 1)
                gs = bass.ds(i * 8, 8)
                for d in range(NDIR):
                    for q, name in enumerate(("s5_b_re", "s5_b_im")):
                        src = a[name][0, d, gs].rearrange("g p c -> p g c")
                        sp.dma_start(bm[64 * q:64 * q + 64, d, :, :], src).then_inc(s5_in, 16)
                        sp.dma_start(bms[64 - 64 * q:128 - 64 * q, d, :, :], src).then_inc(s5_in, 16)
                    for q, name in enumerate(("s5_c_re", "s5_c_im", "s5_c_re")):
                        sp.dma_start(c_in[:, d, q, :], a[name][0, d, gs].rearrange("g c p -> (g c) p"))\
                            .then_inc(s5_in, 16)

            def ffn(first, pre, parts, with_ada):
                wg, wu, wd = (a[f"{pre}_{w}"][0] for w in ("w_gate", "w_up", "w_down"))
                gu_src = [w.rearrange("(k p) c -> p k c", p=P) for w in (wg, wu)]
                wd_src = wd.rearrange("(k p) c -> p k c", p=P)

                def seg(part, i):
                    tiles = part.tiles
                    u0 = first + part.units
                    n = i * part.useg + u0
                    f0 = part.segs * SEG
                    if part.side:
                        s5_batch(i)
                    for v in range(2 * tiles):
                        s = (u0 + v) % 4
                        sp.wait_ge(w_split, n + (v + 1))
                        sp.dma_start(raw(s, KD, P), gu_src[v % 2][:, :, bass.ds(i * (SEG * P) + (f0 + v // 2) * P, P)])\
                            .then_inc(w_here[s], 16)
                        if with_ada:
                            for k in range(KD * v // (2 * tiles), KD * (v + 1) // (2 * tiles)):
                                ada_tile(i + (ADA_START + part.segs), k, part.segs == 0 and k < ADA_RING)
                    for v in range(4):
                        s = (u0 + 2 * tiles + v) % 4
                        sp.wait_ge(w_split, n + (2 * tiles + v + 1))
                        sp.dma_start(raw(s, tiles, 256), wd_src[:, bass.ds(i * SEG + f0, tiles), 256 * v:256 * v + 256])\
                            .then_inc(w_here[s], 16)

                for part in parts:
                    if part.reps == 1:
                        seg(part, 0)
                    else:
                        with sp.Fori(0, part.reps) as i:
                            seg(part, i)

            ffn(UNIT["ffn1"], "ffn1", PARTS1, True)

            w_in = a["w_in"][0].rearrange("(k p) c -> p k c", p=P)

            def wide(n, c0):
                for q in range(4):
                    unit(n + q, w_in[:, 2 * q:2 * q + 2, c0:c0 + 512], raw((n + q) % 4, 2, 512))

            def tall(n, count, c0, c=P):
                for q in range(count):
                    unit(n + q, w_in[:, :, c0 + q * P:c0 + q * P + c], raw((n + q) % 4, KD, c))

            wide(UNIT["u"], C_U)
            tall(UNIT["glr"], 1, C_G, 2 * RANK)
            sp.wait_ge(xn_ok, 2 * KD)
            sp.dma_start(x_scr, x[:, :, 0:NL]).then_inc(x_spilled, 16)
            for k in range(KD):
                ada_tile(ADA_LAST, k)
                if k in (1, 3):
                    tall(UNIT["k"] + k // 2, 1, C_K + P * (k // 2))
                if k in (5, 7):
                    tall(UNIT["q"] + k // 2 - 2, 1, C_Q + P * (k // 2 - 2))
            sp.wait_ge(b_out, 16 + 16 * 4 * BATCHES)
            is_done(sp, JOB["ada8"])
            for b in range(8):
                if b >= 3:
                    sp.wait_ge(st_used, b - 2)
                sp.dma_start(stream[:, b % 3, :].rearrange("p (g c) -> p g c", g=8),
                             b_scr[8 * b:8 * b + 8].rearrange("g p c -> p g c")).then_inc(st_here[b % 3], 16)
            tall(UNIT["v"], 4, C_V)
            tall(UNIT["r"], 4, C_R)
            tall(UNIT["ga"], 8, C_GA)
            tall(UNIT["gb"], 8, C_GB)
            is_done(sp, JOB["vt"] + 5)
            for q in range(2):
                sp.wait_ge(c_out[q], 16 + 32 * BATCHES)
            sp.wait_ge(k_out, 16 + 32 * BATCHES)
            for b in range(8):
                if b >= 2:
                    sp.wait_ge(st_used, 8 + b - 1)
                g0 = 4 * b
                for s in range(CH):
                    sp.dma_start(stream2[GC * s:GC * s + GC, b % 2, 0, :, :].rearrange("p g (t c) -> p g t c", c=GC),
                                 k_scr[:, g0:g0 + 4, 7 - s:15 - s, :]).then_inc(st_here[b % 2], 16)
                sp.dma_start(stream2[:, b % 2, 1, :, :].rearrange("p g (t c) -> p g t c", c=GC),
                             c_scr[:, g0:g0 + 4, 1:9, :]).then_inc(st_here[b % 2], 16)
                sp.dma_start(stream2[:, b % 2, 2, :, :].rearrange("p g (t c) -> p g t c", c=GC),
                             c_scr[:, G + g0:G + g0 + 4, 0:8, :]).then_inc(st_here[b % 2], 16)
            glu_w = a["s5_glu_w"][0].rearrange("(k p) c -> p k c", p=P)
            for q in range(2):
                unit(UNIT["glu"] + q, glu_w[:, :, 256 * q:256 * q + 256], raw((UNIT["glu"] + q) % 4, 4, 256))
            outs = [a[w][0].rearrange("(k p) c -> p k c", p=P) for w in ("s5_out", "gla_out")]
            for q in range(8):
                n = UNIT["merge"] + q
                c0 = 256 * (q // 2)
                unit(n, outs[q % 2][:, :, c0:c0 + 256], raw(n % 4, 4, 256))
            w_o = a["w_o"][0].rearrange("(k p) c -> p k c", p=P)
            for q in range(8):
                n = UNIT["wo"] + q
                if q == 1:
                    is_done(sp, JOB["merge"] + 15)
                    sp.dma_start(x[:, :, 0:NL], x_scr).then_inc(x_back, 16)
                unit(n, w_o[:, :, P * q:P * q + P], raw(n % 4, KD, P))
            ffn(UNIT["ffn2"], "ffn2", PARTS2, False)
            for t in range(4):
                sp.wait_ge(outc_ok, t + 1)
                sp.dma_start(out[0, P * t:P * t + P, :], out_sb[:, t % 2, :]).then_inc(out_done[t % 2], 16)
            for s in range(2):
                sp.wait_ge(out_done[s], 32)

        @block.gpsimd
        def _(pool):
            pool.sem_inc(w_split, 4)
            pool.memset(ident[:, :], 0.0).then_inc(pool_own, 1)
            pool.memset(ones[:, :], 1.0).then_inc(consts, 1)
            pool.memset(eps[:, :], EPS).then_inc(consts, 1)
            pool.memset(halfpi[:, :], math.pi / 2).then_inc(consts, 1)
            pool.wait_ge(pool_own, 1)
            pool.affine_select(out=ident[:, :], in_=ident[:, :], compare_op=ALU.not_equal, fill=1.0, base=0,
                               pattern=[[-1, P]], channel_multiplier=1).then_inc(consts, 1)

            def parts(s, cols, made):
                pool.tensor_scalar(w_hi[:, s, 0:cols], w_raw[:, s, 0:cols], 1.0, 1.0, ALU.mult, ALU.mult)\
                    .then_inc(hi_made, 1)
                pool.wait_ge(hi_made, made)
                pool.tensor_tensor(w_lo[:, s, 0:cols], w_raw[:, s, 0:cols], w_hi[:, s, 0:cols].bitcast(F32),
                                   ALU.subtract).then_inc(w_split, 1)

            def split(n, cols):
                pool.wait_ge(w_here[n % 4], 16 * (n // 4 + 1))
                is_done(pool, last_user(n - 4))
                parts(n % 4, cols, n + 1)

            def ffn(units, jobs, parts_, fresh):
                def seg(part, i):
                    js = Seg(jobs + part.jobs, part.tiles, part.side)
                    for v in range(part.useg):
                        n = units + part.units + v
                        pool.wait_ge(w_here[n % 4], i * (4 * part.useg) + 16 * (n // 4 + 1))
                        if not (fresh and n < 4):
                            user = js.gu(v - 4) if v >= 4 else js.jobs - KD + 2 * v + 1
                            pool.wait_ge(job_done, i * part.jseg + (user + 1))
                        pool.sem_inc(slot_taken, 1)
                        parts(n % 4, part.tiles * 256 if v >= 2 * part.tiles else 1024, i * part.useg + (n + 1))

                for part in parts_:
                    if part.reps == 1:
                        seg(part, 0)
                    else:
                        with pool.Fori(0, part.reps) as i:
                            seg(part, i)

            ffn(UNIT["ffn1"], JOB["ffn1"], PARTS1, True)
            n = UNIT["u"]
            while n < UNIT["ffn2"]:
                split(n, 8 * 2 * RANK if n == UNIT["glr"] else 1024)
                if n == UNIT["u"] + 3:
                    pool.wait_ge(h_ok, 2 * KD)
                    pool.memset(zmask[:, :], 1.0).then_inc(pool_own, 1)
                    pool.memset(tri[:, :, :], 1.0).then_inc(pool_own, 1)
                    pool.memset(gate_up[:, :, :], 0.0).then_inc(gla_c, 1)
                    pool.wait_ge(pool_own, 3)
                    pool.memset(zmask[:, 0:NT:LC], 0.0).then_inc(masks_ok, 1)
                    pool.affine_select(out=tri[:, 0, :], in_=tri[:, 0, :], compare_op=ALU.is_ge, fill=0.0, base=0,
                                       pattern=[[1, P]], channel_multiplier=-1).then_inc(masks_ok, 1)
                    pool.affine_select(out=tri[:, 1, :], in_=tri[:, 1, :], compare_op=ALU.is_ge, fill=0.0, base=0,
                                       pattern=[[-1, P]], channel_multiplier=1).then_inc(masks_ok, 1)
                n += 1
            is_done(pool, JOB["wo"] + 5)
            ffn(UNIT["ffn2"], JOB["ffn2"], PARTS2, False)

        @block.tensor
        def _(pe):

            def split_mm(terms):
                last = None
                first = True
                for n, term in enumerate(terms):
                    if len(term) == 2:
                        pe.wait_ge(*term)
                        continue
                    sh, sl, moving = term
                    for q, (st, part) in enumerate(((sl, 0), (sh, 1), (sh, 0))):
                        for mv in moving:
                            last = pe.matmul(mv[2], st, mv[part], start=(first and q == 0),
                                             stop=(n == len(terms) - 1 and q == 2))
                    first = False
                return last

            def wv(s, k, c):
                return [w[:, s, 0:k * c].rearrange("p (k c) -> p k c", k=k) for w in (w_hi, w_lo)]

            def transpose(o, i):
                return pe.transpose(o, i, ident[0:i.shape[0], 0:i.shape[0]])

            pe.wait_ge(consts, 8)
            pe.wait_ge(x_landed, 16 * 6)
            for k in range(KD):
                j = JOB["x"] + k
                wait_read(pe, j)
                for t in range(6):
                    o = lat(j)[:, P * t:P * t + P] if t < 4 else ctx_(j)[:, P * (t - 4):P * (t - 3)]
                    last = transpose(o, x_in[:, t, P * k:P * k + P])
                last.then_inc(job_done, 1)
                if k == 0:
                    pe.wait_ge(vec_in, 16 * 9)
            j = JOB["vec"]
            wait_read(pe, j)
            transpose(lat(j)[:, 0:P], vecs[:, :]).then_inc(job_done, 1)
            j = JOB["lam"]
            pe.wait_ge(small_in, 16 * SMALL)
            wait_read(pe, j)
            transpose(lat(j)[:, 0:DG], lam_in[:, 0, :])
            transpose(lat(j)[:, P:P + 4], gn_in[:, :])
            transpose(lat(j)[:, DG:2 * DG], lam_in[:, 1, :]).then_inc(job_done, 1)

            def s5_side(i, v, j):
                h = v // 2
                pe.wait_ge(bp_ok, i * 8 + (v + 1))
                if v % 2 == 0:
                    if v == 0:
                        pe.wait_ge(s5_in, i * (16 * 14) + 16 * 14)
                        for d in range(NDIR):
                            for q in range(2):
                                c = (2 * d + q) * P
                                transpose(ctx_(j)[:, c:c + P],
                                          c_in[:, d, q:q + 2, :].rearrange("p r s -> p (r s)"))
                    for g in range(4):
                        last = transpose(lat(j)[:, P * g:P * g + P], bp[:, g, :, :].rearrange("p s c -> p (s c)"))
                else:
                    lag0 = h % 2
                    for g in range(4):
                        last = pe.matmul(lat(j)[0:GC, P * g:P * g + P], bb[:, h % 2, 4 * (h // 2) + g, :],
                                         cp[:, h % 2, g, lag0:lag0 + 8, :].rearrange("p s c -> p (s c)"),
                                         start=True, stop=True)
                last.then_inc(job_done, 1)

            def ada_sums(cols):
                for t in range(KD):
                    for v in range(2):
                        last = pe.matmul(cols[:, t, v:v + 1], ada_acc[:, v, P * t:P * t + P], ones[:, 0:1],
                                         start=True, stop=True)
                return last

            def ada_job(g, j):
                pe.wait_ge(acc_ok, 16 * (g + 1))
                wait_read(pe, j)
                ada_sums(ada_cols(j)).then_inc(job_done, 1)

            def norm_sum(j, n):
                nb = 1 if n == NL else 2
                pe.wait_ge(ssq_ok, norm_count[0] * KD + KD)
                norm_count[0] += 1
                wait_read(pe, j)
                for q in range(nb):
                    c = slice(512 * q, min(512 * q + 512, n))
                    last = pe.matmul((lat, ctx_)[q](j)[:, 0:c.stop - c.start], ones[:, :], ssq[:, c],
                                     start=True, stop=True)
                last.then_inc(job_done, 1)

            norm_count = [0]

            def ffn(units, jobs, parts, n, norms, act_base):
                two = n == NT

                def seg(part, i):
                    tiles = part.tiles
                    u0 = units + part.units
                    un = i * part.useg + u0
                    js = Seg(jobs + part.jobs, tiles, part.side)

                    def slot_free(j):
                        pe.wait_ge(slot_read[j % 4], j // 4 + i * (part.jseg // 4))

                    for v in range(2 * tiles):
                        s, j = (u0 + v) % 4, js.gu(v)
                        pe.wait_ge(w_split, un + (v + 5))
                        slot_free(j)
                        if two and v == 2 * tiles - 1:
                            pe.wait_ge(acc_ok, i * 16 + 16 * (ADA_START + part.segs + 1))
                            ada_sums(ada_cols(j, ADA_COL))
                        wh, wl = wv(s, KD, P)
                        terms = []
                        for k in range(KD):
                            if v == 0 and part.segs == 0:
                                terms.append((h_ok, KD * norms + k + 1))
                            if two:
                                mv = [(h_hi[:, k, 384 * q:384 * q + 384], h_lo[:, k, 384 * q:384 * q + 384],
                                       (lat, ctx_)[q](j)[:, 0:384]) for q in range(2)]
                            else:
                                mv = [(h_hi[:, k, 0:NL], h_lo[:, k, 0:NL], lat(j))]
                            terms.append((wh[:, k, :], wl[:, k, :], mv))
                        split_mm(terms).then_inc(job_done, 1)
                        if part.side:
                            slot_free(js.side(v))
                            s5_side(i, v, js.side(v))
                    for v in range(4):
                        s = (u0 + 2 * tiles + v) % 4
                        pe.wait_ge(w_split, un + (2 * tiles + v + 5))
                        wh, wl = wv(s, tiles, 256)
                        for q in range(2):
                            j = js.down(2 * v + q)
                            slot_free(j)
                            terms = []
                            for k in range(tiles):
                                if v == 0 and q == 0:
                                    terms.append((act_lo_ok, i * SEG + (act_base + part.segs * SEG + k + 1)))
                                mv = [(act_hi[:, k, 0:NL], act_lo[:, k, 0:NL], lat(j))]
                                if two:
                                    mv.append((act_hi[:, k, NL:NT], act_lo[:, k, NL:NT], ctx_(j)[:, 0:NC]))
                                terms.append((wh[:, k, P * q:P * q + P], wl[:, k, P * q:P * q + P], mv))
                            split_mm(terms).then_inc(job_done, 1)

                for part in parts:
                    if part.reps == 1:
                        seg(part, 0)
                    else:
                        with pe.Fori(0, part.reps) as i:
                            seg(part, i)

            norm_sum(JOB["norm0"], NT)
            for g in range(ADA_START):
                ada_job(g, JOB["ada"] + g)
            ffn(UNIT["ffn1"], JOB["ffn1"], PARTS1, NT, 0, 0)
            norm_sum(JOB["norm1"], NT)

            def hview(t, k, cols):
                return t[:, k, :][:, cols]

            def wide_jobs(n, j0, count, cols, rows):
                for t in range(count):
                    j = j0 + t
                    if t == 0:
                        pe.wait_ge(w_split, n + 8)
                    wait_read(pe, j)
                    terms = []
                    for k in range(KD):
                        s = (n + k // 2) % 4
                        if t == 0:
                            terms.append((h_ok, KD + k + 1))
                        mv = [(w_hi[:, s, 512 * (k % 2):512 * (k % 2) + 512], w_lo[:, s, 512 * (k % 2):512 * (k % 2) + 512],
                               lat(j)[0:rows, :])]
                        terms.append((cols(h_hi, k, t), cols(h_lo, k, t), mv))
                    split_mm(terms).then_inc(job_done, 1)

            def tall_jobs(n, j0, count, toks, c=P):
                for t in range(count):
                    j = j0 + t
                    pe.wait_ge(w_split, n + t + 5)
                    wait_read(pe, j)
                    wh, wl = wv((n + t) % 4, KD, c)
                    terms = []
                    for k in range(KD):
                        mv = [(h_hi[:, k, 0:NL], h_lo[:, k, 0:NL], lat(j)[0:c, :])]
                        if toks == NT:
                            mv.append((h_hi[:, k, NL:NT], h_lo[:, k, NL:NT], ctx_(j)[0:c, 0:NC]))
                        terms.append((wh[:, k, :], wl[:, k, :], mv))
                    split_mm(terms).then_inc(job_done, 1)

            wide_jobs(UNIT["u"], JOB["u"], CH, lambda h, k, t: h[:, k, t:NT:CH], NCH)
            tall_jobs(UNIT["glr"], JOB["glr"], 1, NT, 2 * RANK)
            tall_jobs(UNIT["k"], JOB["k"], 2, NT)
            tall_jobs(UNIT["q"], JOB["q"], 2, NL)
            ada_job(ADA_LAST, JOB["ada8"])
            for b in range(8):
                j = JOB["ut"] + b
                if b == 0:
                    for s in range(CH - 4, CH):
                        was_read(pe, JOB["u"] + s)
                wait_read(pe, j)
                for g in range(4):
                    last = transpose(lat(j)[:, NCH * g:NCH * g + NCH],
                                     u_tok[:, 4 * b + g, :, :].rearrange("p s c -> p (s c)"))
                last.then_inc(job_done, 1)
            for b in range(16):
                j = JOB["xs"] + b
                if b == 0:
                    for q in range(4, 8):
                        was_read(pe, JOB["ut"] + q)
                if b % 2 == 0:
                    pe.wait_ge(st_here[b // 2 % 3], 16 * (b // 6 + 1))
                wait_read(pe, j)
                for q in range(4):
                    g = (4 * b + q) % G
                    e = (4 * b + q) % 8
                    last = pe.matmul(lat(j)[:, NCH * q:NCH * q + NCH], stream[:, b // 2 % 3, P * e:P * e + P],
                                     ut[:, g, :], start=True, stop=True)
                last.then_inc(job_done, 1)
                if b % 2:
                    is_done(pe, j)
                    pe.sem_inc(st_used, 1)

            tall_jobs(UNIT["v"], JOB["v"], 4, NT)
            for t in range(6):
                j = JOB["vt"] + t
                if t == 0:
                    for q in range(4):
                        was_read(pe, JOB["v"] + q)
                wait_read(pe, j)
                for q in range(4):
                    last = transpose(lat(j)[:, P * q:P * q + P], v_t[:, q, P * t:P * t + P])
                last.then_inc(job_done, 1)
            tall_jobs(UNIT["r"], JOB["r"], 4, NL)
            tall_jobs(UNIT["ga"], JOB["ga"], 8, NL)
            tall_jobs(UNIT["gb"], JOB["gb"], 8, NL)
            def gate_logits(p):
                ti, d = p // 2, p % 2
                j = GJ["z", p]
                wait_read(pe, j)
                for q in range(2):
                    last = pe.matmul((lat, ctx_)[q](j)[:, 0:384], gate_up[:, d, P * ti:P * ti + P],
                                     glr[:, 384 * q:384 * q + 384], start=True, stop=True)
                last.then_inc(job_done, 1)

            pe.wait_ge(small_in, 16 * (SMALL + 2))
            gate_logits(0)
            pe.wait_ge(states_ok, 1)
            for b in range(8):
                j = JOB["y"] + b
                pe.wait_ge(st_here[b % 2], 16 * (3, 3)[b % 2] + 160 * (b // 2 + 1))
                wait_read(pe, j)
                for q in range(4):
                    g = 4 * b + q
                    o = lat(j)[0:LCH, P * q:P * q + P]
                    c0 = NC // CH
                    pe.matmul(o, ut[:, g, 0:LCH], stream2[:, b % 2, 0, q, :], start=True, stop=False)
                    pe.matmul(o, xs[:, c0 - 1:c0 - 1 + LCH, g], stream2[:, b % 2, 1, q, :], start=False, stop=False)
                    last = pe.matmul(o, hb[:, :, g], stream2[:, b % 2, 2, q, :],
                                     start=False, stop=True)
                last.then_inc(job_done, 1)
                is_done(pe, j)
                pe.sem_inc(st_used, 1)
            for c in range(4):
                j = JOB["yt"] + c
                if c == 0:
                    for q in range(4, 8):
                        was_read(pe, JOB["y"] + q)
                wait_read(pe, j)
                for t in range(CH):
                    last = transpose(lat(j)[:, LCH * t:LCH * t + LCH], y_tok[:, t, P * c:P * c + P])
                last.then_inc(job_done, 1)
            pe.wait_ge(yl_ok, 4)
            for q in range(2):
                n = UNIT["glu"] + q
                pe.wait_ge(w_split, n + 5)
                wh, wl = wv(n % 4, 4, 256)
                for h in range(2):
                    j = JOB["glu"] + 2 * q + h
                    wait_read(pe, j)
                    split_mm([(wh[:, k, P * h:P * h + P], wl[:, k, P * h:P * h + P],
                               [(y_hi[:, k, :], y_lo[:, k, :], lat(j))]) for k in range(4)]).then_inc(job_done, 1)
            for p in range(4):
                ti, d = p // 2, p % 2
                if p < 3:
                    gate_logits(p + 1)
                j = GJ["ket", p]
                pe.wait_ge(e_d, p + 1)
                wait_read(pe, j)
                for t in range(6):
                    o = lat(j)[:, P * t:P * t + P] if t < 4 else ctx_(j)[:, P * (t - 4):P * (t - 3)]
                    last = transpose(o, ke[:, P * t:P * t + P])
                last.then_inc(job_done, 1)
                for hp in range(2):
                    j = GJ["sc", p] + hp
                    wait_read(pe, j)
                    for t in range(4):
                        last = pe.matmul(lat(j)[:, P * t:P * t + P], kz[:, hp, P * t:P * t + P],
                                         e1q[:, P * t:P * t + P], start=True, stop=True)
                    last.then_inc(job_done, 1)
                was_read(pe, GJ["ket", p])
                order = (4, 5, 0, 1, 2, 3) if d == 0 else (5, 4, 3, 2, 1, 0)
                for half in range(2):
                    j = GJ["kv", p] + half
                    wait_read(pe, j)
                    for q in range(3):
                        t = order[3 * half + q]
                        for par in range(2):
                            for hp in range(2):
                                hd = 2 * ti + hp
                                last = pe.matmul((lat, ctx_)[par](j)[64 * hp:64 * hp + 64, P * q:P * q + P],
                                                 ket[64 * par:64 * par + 64, t, 64 * hp:64 * hp + 64],
                                                 v_sb[64 * par:64 * par + 64, t, DV * hd:DV * hd + DV],
                                                 start=True, stop=True)
                    last.then_inc(job_done, 1)
                if d == 0:
                    continue
                pe.wait_ge(s_ok, p + 1)
                for t in range(4):
                    j = GJ["out", p] + t
                    wait_read(pe, j)
                    for hp in range(2):
                        hd = 2 * ti + hp
                        c = slice(DV * hp, DV * hp + DV)
                        for dd in range(2):
                            pe.matmul(lat(j)[:, c], at_sb[:, dd, hp, t, :], v_sb[:, t, DV * hd:DV * hd + DV],
                                      start=(dd == 0), stop=False, skip_group_check=True)
                        for par in range(2):
                            for dd in range(2):
                                last = pe.matmul(lat(j)[64 * par:64 * par + 64, c],
                                                 qz[:, dd, hp, P * t + 64 * par:P * t + 64 * par + 64],
                                                 s_st[:, dd, 2 * t + par, :], start=False,
                                                 stop=(par == 1 and dd == 1), skip_group_check=True)
                    last.then_inc(job_done, 1)
            pe.wait_ge(ybtok_ok, 1)
            for c in range(4):
                j = JOB["ybt"] + c
                wait_read(pe, j)
                for t in range(4):
                    last = transpose(lat(j)[:, P * t:P * t + P], o_sb[:, t, P * c:P * c + P])
                last.then_inc(job_done, 1)
            pe.wait_ge(yb_ok, 4)
            pe.wait_ge(yal_ok, 4)
            for q in range(8):
                n = UNIT["merge"] + q
                pe.wait_ge(w_split, n + 5)
                wh, wl = wv(n % 4, 4, 256)
                yh, yl = ((ya_hi, ya_lo), (yb_hi, yb_lo))[q % 2]
                for h in range(2):
                    j = JOB["merge"] + 2 * q + h
                    wait_read(pe, j)
                    split_mm([(wh[:, k, P * h:P * h + P], wl[:, k, P * h:P * h + P],
                               [(yh[:, k, :], yl[:, k, :], lat(j))]) for k in range(4)]).then_inc(job_done, 1)
            pe.wait_ge(m_ok, KD)
            for q in range(KD):
                n, j = UNIT["wo"] + q, JOB["wo"] + q
                pe.wait_ge(w_split, n + 5)
                wait_read(pe, j)
                wh, wl = wv(n % 4, KD, P)
                split_mm([(wh[:, k, :], wl[:, k, :], [(m_hi[:, k, :], m_lo[:, k, :], lat(j))])
                          for k in range(KD)]).then_inc(job_done, 1)
            norm_sum(JOB["norm2"], NL)
            ffn(UNIT["ffn2"], JOB["ffn2"], PARTS2, NL, 2, FF // P)
            norm_sum(JOB["norm3"], NL)
            pe.wait_ge(fin_ok, KD)
            for t in range(4):
                j = JOB["out"] + t
                wait_read(pe, j)
                for k in range(KD):
                    last = transpose((lat if k < 4 else ctx_)(j)[:, P * (k % 4):P * (k % 4) + P],
                                     x[:, k, P * t:P * t + P])
                last.then_inc(job_done, 1)

        @block.scalar
        def _(act):
            own = [0]

            def link(ins):
                own[0] += 1
                ins.then_inc(act_own, 1)
                act.wait_ge(act_own, own[0])

            rows = [("ada_b", 72), ("ffn1_norm", 8), ("mix_norm", 8), ("ffn2_norm", 8), ("final_norm", 8), ("c", 8),
                    ("c_ctx", 8), ("s5_glu_b", 4), ("gla_gate_b", 4)]
            r0 = 0
            for name, n in rows:
                src = a[name]
                while len(src.shape) > 1:
                    src = src.rearrange("a b -> (a b)") if len(src.shape) == 2 else src.rearrange("a b c -> (a b c)")
                act.dma_start(vecs[r0:r0 + n, :], src.rearrange("(r p) -> r p", p=P)).then_inc(vec_in, 16)
                r0 += n
            for q, name in enumerate(("s5_lambda_re", "s5_lambda_im")):
                for h in range(2):
                    act.dma_start(lam_in[:, q, SP5 * h:SP5 * h + SP5], a[name][0].rearrange("d g p -> (d g) p"))\
                        .then_inc(small_in, 16)
            act.dma_start(s5t[:, 0, :], a["s5_log_dt"][0].rearrange("d g -> (d g)").partition_broadcast(P))\
                .then_inc(small_in, 16)
            act.dma_start(gn_in[:, :], a["gla_norm"][0].rearrange("(r p) -> r p", p=P)).then_inc(small_in, 16)
            act.dma_start(dg5[:, :], a["s5_d"][0].rearrange("(g c) -> c g", c=GC),
                          allow_slow_non_contiguous=True).then_inc(small_in, 16)

            for k in range(KD):
                j = JOB["x"] + k
                is_done(act, j)
                act.activation(x[:, k, 0:NL], lat(j), ACT.Copy)
                act.activation(x[:, k, NL:NT], ctx_(j)[:, 0:NC], ACT.Copy).then_inc(slot_read[j % 4], 1)
            j = JOB["vec"]
            is_done(act, j)
            act.activation(vt[:, :], lat(j)[:, 0:P], ACT.Copy).then_inc(slot_read[j % 4], 1)
            was_read(act, j)
            for v, row in enumerate((104, 112)):
                ins = act.activation(cs[:, :, v], vt[:, row:row + 8], ACT.Silu)
            ins.then_inc(silu_c, 1)

            def s5_trig():
                act.wait_ge(s5_dve, 1)
                act.activation(s5t[:, 8, :], s5t[:, 4, :], ACT.Exp).then_inc(s5_act, 1)
                act.activation(s5t[:, 9, :], s5t[:, 6, :], ACT.Sin).then_inc(s5_act, 1)
                link(act.activation(s5t[:, 10, :], s5t[:, 6, :], ACT.Abs))
                act.activation(s5t[:, 11, :], s5t[:, 10, :], ACT.Sin, bias=halfpi[:, :], scale=-1.0).then_inc(s5_act, 1)

            def s5_side(i, f, j):
                act.wait_ge(b_out, i * 64 + 16 * (f + 1))
                if f == 0:
                    cv = ctx_(j).rearrange("p (d q c) -> p d q c", d=NDIR, q=2)
                    for o, q, sg in ((cm, 0, nsgn), (cms, 1, sgn)):
                        act.activation(o[:, :, :, :].rearrange("p d g c -> p d (g c)"), cv[:, :, q, :], ACT.Copy,
                                       scale=sg[:, 0:1])
                act.activation(bt_sb[:, :, :].rearrange("p g c -> p (g c)"), lat(j), ACT.Copy)\
                    .then_inc(slot_read[j % 4], 1)

            def s5_out(i, f, j_value):
                g0 = bass.ds(i * 8 + (G * (f % 2) + 4 * (f // 2)), 4)
                act.wait_ge(*j_value)
                act.dma_start(b_scr[g0].rearrange("g p c -> p g c"), bt_sb[:, :, :]).then_inc(b_out, 16)
                act.wait_ge(bp_ok, i * 8 + (2 * f + 2))
                act.dma_start(c_scr[:, g0, :, :], cp[:, f % 2, :, :, :]).then_inc(c_out[f % 2], 16)

            def norm(q, j, n):
                for k in range(KD):
                    if q == 0:
                        was_read(act, JOB["x"] + k)
                    else:
                        was_read(act, (JOB["norm1"] - KD, JOB["wo"], JOB["norm3"] - KD)[q - 1] + k)
                    if k >= 2 or q:
                        act.wait_ge(ssq_ok, KD * q + k - 1)
                    act.activation(silu[:, k % 2, 0:n], x[:, k, 0:n], ACT.Square).then_inc(sq_ok, 1)
                is_done(act, j)
                if q == 1:
                    act.wait_ge(k_out, 16 + 32 * BATCHES)
                ins = act.activation(rstd[:, 0:NL], lat(j), ACT.Sqrt, bias=eps[:, :], scale=1.0 / D)
                if n == NT:
                    ins = act.activation(rstd[:, NL:NT], ctx_(j)[:, 0:NC], ACT.Sqrt, bias=eps[:, :], scale=1.0 / D)
                ins.then_inc(slot_read[j % 4], 1)
                if q == 3:
                    return
                act.wait_ge(cols_ok, q + 1)
                for k in range(KD):
                    act.wait_ge(xn_ok, KD * q + k + 1)
                    parts = [(slice(0, NL), 0)] + ([(slice(NL, NT), 1)] if n == NT else [])
                    for c, v in parts:
                        ins = act.activation(h_hi[:, k, c], gu[:, k % 2, c], ACT.Identity,
                                             bias=mod[:, 24 * q + k, v:v + 1])
                    ins.then_inc(h_hi_ok, 1)

            def ffn(jobs, parts, n):
                def seg(part, i):
                    js = Seg(jobs + part.jobs, part.tiles, part.side)
                    for f in range(part.tiles):
                        jg, ju = js.gu(2 * f), js.gu(2 * f + 1)
                        dst, src = silu[:, f % 2, 0:n], lat(jg)
                        if n == NT:
                            dst, src = dst.rearrange("p (b c) -> p b c", b=2), both(jg, 384)
                        act.wait_ge(job_done, (jg + 1) + i * part.jseg)
                        act.activation(dst, src, ACT.Silu).then_inc(slot_read[jg % 4], 1)
                        if part.side:
                            j = js.side(2 * f)
                            act.wait_ge(job_done, (j + 1) + i * part.jseg)
                            s5_side(i, f, j)
                            s5_out(i, f, (slot_read[j % 4], (j // 4 + 1) + i * (part.jseg // 4)))
                        act.wait_ge(slot_read[ju % 4], (ju // 4 + 1) + i * (part.jseg // 4))
                        act.activation(act_hi[:, f, 0:n], gu[:, f % 2, 0:n], ACT.Copy).then_inc(act_hi_ok, 1)
                        if n == NT and part.segs == 0 and f == 1:
                            s5_trig()
                        if part.side and f % 2:
                            act.wait_ge(k_ok, i * 2 + (f // 2 + 1))
                            act.dma_start(k_scr[:, bass.ds(i * 8 + 4 * (f // 2), 4), :, :], kf[:, :, :, :])\
                                .then_inc(k_out, 16)

                for part in parts:
                    if part.reps == 1:
                        seg(part, 0)
                    else:
                        with act.Fori(0, part.reps) as i:
                            seg(part, i)

            act.wait_ge(small_in, 16 * SMALL)
            act.activation(s5t[:, 1, :], s5t[:, 0, :], ACT.Exp).then_inc(s5_act, 1)
            norm(0, JOB["norm0"], NT)
            ffn(JOB["ffn1"], PARTS1, NT)
            norm(1, JOB["norm1"], NT)

            act.wait_ge(h_ok, 2 * KD)
            for s in range(CH):
                j = JOB["u"] + s
                is_done(act, j)
                act.activation(u_tok[:, :, s, :], lat(j)[0:NCH, :].rearrange("p (g c) -> p g c", c=GC), ACT.Copy)\
                    .then_inc(slot_read[j % 4], 1)
            act.wait_ge(gla_c, 1)
            for d in range(2):
                act.dma_start(gate_up[RANK * d:RANK * d + RANK, d, :], a["gla_gate_up"][0, d]).then_inc(small_in, 16)

            def w_major(t):
                return t.rearrange("p (w r) -> p r w", r=ROWS)

            def row_major(t):
                return t.rearrange("p (r w) -> p r w", w=GRID_W)

            def evac_tokens(j, dst, n, rows, scale=1.0):
                is_done(act, j)
                ins = act.activation(w_major(dst[:, 0:NL]), row_major(lat(j)[0:rows, :]), ACT.Copy, scale=scale)
                if n == NT:
                    ins = act.activation(dst[:, NL:NT], ctx_(j)[0:rows, 0:NC], ACT.Copy)
                ins.then_inc(slot_read[j % 4], 1)

            evac_tokens(JOB["glr"], glr[:, :], NT, 2 * RANK)
            for q in range(2):
                evac_tokens(JOB["k"] + q, kt[:, q, :], NT, P)
            for q in range(2):
                evac_tokens(JOB["q"] + q, qt[:, q, :], NL, P, DK ** -0.5)
            for b in range(8):
                j = JOB["ut"] + b
                is_done(act, j)
                act.activation(ut[:, 4 * b:4 * b + 4, :], lat(j)[:, 0:4 * NCH].rearrange("p (g c) -> p g c", g=4),
                               ACT.Copy).then_inc(slot_read[j % 4], 1)
            act.wait_ge(x_spilled, 16)
            nctx = NC // CH
            for b in range(16):
                j = JOB["xs"] + b
                is_done(act, j)
                src = lat(j)[:, 0:4 * NCH].rearrange("p (g c) -> p c g", g=4)
                dgs = slice(4 * b, 4 * b + 4)
                lats, ctxs = src[:, 0:LCH, :], src[:, LCH:NCH, :]
                if b >= 8:
                    lats, ctxs = lats[:, ::-1, :], ctxs[:, ::-1, :]
                act.activation(xs[:, nctx:NCH, dgs], lats, ACT.Copy)
                act.activation(xs[:, 0:nctx, dgs], ctxs, ACT.Copy).then_inc(slot_read[j % 4], 1)
            for q in range(4):
                evac_tokens(JOB["v"] + q, v_t[:, q, :], NT, P)
            for t in range(6):
                j = JOB["vt"] + t
                is_done(act, j)
                act.activation(v_sb[:, t, :], lat(j), ACT.Copy).then_inc(slot_read[j % 4], 1)
            for t in range(4):
                j = JOB["r"] + t
                is_done(act, j)
                act.activation(r_sb[:, t, :], lat(j), ACT.Silu).then_inc(slot_read[j % 4], 1)
            for t in range(16):
                j = JOB["ga"] + t
                is_done(act, j)
                if t >= 2:
                    act.wait_ge(gate_out[t % 2], 16 * (t // 2))
                act.activation(gate_buf[:, t % 2, :], lat(j), ACT.Sigmoid).then_inc(slot_read[j % 4], 1)
                was_read(act, j)
                act.dma_start(g_scr[:, t, :], gate_buf[:, t % 2, :]).then_inc(gate_out[t % 2], 16)
            def softplus(p):
                g = g_a[p % 2]
                if p >= 2:
                    act.wait_ge(e_d, p - 1)
                is_done(act, GJ["z", p])
                link(act.activation(g[:, :].rearrange("p (b c) -> p b c", b=2), both(GJ["z", p], 384), ACT.Abs,
                                    bias=vt[:, 124 + 2 * (p % 2) + p // 2:125 + 2 * (p % 2) + p // 2]))
                link(act.activation(g[:, :], g[:, :], ACT.Exp, scale=-1.0))
                act.activation(g[:, :], g[:, :], ACT.Ln, bias=ones[:, 0:1]).then_inc(z_a, 1)

            def decays(p):
                act.wait_ge(z_d, p + 1)
                gv = g_c[:, :].rearrange("p (c t) -> p c t", t=LC)
                act.activation(g_a[p % 2][:, 0:NL], g_b[:, 0:NL], ACT.Exp, scale=1.0 / 16)
                link(act.activation(decay[:, p % 2, :], gv[:, :, (LC - 1 if p % 2 == 0 else 0)], ACT.Exp, scale=1.0 / 16))
                act.activation(g_b[:, 0:NL], g_b[:, 0:NL], ACT.Exp, scale=-1.0 / 16)
                act.activation(g_d[:, :], g_d[:, :], ACT.Exp, scale=1.0 / 16)
                act.activation(g_c[:, 0:NL], g_c[:, 0:NL], ACT.Exp, scale=1.0 / 16).then_inc(e_a, 1)

            softplus(0)
            for b in range(8):
                j = JOB["y"] + b
                if b == 2:
                    decays(0)
                is_done(act, j)
                act.activation(y_tok[:, :, 64 * b:64 * b + 64].rearrange("p t (g c) -> p t g c", c=GC),
                               lat(j)[0:LCH, :].rearrange("p (g t c) -> p t g c", g=4, c=GC), ACT.Gelu_apprx_tanh)\
                    .then_inc(slot_read[j % 4], 1)


            def token_order(t):
                return t.rearrange("p (k t) -> p t k", t=CH)

            for c in range(4):
                j = JOB["yt"] + c
                is_done(act, j)
                src = lat(j).rearrange("p (t k) -> p t k", t=CH)
                act.activation(token_order(y32[:, c, :]), src, ACT.Copy)
                act.activation(token_order(y_hi[:, c, :]), src, ACT.Copy).then_inc(yh_ok, 1)
            for c in range(4):
                j = JOB["glu"] + c
                is_done(act, j)
                if c < 2:
                    act.wait_ge(gate_out[c], 128)
                act.activation(gate_buf[:, c % 2, :], lat(j), ACT.Sigmoid, bias=vt[:, 120 + c:121 + c])\
                    .then_inc(slot_read[j % 4], 1)
                act.wait_ge(ya_ok, c + 1)
                if c == 3:
                    for e in range(4):
                        act.activation(ya_hi[:, e, :], y32[:, e, :], ACT.Copy).then_inc(glu_sig, 1)
            for p in range(4):
                if p < 3:
                    softplus(p + 1)
                j = GJ["ket", p]
                is_done(act, j)
                act.activation(ket[:, 0:4, :].rearrange("p t c -> p (t c)"), lat(j), ACT.Copy)
                act.activation(ket[:, 4:6, :].rearrange("p t c -> p (t c)"), ctx_(j)[:, 0:2 * P], ACT.Copy)\
                    .then_inc(slot_read[j % 4], 1)
                if p < 3:
                    decays(p + 1)
                if p % 2 == 0:
                    continue
                for t in range(4):
                    j = GJ["out", p] + t
                    is_done(act, j)
                    act.activation(o_sb[:, t, DV * (p - 1):DV * (p - 1) + 2 * DV], lat(j)[:, 0:2 * DV], ACT.Copy)\
                        .then_inc(slot_read[j % 4], 1)
                    was_read(act, j)
                    act.sem_inc(o_ok, 1)
            def load_gates(t):
                for br in range(2):
                    act.dma_start(gates[:, t % 2, br, :], g_scr[:, KD * br + t, :]).then_inc(gate_in[t % 2], 16)

            for t in range(2):
                load_gates(t)
            act.wait_ge(o_rs, 1)
            act.activation(oms[:, :], oms[:, :], ACT.Sqrt, bias=eps[:, :], scale=1.0 / DV).then_inc(o_rs, 1)
            for c in range(4):
                j = JOB["ybt"] + c
                was_read(act, j)
                act.activation(yb_hi[:, c, :], r_sb[:, c, :], ACT.Copy).then_inc(ybh_ok, 1)
            for t in range(KD):
                act.wait_ge(m32_ok, t + 1)
                act.activation(m_hi[:, t, :], mt[:, t % 2, 2, :], ACT.Copy).then_inc(mh_ok, 1)
                if t + 2 < KD:
                    load_gates(t + 2)
            norm(2, JOB["norm2"], NL)
            ffn(JOB["ffn2"], PARTS2, NL)
            norm(3, JOB["norm3"], NL)
            for t in range(4):
                j = JOB["out"] + t
                is_done(act, j)
                if t >= 2:
                    act.wait_ge(out_done[t % 2], 16)
                act.activation(out_sb[:, t % 2, :].rearrange("p (b c) -> p b c", b=2), both(j, 512), ACT.Copy)\
                    .then_inc(slot_read[j % 4], 1)
                was_read(act, j)
                act.sem_inc(outc_ok, 1)

        @block.vector
        def _(dve):
            own = [0]

            def link(ins):
                own[0] += 1
                ins.then_inc(dve_own, 1)
                dve.wait_ge(dve_own, own[0])

            TT, TS, STT = dve.tensor_tensor, dve.tensor_scalar, dve.scalar_tensor_tensor
            dve.memset(sgn[0:64, :], -1.0).then_inc(consts, 1)
            dve.memset(sgn[64:128, :], 1.0).then_inc(consts, 1)
            dve.memset(nsgn[0:64, :], 1.0).then_inc(consts, 1)
            dve.memset(nsgn[64:128, :], -1.0).then_inc(consts, 1)
            dve.sem_inc(s5_in_used, 1)
            dve.sem_inc(b_out, 16)
            dve.sem_inc(k_out, 16)
            for q in range(2):
                dve.sem_inc(c_out[q], 16)

            f = [s5t[:, q, :] for q in range(16)]
            dt, lr, li, th = f[1], f[2], f[3], f[6]

            def s5_lambda():
                j = JOB["lam"]
                is_done(dve, j)
                dve.tensor_copy(li, lat(j)[:, DG:2 * DG])
                dve.tensor_copy(gn[:, :], lat(j)[:, P:P + 4])
                TS(lr, lat(j)[:, 0:DG], -1e-4, None, ALU.min).then_inc(slot_read[j % 4], 1)

            def s5_angle():
                was_read(dve, JOB["lam"])
                dve.wait_ge(s5_act, 1)
                TT(f[4], lr, dt, ALU.mult)
                link(TT(f[5], li, dt, ALU.mult))
                link(TS(f[7], f[5], 1.0 / TWO_PI, ROUND, ALU.mult, ALU.add))
                link(TS(f[7], f[7], -ROUND, None, ALU.add))
                link(STT(f[6], f[7], -PI_1, f[5], ALU.mult, ALU.add))
                link(STT(f[6], f[7], -PI_2, f[6], ALU.mult, ALU.add))
                link(STT(f[6], f[7], -PI_3, f[6], ALU.mult, ALU.add))
                TS(th, f[6], PI_MAX, -PI_MAX, ALU.min, ALU.max).then_inc(s5_dve, 1)
                link(TT(f[12], lr, lr, ALU.mult))
                link(TT(f[13], li, li, ALU.mult))
                link(TT(f[12], f[12], f[13], ALU.add))
                link(dve.reciprocal(f[12], f[12]))

            def s5_powers():
                dve.wait_ge(s5_act, 4)
                dve.memset(pr[:, 0, :], 1.0)
                dve.memset(pis[:, 0, :], 0.0)
                TT(pr[:, 1, :], f[8], f[11], ALU.mult)
                link(TT(f[9], f[8], f[9], ALU.mult))
                link(TS(f[13], pr[:, 1, :], -1.0, None, ALU.add))
                link(TT(f[14], f[13], lr, ALU.mult))
                link(TT(f[15], f[9], li, ALU.mult))
                link(TT(f[14], f[14], f[15], ALU.add))
                TT(coef[:, 0, :], f[14], f[12], ALU.mult)
                link(TT(f[15], f[13], li, ALU.mult))
                link(TT(f[13], f[9], lr, ALU.mult))
                link(TT(f[15], f[13], f[15], ALU.subtract))
                link(TT(f[15], f[15], f[12], ALU.mult))
                TS(coef[:, 1, :], f[15], sgn[:, 0:1], None, ALU.mult)
                link(dve.tensor_copy(pis[:, 1, :], f[9]))
                for q in range(2, 9):
                    TT(f[0], pr[:, q - 1, :], pr[:, 1, :], ALU.mult)
                    TT(f[10], pis[:, q - 1, :], f[9], ALU.mult)
                    TT(f[13], pr[:, q - 1, :], f[9], ALU.mult)
                    link(TT(f[14], pis[:, q - 1, :], pr[:, 1, :], ALU.mult))
                    TT(pr[:, q, :], f[0], f[10], ALU.subtract)
                    link(TT(pis[:, q, :], f[13], f[14], ALU.add))
                link(TS(pis[:, :, :], pis[:, :, :], sgn[:, 0:1], None, ALU.mult))
                dve.tensor_copy(lam8[:, 0, :], pr[:, 8, :])
                link(TS(lam8[:, 1, :], pis[:, 8, :], -1.0, None, ALU.mult))

            s5_n = [0]

            def s5_link(i, ins):
                s5_n[0] += 1
                ins.then_inc(s5_own, 1)
                dve.wait_ge(s5_own, i * S5_LINKS + s5_n[0])

            def s5_input(i):
                dve.wait_ge(s5_in, i * (16 * 14) + 16 * 14)

                def c(q):
                    return coef[:, q, :].rearrange("p (d g) -> p d g", d=NDIR)[:, :, bass.ds(i * 8, 8)]\
                        .unsqueeze(3).to_broadcast([P, NDIR, 8, GC])

                s_bb, s_bbs, s_bm, s_bms, tmp = (t[:, :, :, :] for t in (bb, bbs, bm, bms, bb_t))
                TT(s_bb, s_bm, c(0), ALU.mult)
                TT(s_bbs, s_bms, c(0), ALU.mult)
                s5_link(i, TT(tmp, s_bms, c(1), ALU.mult))
                s5_link(i, TT(s_bb, s_bb, tmp, ALU.add))
                s5_link(i, TT(tmp, s_bm, c(1), ALU.mult))
                s5_link(i, TT(s_bbs, s_bbs, tmp, ALU.subtract))

            def half_power(q, n, rev):
                w = pw[:, q, 0:n, :]
                if rev:
                    w = w[:, ::-1, :]
                return w.rearrange("p s g -> p g s").unsqueeze(3).to_broadcast([P, 4, n, GC])

            def half_matrix(t, h, n):
                return t[:, h % 2, 4 * (h // 2):4 * (h // 2) + 4, :].unsqueeze(2).to_broadcast([P, 4, n, GC])

            def s5_b(i, h):
                if h:
                    dve.wait_ge(bp_ok, i * 8 + 2 * h)
                tmp, fwd = ptmp[:, :, 0:CH, :], h % 2 == 0
                s5_link(i, dve.tensor_copy(pw[:, :, :, :],
                                           powers[:, :, :, bass.ds(i * 8 + (G * (h % 2) + 4 * (h // 2)), 4)]))
                TT(bp[:, :, :, :], half_power(0, CH, fwd), half_matrix(bb, h, CH), ALU.mult)
                s5_link(i, TT(tmp, half_power(1, CH, fwd), half_matrix(bbs, h, CH), ALU.mult))
                TT(bp[:, :, :, :], bp[:, :, :, :], tmp, ALU.add).then_inc(bp_ok, 1)

            def s5_c(i, h):
                dve.wait_ge(bp_ok, i * 8 + (2 * h + 1))
                dve.wait_ge(c_out[h % 2], i * 32 + (16 * (h // 2) + 16))
                o, rev = cp[:, h % 2, :, :, :], h % 2 == 1
                TT(o, half_power(0, 9, rev), half_matrix(cm, h, 9), ALU.mult)
                s5_link(i, TT(ptmp[:, :, :, :], half_power(1, 9, rev), half_matrix(cms, h, 9), ALU.mult))
                TT(o, o, ptmp[:, :, :, :], ALU.subtract).then_inc(bp_ok, 1)

            def s5_lags(i, h, j, read):
                src = lat(j)[0:GC, :].rearrange("p (g t c) -> p g t c", g=4, c=GC)
                if h % 2 == 0:
                    dve.wait_ge(k_out, i * 32 + (16 * (h // 2) + 16))
                    dve.tensor_copy(kf[:, :, 7:15, :], src).then_inc(slot_read[j % 4], 1)
                    read()
                    return
                dve.tensor_copy(kf[:, :, 0:7, :], src[:, :, 0:7, :])
                TT(kf[:, :, 7, :], src[:, :, 7, :], kf[:, :, 7, :], ALU.add).then_inc(slot_read[j % 4], 1)
                dve.wait_ge(bp_ok, i * 8 + min(2 * h + 3, 8))
                tmp = ptmp[0:GC, :, 0, :]
                s5_link(i, TT(tmp, dg5[:, bass.ds(i * 8 + 4 * (h // 2), 4)].unsqueeze(2).to_broadcast([GC, 4, GC]),
                              ident[0:GC, 0:GC].unsqueeze(1).to_broadcast([GC, 4, GC]), ALU.mult))
                TT(kf[:, :, 7, :], kf[:, :, 7, :], tmp, ALU.add).then_inc(k_ok, 1)

            def ada_add(g, k):
                s = k % ADA_RING
                tile = ada_w[:, s, :]
                if isinstance(g, int) and g < ADA_START:
                    t = KD * g + k
                    tile = ada_w0[:, t % ADA_RING0, :]
                    dve.wait_ge(ada_here0[t % ADA_RING0], 16 * (t // ADA_RING0 + 1))
                else:
                    dve.wait_ge(ada_here[s], (g - ADA_START) * (16 * KD // ADA_RING) + 16 * (k // ADA_RING + 1))
                for v in range(2):
                    if k == 0:
                        TS(ada_acc[:, v, :], tile, cs[:, k, v:v + 1], None, ALU.mult).then_inc(acc_ok, 1)
                    else:
                        dve.wait_ge(acc_ok, g * 16 + (2 * k + v - 1))
                        STT(ada_acc[:, v, :], tile, cs[:, k, v:v + 1], ada_acc[:, v, :],
                            ALU.mult, ALU.add).then_inc(acc_ok, 1)

            def ada_bias(cols, t):
                return TT(mod[:, t, :], cols, vt[:, t].unsqueeze(2).to_broadcast([P, KD, 2]), ALU.add)

            def scale_cols(q, g_row):
                STT(amul[:, q, :, :], mod[:, 24 * q + 8:24 * q + 16, :], 1.0,
                    vt[:, g_row:g_row + 8].unsqueeze(2).to_broadcast([P, 8, 2]), ALU.add, ALU.mult).then_inc(cols_ok, 1)

            def add_square(q, k, n):
                dve.wait_ge(sq_ok, KD * q + k + 1)
                if k == 0:
                    dve.tensor_copy(ssq[:, 0:n], silu[:, 0, 0:n]).then_inc(ssq_ok, 1)
                else:
                    dve.wait_ge(ssq_ok, KD * q + k)
                    TT(ssq[:, 0:n], ssq[:, 0:n], silu[:, k % 2, 0:n], ALU.add).then_inc(ssq_ok, 1)

            def norm_root(j, n):
                was_read(dve, j)
                link(dve.reciprocal(rstd[:, 0:n], rstd[:, 0:n]))

            def norm(q, n):
                if q == 3:
                    for k in range(KD):
                        STT(x[:, k, 0:n], x[:, k, 0:n], vt[:, 96 + k:97 + k], rstd[:, 0:n], ALU.mult, ALU.mult)\
                            .then_inc(fin_ok, 1)
                    return
                parts = [(slice(0, NL), 0)] + ([(slice(NL, NT), 1)] if n == NT else [])

                def xn(k):
                    if k >= 2:
                        dve.wait_ge(h_ok, KD * q + k - 1)
                    for c, v in parts:
                        ins = STT(gu[:, k % 2, c], x[:, k, c], amul[:, q, k, v:v + 1], rstd[:, c], ALU.mult, ALU.mult)
                    ins.then_inc(xn_ok, 1)

                dve.wait_ge(cols_ok, q + 1)
                xn(0)
                for k in range(KD):
                    if k + 1 < KD:
                        xn(k + 1)
                    dve.wait_ge(xn_ok, KD * q + k + 1)
                    dve.wait_ge(h_hi_ok, KD * q + k + 1)
                    for c, v in parts:
                        ins = STT(h_lo[:, k, c], gu[:, k % 2, c], mod[:, 24 * q + k, v:v + 1],
                                  h_hi[:, k, c].bitcast(F32), ALU.add, ALU.subtract)
                    ins.then_inc(h_ok, 1)

            def ffn(jobs, parts, n, q, act_base):
                def seg(part, i):
                    tiles = part.tiles
                    js = Seg(jobs + part.jobs, tiles, part.side)
                    a0 = act_base + part.segs * SEG
                    s5_n[0] = 0

                    def done(j):
                        dve.wait_ge(job_done, (j + 1) + i * part.jseg)

                    def read(j):
                        dve.wait_ge(slot_read[j % 4], (j // 4 + 1) + i * (part.jseg // 4))

                    ada = ((0, 3), (3, 6), (6, 8), (8, 8)) if tiles == SEG else ((0, 5), (5, 8))
                    for f_ in range(tiles):
                        jg, ju = js.gu(2 * f_), js.gu(2 * f_ + 1)
                        if part.side and f_ == 0:
                            s5_input(i)
                            s5_b(i, 0)
                        if q == 0:
                            for k in range(*ada[f_]):
                                ada_add(i + (ADA_START + part.segs), k)
                        if part.side:
                            if f_ == 0:
                                read(js.side(0))
                                dve.sem_inc(s5_in_used, 1)
                            s5_c(i, f_)
                        read(jg)
                        done(ju)
                        if n == NT:
                            dst, sl = (t[:, f_ % 2, :].rearrange("p (b c) -> p b c", b=2) for t in (gu, silu))
                            src = both(ju, 384)
                        else:
                            dst, src, sl = gu[:, f_ % 2, 0:n], lat(ju), silu[:, f_ % 2, 0:n]
                        if q == 0 and f_ == tiles - 1:
                            ada_bias(ada_cols(ju, ADA_COL), bass.ds(i * KD + KD * (ADA_START + part.segs), KD))
                        STT(dst, src, 0.5, sl, ALU.mult, ALU.mult).then_inc(slot_read[ju % 4], 1)
                        read(ju)
                        dve.wait_ge(act_hi_ok, i * SEG + (a0 + f_ + 1))
                        TT(act_lo[:, f_, 0:n], gu[:, f_ % 2, 0:n], act_hi[:, f_, 0:n].bitcast(F32), ALU.subtract)\
                            .then_inc(act_lo_ok, 1)
                        if q == 0 and part.segs == 0:
                            if f_ == 0:
                                s5_angle()
                            if f_ == 2:
                                s5_powers()
                        if part.side:
                            j = js.side(2 * f_ + 1)
                            if f_ + 1 < SEG:
                                s5_b(i, f_ + 1)
                            done(j)
                            s5_lags(i, f_, j, lambda: read(j))
                    for k in range(KD):
                        j = js.down(k)
                        done(j)
                        g = 24 * q + 16 + k
                        ins = STT(x[:, k, 0:NL], lat(j), mod[:, g, 0:1], x[:, k, 0:NL], ALU.mult, ALU.add)
                        if n == NT:
                            ins = STT(x[:, k, NL:NT], ctx_(j)[:, 0:NC], mod[:, g, 1:2], x[:, k, NL:NT],
                                      ALU.mult, ALU.add)
                        ins.then_inc(slot_read[j % 4], 1)
                        if tiles == TAIL and k:
                            add_square(q + 1, k - 1, n)
                    if tiles == TAIL:
                        add_square(q + 1, KD - 1, n)
                    read(js.down(KD - 1))
                    assert not part.side or s5_n[0] == S5_LINKS

                for part in parts:
                    if part.reps == 1:
                        seg(part, 0)
                    else:
                        with dve.Fori(0, part.reps) as i:
                            seg(part, i)

            for k in range(KD):
                add_square(0, k, NT)
            s5_lambda()
            dve.wait_ge(silu_c, 1)
            for g in range(ADA_START):
                j = JOB["ada"] + g
                for k in range(KD):
                    ada_add(g, k)
                if g == 0:
                    norm_root(JOB["norm0"], NT)
                is_done(dve, j)
                ada_bias(ada_cols(j), slice(KD * g, KD * g + KD)).then_inc(slot_read[j % 4], 1)
            was_read(dve, j)
            scale_cols(0, 72)
            norm(0, NT)
            ffn(JOB["ffn1"], PARTS1, NT, 0, 0)
            scale_cols(1, 80)
            scale_cols(2, 88)
            norm_root(JOB["norm1"], NT)
            norm(1, NT)
            for k in range(KD):
                ada_add(ADA_LAST, k)
            is_done(dve, JOB["ada8"])
            ada_bias(ada_cols(JOB["ada8"]), slice(KD * ADA_LAST, KD * ADA_LAST + KD)).then_inc(slot_read[JOB["ada8"] % 4], 1)

            for q in range(4):
                was_read(dve, JOB["xs"] + 12 + q)

            def step(jj, count, first=False):
                prev, cur = xs[:, jj - 1, :], xs[:, jj, :]
                if isinstance(jj, int) is False:
                    prev = xs[:, bass.ds(jj - 1, 1), :].rearrange("p a g -> p (a g)")
                    cur = xs[:, bass.ds(jj, 1), :].rearrange("p a g -> p (a g)")
                if not first:
                    dve.wait_ge(scan_step, count)
                TT(st1[:, :], prev, lam8[:, 0, :], ALU.mult).then_inc(scan_step, 1)
                TT(st2[0:64, :], prev[64:128, :], lam8[64:128, 1, :], ALU.mult).then_inc(scan_step, 1)
                TT(st2[64:128, :], prev[0:64, :], lam8[0:64, 1, :], ALU.mult).then_inc(scan_step, 1)
                dve.wait_ge(scan_step, count + 1)
                TT(cur, cur, st1[:, :], ALU.add).then_inc(scan_step, 1)
                dve.wait_ge(scan_step, count + 4)
                TT(cur, cur, st2[:, :], ALU.add).then_inc(scan_step, 1)

            step(1, 0, first=True)
            with dve.Fori(0, 31) as i:
                for q in range(3):
                    jj = i * 3 + (2 + q)
                    count = i * 15 + (5 + 5 * q)
                    prev = xs[:, bass.ds(i * 3 + (1 + q), 1), :].rearrange("p a g -> p (a g)")
                    cur = xs[:, bass.ds(i * 3 + (2 + q), 1), :].rearrange("p a g -> p (a g)")
                    dve.wait_ge(scan_step, count)
                    TT(st1[:, :], prev, lam8[:, 0, :], ALU.mult).then_inc(scan_step, 1)
                    TT(st2[0:64, :], prev[64:128, :], lam8[64:128, 1, :], ALU.mult).then_inc(scan_step, 1)
                    TT(st2[64:128, :], prev[0:64, :], lam8[0:64, 1, :], ALU.mult).then_inc(scan_step, 1)
                    dve.wait_ge(scan_step, i * 15 + (5 + 5 * q + 1))
                    TT(cur, cur, st1[:, :], ALU.add).then_inc(scan_step, 1)
                    dve.wait_ge(scan_step, i * 15 + (5 + 5 * q + 4))
                    TT(cur, cur, st2[:, :], ALU.add).then_inc(scan_step, 1)
            dve.wait_ge(scan_step, 5 * 94)
            is_done(dve, JOB["gb"] + 7)
            dve.tensor_copy(hb[:, :, :], xs[:, NC // CH - 1:NC // CH - 1 + LCH, G:DG][:, ::-1, :]).then_inc(states_ok, 1)
            dve.wait_ge(masks_ok, 3)
            for t in (tri[0:64, 0, 64:128], tri[64:128, 1, 0:64], kz[:, :, :], qz[:, :, :, :], at_sb[:, :, :, :, :]):
                link(dve.memset(t, 0.0))

            def cumulate(p):
                ti, d = p // 2, p % 2
                j = GJ["z", p]
                gb_col = vt[:, 124 + 2 * d + ti:125 + 2 * d + ti]
                is_done(dve, j)
                dve.wait_ge(z_a, p + 1)
                link(TS(g_b[:, :].rearrange("p (b c) -> p b c", b=2), both(j, 384), gb_col, 0.0, ALU.add, ALU.min))
                dve.sem_inc(slot_read[j % 4], 1)
                link(TT(g_b[:, :], g_b[:, :], g_a[p % 2][:, :], ALU.subtract))
                step = 1 if d == 0 else -1
                link(dve.tensor_tensor_scan(g_c[:, ::step], zmask[:, :], g_b[:, ::step], 0.0, ALU.mult, ALU.add))
                gv = g_c[:, :].rearrange("p (c t) -> p c t", t=LC)
                ref, last = (LC // 2, LC - 1) if d == 0 else (LC // 2 - 1, 0)
                TT(g_b[:, 0:NL].rearrange("p (c t) -> p c t", t=LC), gv[:, 0:8, :],
                   gv[:, 0:8, ref:ref + 1].to_broadcast([P, 8, LC]), ALU.subtract)
                TT(g_d[:, :].rearrange("p (c t) -> p c t", t=LC), gv[:, :, last:last + 1].to_broadcast([P, 12, LC]),
                   gv, ALU.subtract).then_inc(z_d, 1)

            def decayed(p):
                ti, d = p // 2, p % 2
                dve.wait_ge(e_a, p + 1)
                TT(e1q[:, :], qt[:, ti, :], g_a[p % 2][:, 0:NL], ALU.mult)
                for hp in range(2):
                    r = slice(64 * hp, 64 * hp + 64)
                    TT(kz[r, hp, :], kt[r, ti, 0:NL], g_b[r, 0:NL], ALU.mult)
                TT(ke[:, :], kt[:, ti, :], g_d[:, :], ALU.mult).then_inc(e_d, 1)
                if p == 2:
                    is_done(dve, GJ["out", 1] + 3)
                for hp in range(2):
                    r = slice(64 * hp, 64 * hp + 64)
                    ins = TT(qz[r, d, hp, :], qt[r, ti, :], g_c[r, 0:NL], ALU.mult)
                link(ins)

            cumulate(0)
            decayed(0)
            for c in range(4):
                j = JOB["yt"] + c
                dve.wait_ge(yh_ok, c + 1)
                TT(y_lo[:, c, :], y32[:, c, :], y_hi[:, c, :].bitcast(F32), ALU.subtract).then_inc(yl_ok, 1)
                dve.sem_inc(slot_read[j % 4], 1)
            for c in range(4):
                was_read(dve, JOB["glu"] + c)
                TT(y32[:, c, :], y32[:, c, :], gate_buf[:, c % 2, :], ALU.mult).then_inc(ya_ok, 1)
            for c in range(4):
                dve.wait_ge(glu_sig, c + 1)
                dve.wait_ge(ya_ok, 4)
                TT(ya_lo[:, c, :], y32[:, c, :], ya_hi[:, c, :].bitcast(F32), ALU.subtract).then_inc(yal_ok, 1)

            for p in range(4):
                d = p % 2
                if p:
                    decayed(p)
                if p < 3:
                    cumulate(p + 1)
                for hp in range(2):
                    j = GJ["sc", p] + hp
                    is_done(dve, j)
                    dve.copy_predicated(at_sb[:, d, hp, :, :],
                                        tri[:, d, :].unsqueeze(1).to_broadcast([P, 4, P]).bitcast(I32),
                                        lat(j).rearrange("p (t c) -> p t c", t=4)).then_inc(slot_read[j % 4], 1)
                order = (4, 5, 0, 1, 2, 3) if d == 0 else (5, 4, 3, 2, 1, 0)
                nth = 0
                prev = None
                for half in range(2):
                    j = GJ["kv", p] + half
                    is_done(dve, j)
                    for q in range(3):
                        t = order[3 * half + q]
                        for par in ((0, 1) if d == 0 else (1, 0)):
                            c = 2 * t + par
                            kv = (lat, ctx_)[par](j)[:, P * q:P * q + P]
                            if nth < 3:
                                nxt = s_cur[:, d, nth % 2, :]
                            elif nth < 11:
                                nc_ = nth - 3
                                nxt = s_st[:, d, nc_ if d == 0 else 7 - nc_, :]
                            else:
                                nxt = None
                            if nth == 0:
                                link(dve.tensor_copy(nxt, kv))
                            elif nxt is not None:
                                link(STT(nxt, prev, decay[:, p % 2, c:c + 1], kv, ALU.mult, ALU.add))
                            prev = nxt
                            nth += 1
                    dve.sem_inc(slot_read[j % 4], 1)
                dve.sem_inc(s_ok, 1)
            dve.wait_ge(o_ok, 8)
            ov = o_sb[:, :, :].rearrange("p t (h e) -> p (t h) e", h=HEADS)
            link(TT(osq[:, :, :], o_sb[:, :, :], o_sb[:, :, :], ALU.mult))
            dve.tensor_reduce(oms[:, :], osq[:, :, :].rearrange("p t (h e) -> p (t h) e", h=HEADS), AX.X, ALU.add)\
                .then_inc(o_rs, 1)
            dve.wait_ge(o_rs, 2)
            link(dve.reciprocal(oms[:, :], oms[:, :]))
            TT(ov, ov, oms[:, :].unsqueeze(2).to_broadcast([P, 16, DV]), ALU.mult).then_inc(ybtok_ok, 1)
            for c in range(4):
                j = JOB["ybt"] + c
                is_done(dve, j)
                STT(r_sb[:, c, :].rearrange("p (r w) -> p r w", w=GRID_W), lat(j).rearrange("p (w r) -> p r w", r=ROWS),
                    gn[:, c:c + 1], r_sb[:, c, :].rearrange("p (r w) -> p r w", w=GRID_W), ALU.mult, ALU.mult)\
                    .then_inc(slot_read[j % 4], 1)
            for c in range(4):
                dve.wait_ge(ybh_ok, c + 1)
                TT(yb_lo[:, c, :], r_sb[:, c, :], yb_hi[:, c, :].bitcast(F32), ALU.subtract).then_inc(yb_ok, 1)
            for t in range(KD):
                ja = JOB["merge"] + 4 * (t // 2) + t % 2
                jb = ja + 2
                dve.wait_ge(gate_in[t % 2], 32 * (t // 2 + 1))
                if t >= 2:
                    dve.wait_ge(mh_ok, t - 1)
                is_done(dve, ja)
                TT(mt[:, t % 2, 0, :], lat(ja), gates[:, t % 2, 0, :], ALU.mult).then_inc(slot_read[ja % 4], 1)
                is_done(dve, jb)
                TT(mt[:, t % 2, 1, :], lat(jb), gates[:, t % 2, 1, :], ALU.mult).then_inc(slot_read[jb % 4], 1)
                was_read(dve, ja)
                was_read(dve, jb)
                TT(mt[:, t % 2, 2, :], mt[:, t % 2, 0, :], mt[:, t % 2, 1, :], ALU.add).then_inc(m32_ok, 1)
                dve.wait_ge(m32_ok, t + 1)
                dve.wait_ge(mh_ok, t + 1)
                TT(m_lo[:, t, :], mt[:, t % 2, 2, :], m_hi[:, t, :].bitcast(F32), ALU.subtract).then_inc(m_ok, 1)
            dve.wait_ge(x_back, 16)
            for k in range(KD):
                j = JOB["wo"] + k
                is_done(dve, j)
                STT(x[:, k, 0:NL], lat(j), mod[:, 40 + k, 0:1], x[:, k, 0:NL], ALU.mult, ALU.add)\
                    .then_inc(slot_read[j % 4], 1)
                if k:
                    add_square(2, k - 1, NL)
            add_square(2, KD - 1, NL)
            norm_root(JOB["norm2"], NL)
            norm(2, NL)
            ffn(JOB["ffn2"], PARTS2, NL, 2, FF // P)
            norm_root(JOB["norm3"], NL)
            norm(3, NL)


_INS = ['x', 'c', 'ctx', 'c_ctx', 'ada_w', 'ada_b', 'ffn1_norm', 'ffn1_w_gate', 'ffn1_w_up', 'ffn1_w_down', 'mix_norm',
        'w_in', 's5_lambda_re', 's5_lambda_im', 's5_log_dt', 's5_b_re', 's5_b_im', 's5_c_re', 's5_c_im', 's5_d',
        's5_glu_w', 's5_glu_b', 's5_out', 'gla_gate_up', 'gla_gate_b', 'gla_norm', 'gla_out', 'w_o', 'ffn2_norm',
        'ffn2_w_gate', 'ffn2_w_up', 'ffn2_w_down', 'final_norm']


def kernel(**inputs):
    import numpy as _np
    import concourse.bacc as _bacc
    from concourse import mybir as _mybir
    from concourse.bass_utils import run_bass_kernel_spmd as _run

    nc = _bacc.Bacc("TRN2", target_bir_lowering=False, num_devices=1)
    arrays, args = {}, {}
    for name in _INS:
        v = _np.ascontiguousarray(inputs[name])
        arrays[f"in_{name}_dram"] = v
        args[name] = nc.dram_tensor(f"in_{name}_dram", v.shape, _mybir.dt.from_np(v.dtype), kind="ExternalInput").ap()
    out = nc.dram_tensor("out_0_dram", (1, NL, D), _mybir.dt.float32, kind="ExternalOutput").ap()
    build(nc, args, out)
    r = _run(nc, [arrays], core_ids=[0])
    return r.results[0]["out_0_dram"]
```

```python
from contextlib import ExitStack
import math

import numpy as np
import concourse.bass as bass
from concourse import mybir

F32 = mybir.dt.float32
F32R = mybir.dt.float32r
I32 = mybir.dt.int32
ALU = mybir.AluOpType
ACT = mybir.ActivationFunctionType
AX = mybir.AxisListType

P = 128
D = 1024
KD = D // P
FF = 2816
NL, NC = 512, 256
NT = NL + NC
EPS = 1e-6
G, GC, SP5 = 32, 16, 64
W5 = G * GC
NDIR = 2
DG = NDIR * G
CH = 8
NCH = NT // CH
LCH = NL // CH
HEADS, DK, DV = 4, 64, 128
KEY, VAL = HEADS * DK, HEADS * DV
RANK = 16
LC = 64
GRID_W = 64
ROWS = NL // GRID_W
C_U, C_Q, C_K, C_V, C_R, C_G = 0, 512, 768, 1024, 1536, 2048
C_GA, C_GB = 2080, 3104

SEG = 4
NSEG = FF // P // SEG
TAIL = FF // P - NSEG * SEG
SLOTS = 4
USEG = 2 * SEG + 4
FFN_UNITS = NSEG * USEG + 2 * TAIL + 4


class Seg:
    def __init__(self, jobs, tiles, side):
        self.jobs, self.step = jobs, 2 if side else 1
        self.down0 = 2 * tiles * self.step
        self.count = self.down0 + KD

    def gu(self, v):
        return self.jobs + v * self.step

    def side(self, v):
        return self.jobs + v * self.step + 1

    def down(self, k):
        return self.jobs + self.down0 + k


class Part:
    def __init__(self, reps, tiles, side, segs, units, jobs):
        self.reps, self.tiles, self.side, self.segs, self.units, self.jobs = reps, tiles, side, segs, units, jobs
        self.useg = 2 * tiles + 4
        self.jseg = Seg(0, tiles, side).count


def _parts(spec):
    parts, segs, units, jobs = [], 0, 0, 0
    for reps, tiles, side in spec:
        p = Part(reps, tiles, side, segs, units, jobs)
        parts.append(p)
        segs, units, jobs = segs + reps, units + reps * p.useg, jobs + reps * p.jseg
    return parts, jobs


BATCHES = G // 8
assert BATCHES == NSEG - 1
PARTS1, FFN1_JOBS = _parts([(1, SEG, False), (NSEG - 1, SEG, True), (1, TAIL, False)])
PARTS2, FFN2_JOBS = _parts([(NSEG, SEG, False), (1, TAIL, False)])

ADA_START = 2
ADA_RING0, ADA_RING = 6, 2
ADA_LAST = ADA_START + NSEG + 1

UNIT, JOB = {}, {}


def _number(table, parts):
    n = 0
    for name, count in parts:
        table[name] = n
        n += count
    table["end"] = n


_number(UNIT, [("ffn1", FFN_UNITS), ("u", 4), ("glr", 1), ("k", 2), ("q", 2), ("r", 4), ("v", 4), ("ga", 8),
               ("gb", 8), ("glu", 2), ("ma", 4), ("mb", 4), ("wo", 8), ("ffn2", FFN_UNITS)])
_number(JOB, [("vec", 1), ("x", KD), ("ada0", 1), ("lam", 1), ("norm0", 2), ("ada1", 1), ("ffn1", FFN1_JOBS), ("norm1", 2),
              ("u", CH), ("glr", 1), ("k", 2), ("q", 2), ("ada8", 1), ("chunks", 28), ("v", 4), ("vt", 6),
              ("ga", 8), ("gb", 8), ("z0", 1), ("y", 8), ("yt", 4), ("z1", 1), ("glu", 4), ("gla", 38), ("ybt", 4), ("mb", KD),
              ("wo", KD), ("norm2", 2), ("ffn2", FFN2_JOBS), ("norm3", 2), ("out", 4)])
NADA = 9 * KD

GJ = {("z", 0): JOB["z0"], ("z", 1): JOB["z1"]}
MA_JOB = []
MA_AFTER = {("kv", 0): 2, ("kv", 1): 2, ("kv", 2): 1, ("kv", 3): 2, ("out", 3): 1}


def _gla_jobs():
    n = JOB["gla"]
    for p in range(4):
        for name, count in (("z", int(p in (1, 2))), ("ket", 1), ("sc", 2), ("kv", 2), ("out", 4 * (p % 2))):
            if count:
                GJ[(name, p + 1 if name == "z" else p)] = n
            n += count
            for _ in range(MA_AFTER.get((name, p), 0)):
                MA_JOB.append(n)
                n += 1
    assert n == JOB["ybt"] and len(MA_JOB) == KD


_gla_jobs()


CHUNK_ORDER = [("ut", 4), ("r", 1), ("ut", 4), ("r", 1), ("xs", 6), ("r", 1), ("xs", 6), ("r", 1), ("xs", 4)]
CHUNK_JOBS = []
for _name, _count in CHUNK_ORDER:
    for _ in range(_count):
        CHUNK_JOBS.append((_name, sum(n == _name for n, _, _ in CHUNK_JOBS), JOB["chunks"] + len(CHUNK_JOBS)))
CJ = {(n, b): j for n, b, j in CHUNK_JOBS}


def last_user(n):
    if UNIT["r"] <= n < UNIT["r"] + 4:
        return CJ["r", n - UNIT["r"]]
    for name in ("glr", "k", "q", "v", "ga", "gb", "wo"):
        if UNIT[name] <= n < UNIT[name] + {"glr": 1, "k": 2, "q": 2, "v": 4}.get(name, 8):
            return JOB[name] + n - UNIT[name]
    if UNIT["ma"] <= n < UNIT["ma"] + 4:
        return MA_JOB[2 * (n - UNIT["ma"]) + 1]
    for name in ("glu", "mb"):
        if UNIT[name] <= n < UNIT[name] + {"glu": 2, "mb": 4}[name]:
            return JOB[name] + 2 * (n - UNIT[name]) + 1
    if UNIT["u"] <= n < UNIT["u"] + 4:
        return JOB["u"] + CH - 1
    v = n - (UNIT["u"] - 4)
    if 0 <= v < 4:
        return JOB["norm1"] - KD + 2 * v + 1
    raise ValueError(n)

TWO_PI = 2 * math.pi
PI_1 = 6.28125
PI_2 = float(np.float32(np.round((TWO_PI - PI_1) * 2**20) / 2**20))
PI_3 = float(np.float32(TWO_PI - PI_1 - PI_2))
ROUND = 12582912.0
PI_MAX = 3.1415925


def build(nc, a, out):
    b_scr = nc.dram_tensor("b_scr", [DG, P, P], F32).ap()
    c_scr = nc.dram_tensor("c_scr", [P, DG, 9, GC], F32).ap()
    k_scr = nc.dram_tensor("k_scr", [GC, G, 15, GC], F32).ap()
    x_scr = nc.dram_tensor("x_scr", [P, KD, NL], F32).ap()
    g_scr = nc.dram_tensor("g_scr", [P, 2 * KD, NL], F32).ap()

    base = (nc.sbuf_base + 63) // 64 * 64
    top = [base]

    def place(name, shape, dt, at=None):
        size = int(np.prod(shape[1:])) * 4
        off = top[0] if at is None else at
        t = nc.alloc_sbuf_tensor_at(name, shape, dt, offset=off)
        if at is None:
            top[0] += (size + 63) // 64 * 64
        assert off + size <= nc.sbuf_usable_end, (name, off + size)
        return t

    KB = 1024
    w_raw = place("w_raw", [P, SLOTS, 1024], F32)
    w_hi = place("w_hi", [P, SLOTS, 1024], F32R)
    w_lo = place("w_lo", [P, SLOTS, 1024], F32R)
    h_at = top[0]
    h_hi = place("h_hi", [P, KD, NT], F32R)
    h_lo = place("h_lo", [P, KD, NT], F32R)
    x_at = top[0]
    x = place("x", [P, KD, NT], F32)
    ident = place("ident", [P, P], F32)
    ones = place("ones", [P, P], F32)
    vt = place("vt", [P, P], F32)
    mod = place("mod", [P, NADA, 2], F32)
    amul = place("amul", [P, 3, KD, 2], F32)
    cs = place("cs", [P, KD, 2], F32)
    eps = place("eps", [P, 1], F32)
    halfpi = place("halfpi", [P, 1], F32)
    sgn = place("sgn", [P, 1], F32)
    nsgn = place("nsgn", [P, 1], F32)
    lam8 = place("lam8", [P, 2, DG], F32)
    gn_in = place("gn_in", [4, P], F32)
    gn = place("gn", [P, 4], F32)
    hb = place("hb", [P, LCH, G], F32, at=h_at + 40 * KB)
    dg5 = place("dg5", [GC, G], F32)
    root = place("root", [P, NT // P], F32)
    decay = place("decay", [P, 2, 12], F32)
    oms = place("oms", [P, 16], F32)
    scratch_at = top[0]
    vecs = place("vecs", [P, P], F32, at=scratch_at)
    act_hi = place("act_hi", [P, SEG, NT], F32R)
    act_lo = place("act_lo", [P, SEG, NT], F32R)
    silu = place("silu", [P, 2, NT], F32)
    gu = place("gu", [P, 2, NT], F32)
    ssq = place("ssq", [P, NT], F32)
    rstd_w = place("rstd_w", [P, NT // P, P], F32)
    s5_at = top[0] - 2 * NT * 4
    ada_at = (nc.sbuf_usable_end - 4 * (ADA_RING + 2) * D) // 64 * 64
    ada_w = place("ada_w", [P, ADA_RING, D], F32, at=ada_at)
    ada_acc = place("ada_acc", [P, 2, D], F32, at=ada_at + 4 * ADA_RING * D)

    m = [scratch_at]

    def mix(name, shape, dt=F32):
        size = int(np.prod(shape[1:])) * 4
        t = place(name, shape, dt, at=m[0])
        m[0] += (size + 63) // 64 * 64
        return t

    u_at = m[0]
    u_tok = mix("u_tok", [NCH, G, CH, GC])
    ut_at = m[0]
    ut = mix("ut", [P, G, NCH])
    qt = mix("qt", [P, 2, NL])
    kt = mix("kt", [P, 2, NT])
    v_sb = mix("v_sb", [P, 6, VAL])
    r_sb = mix("r_sb", [P, 4, NL])
    glr = mix("glr", [2 * RANK, NT])
    zmask = mix("zmask", [P, NT])
    tri = mix("tri", [P, 2, P])
    gate_up = mix("gate_up", [2 * RANK, 2, KEY])
    stream_at = m[0]
    stream = mix("stream", [P, 3, 1024])
    stream2 = [place(f"stream2_{b}", [P, 3, 4, P], F32, at=o)
               for b, o in enumerate((stream_at, stream_at + 6 * KB, h_at + 17 * KB))]
    xs_at = x_at
    xs = place("xs", [P, NCH, DG], F32, at=x_at)
    st1 = mix("st1", [P, DG])
    st2 = mix("st2", [P, DG])
    gate_buf = mix("gate_buf", [P, 2, NL])
    assert m[0] <= nc.sbuf_usable_end
    v_t = place("v_t", [P, 4, NT], F32, at=stream_at)
    y_tok = place("y_tok", [LCH, CH, W5], F32, at=u_at)
    y32 = place("y32", [P, 4, NL], F32, at=xs_at)
    y_hi = place("y_hi", [P, 4, NL], F32R, at=xs_at + 8 * KB)
    y_lo = place("y_lo", [P, 4, NL], F32R, at=xs_at + 16 * KB)
    ya_hi = place("ya_hi", [P, 4, NL], F32R, at=ut_at)
    e1q = place("e1q", [P, NL], F32, at=h_at)
    kz = place("kz", [P, 2, NL], F32, at=h_at + 2 * KB)
    qz = place("qz", [P, 2, 2, NL], F32, at=h_at + 6 * KB)
    ke = place("ke", [P, NT], F32, at=h_at + 14 * KB)
    ket = place("ket", [P, 6, P], F32, at=h_at + 17 * KB)
    at_sb = place("at_sb", [P, 2, 2, 4, P], F32, at=h_at + 20 * KB)
    g_a = [place("g_a0", [P, NT], F32, at=h_at + 28 * KB), place("g_a1", [P, NT], F32, at=u_at + 12 * KB)]
    g_b = place("g_b", [P, NT], F32, at=h_at + 31 * KB)
    g_c = place("g_c", [P, NT], F32, at=h_at + 34 * KB)
    g_d = place("g_d", [P, NT], F32, at=h_at + 37 * KB)
    s_st = place("s_st", [P, 2, 8, DV], F32, at=u_at)
    s_cur = place("s_cur", [P, 2, 2, DV], F32, at=u_at + 8 * KB)
    o_sb = place("o_sb", [P, 4, VAL], F32, at=h_at + 40 * KB)
    osq = place("osq", [P, 4, VAL], F32, at=h_at)
    yb_hi = place("yb_hi", [P, 4, NL], F32R, at=xs_at)
    yb_lo = place("yb_lo", [P, 4, NL], F32R, at=xs_at + 8 * KB)
    ya_lo = place("ya_lo", [P, 4, NL], F32R, at=xs_at + 16 * KB)
    m_hi = place("m_hi", [P, KD, NL], F32R, at=h_at)
    m_lo = place("m_lo", [P, KD, NL], F32R, at=h_at + 16 * KB)
    mt = place("mt", [P, 2, 3, NL], F32, at=h_at + 32 * KB)
    ma = place("ma", [P, KD, NL], F32, at=stream_at)
    gates = place("gates", [P, 2, 2, NL], F32, at=u_at)

    x_in = place("x_in", [P, 6, D], F32, at=h_at)
    ada_w0 = place("ada_w0", [P, ADA_RING0, D], F32, at=h_at + 24 * KB)

    s5p = [s5_at]

    def prep(name, shape):
        t = place(name, shape, F32, at=s5p[0])
        s5p[0] += (int(np.prod(shape[1:])) * 4 + 63) // 64 * 64
        assert s5p[0] <= ada_at, name
        return t

    bm = prep("bm", [P, NDIR, 8, GC])
    bms = prep("bms", [P, NDIR, 8, GC])
    c_in = prep("c_in", [P, NDIR, 3, SP5])
    bb_t = prep("bb_t", [P, NDIR, 8, GC])
    kf = prep("kf", [GC, 4, 15, GC])
    powers = prep("powers", [P, 2, 9, DG])
    pr, pis = powers[:, 0, :, :], powers[:, 1, :, :]
    pw = prep("pw", [P, 2, 9, 4])
    coef = prep("coef", [P, 2, DG])
    bb = prep("bb", [P, NDIR, 8, GC])
    bbs = prep("bbs", [P, NDIR, 8, GC])
    cm = prep("cm", [P, NDIR, 8, GC])
    cms = prep("cms", [P, NDIR, 8, GC])
    s5t_at = s5p[0]
    bp = prep("bp", [P, 4, CH, GC])
    cp = prep("cp", [P, 2, 4, 9, GC])
    ptmp = prep("ptmp", [P, 4, 9, GC])
    bt_sb = prep("bt_sb", [P, 4, P])
    s5t = place("s5t", [P, 16, DG], F32, at=s5t_at)
    lam_in = place("lam_in", [DG, 2, P], F32, at=s5t_at + 4 * KB)
    out_sb = place("out_sb", [P, 2, D], F32, at=h_at)

    ps = nc.alloc_psum_tensor("ps", [P, 8, 512], F32)

    def lat(j):
        return ps[:, 2 * (j % 4), :]

    def ctx_(j):
        return ps[:, 2 * (j % 4) + 1, :]

    def both(j, n):
        return ps[:, 2 * (j % 4):2 * (j % 4) + 2, 0:n]

    def ada_cols(j, c0=0):
        return lat(j)[:, c0:c0 + 2 * KD].rearrange("p (t v) -> p t v", v=2)

    ADA_COL = 384

    with ExitStack() as es:
        def sem(name):
            return es.enter_context(nc.semaphore(name))

        job_done = sem("job_done")
        slot_read = [sem(f"slot_read{s}") for s in range(4)]
        w_here = [sem(f"w_here{s}") for s in range(4)]
        w_split = sem("w_split")
        hi_made = sem("hi_made")
        ada_here0 = [sem(f"ada_first{s}") for s in range(ADA_RING0)]
        ada_here = [sem(f"ada_here{s}") for s in range(ADA_RING)]
        ada_used = sem("ada_used")
        acc_ok = sem("acc_ok")
        consts = sem("consts")
        small_in = sem("small_in")
        vec_in = sem("vec_in")
        s5_in = sem("s5_in")
        s5_own = sem("s5_own")
        s5_in_used = sem("s5_in_used")
        x_landed = sem("x_landed")
        silu_c = sem("silu_c")
        cols_ok = sem("cols_ok")
        act_hi_ok = sem("act_hi_ok")
        act_lo_ok = sem("act_lo_ok")
        sq_ok = sem("sq_ok")
        ssq_ok = sem("ssq_ok")
        rstd_ok = sem("rstd_ok")
        xn_ok = sem("xn_ok")
        h_hi_ok = sem("h_hi_ok")
        h_ok = sem("h_ok")
        dve_own = sem("dve_own")
        act_own = sem("act_own")
        pool_own = sem("pool_own")
        slot_taken = sem("slot_taken")
        s5_act = sem("s5_act")
        s5_dve = sem("s5_dve")
        bp_ok = sem("bp_ok")
        c_out = [sem("c_out0"), sem("c_out1")]
        b_out = sem("b_out")
        k_ok = sem("k_ok")
        k_out = sem("k_out")
        x_spilled = sem("x_spilled")
        x_back = sem("x_back")
        st_here = [sem(f"st_here{s}") for s in range(3)]
        st_used = sem("st_used")
        scan_step = sem("scan_step")
        states_ok = sem("states_ok")
        yh_ok = sem("yh_ok")
        yl_ok = sem("yl_ok")
        glu_sig = sem("glu_sig")
        ya_ok = sem("ya_ok")
        yal_ok = sem("yal_ok")
        gate_out = [sem("gate_out0"), sem("gate_out1")]
        gate_in = [sem(f"gate_in{s}") for s in range(2)]
        gla_c = sem("gla_c")
        masks_ok = sem("masks_ok")
        z_a = sem("z_a")
        z_d = sem("z_d")
        e_a = sem("e_a")
        e_d = sem("e_d")
        s_ok = sem("s_ok")
        o_ok = sem("o_ok")
        o_rs = sem("o_rs")
        ybh_ok = sem("ybh_ok")
        yb_ok = sem("yb_ok")
        ybtok_ok = sem("ybtok_ok")
        m32_ok = sem("m32_ok")
        mh_ok = sem("mh_ok")
        m_ok = sem("m_ok")
        fin_ok = sem("fin_ok")
        outc_ok = sem("outc_ok")
        out_done = [sem("out_done0"), sem("out_done1")]

        block = es.enter_context(nc.Block())

        def wait_read(eng, j):
            if j >= 4:
                eng.wait_ge(slot_read[j % 4], j // 4)

        def was_read(eng, j):
            eng.wait_ge(slot_read[j % 4], j // 4 + 1)

        def is_done(eng, j):
            eng.wait_ge(job_done, j + 1)

        S5_LINKS = 4 + 12 + 2
        SMALL = 7

        @block.sync
        def _(sp):
            def unit(n, src, view):
                s = n % 4 if isinstance(n, int) else None
                sp.wait_ge(w_split, n + 1)
                sp.dma_start(view, src).then_inc(w_here[s], 16)

            def raw(s, k, c):
                return w_raw[:, s, 0:k * c].rearrange("p (k c) -> p k c", k=k)

            def ada_src(g, k):
                return a["ada_w"][0][P * k:P * k + P, bass.ds(g * D, D)]

            def ada_tile(g, k, first=False):
                s = k % ADA_RING
                if not first:
                    sp.wait_ge(acc_ok, (g - 1) * 16 + (2 * (k - ADA_RING) + 2))
                sp.dma_start(ada_w[:, s, :], ada_src(g, k)).then_inc(ada_here[s], 16)

            for t in range(4):
                sp.dma_start(x_in[:, t, :], a["x"][0, P * t:P * t + P, :]).then_inc(x_landed, 16)
            for t in range(2):
                sp.dma_start(x_in[:, 4 + t, :], a["ctx"][0, P * t:P * t + P, :]).then_inc(x_landed, 16)
            for k in range(KD):
                for g in (1, 0):
                    s = 2 * (k % (ADA_RING0 // 2)) + g
                    past = k - ADA_RING0 // 2
                    if past >= 0:
                        if g:
                            sp.wait_ge(acc_ok, 2 * past + 2)
                        else:
                            sp.wait_ge(ada_used, past + 1)
                    sp.dma_start(ada_w0[:, s, :], ada_src(g, k)).then_inc(ada_here0[s], 16)

            def s5_batch(i):
                sp.wait_ge(s5_in_used, i + 1)
                gs = bass.ds(i * 8, 8)
                for d in range(NDIR):
                    for q, name in enumerate(("s5_b_re", "s5_b_im")):
                        src = a[name][0, d, gs].rearrange("g p c -> p g c")
                        sp.dma_start(bm[64 * q:64 * q + 64, d, :, :], src).then_inc(s5_in, 16)
                        sp.dma_start(bms[64 - 64 * q:128 - 64 * q, d, :, :], src).then_inc(s5_in, 16)
                    for q, name in enumerate(("s5_c_re", "s5_c_im", "s5_c_re")):
                        sp.dma_start(c_in[:, d, q, :], a[name][0, d, gs].rearrange("g c p -> (g c) p"))\
                            .then_inc(s5_in, 16)

            def ffn(first, pre, parts, with_ada):
                wg, wu, wd = (a[f"{pre}_{w}"][0] for w in ("w_gate", "w_up", "w_down"))
                gu_src = [w.rearrange("(k p) c -> p k c", p=P) for w in (wg, wu)]
                wd_src = wd.rearrange("(k p) c -> p k c", p=P)

                def seg(part, i):
                    tiles = part.tiles
                    u0 = first + part.units
                    n = i * part.useg + u0
                    f0 = part.segs * SEG
                    if part.side:
                        s5_batch(i)
                    for v in range(2 * tiles):
                        s = (u0 + v) % 4
                        sp.wait_ge(w_split, n + (v + 1))
                        sp.dma_start(raw(s, KD, P), gu_src[v % 2][:, :, bass.ds(i * (SEG * P) + (f0 + v // 2) * P, P)])\
                            .then_inc(w_here[s], 16)
                        if with_ada:
                            for k in range(KD * v // (2 * tiles), KD * (v + 1) // (2 * tiles)):
                                ada_tile(i + (ADA_START + part.segs), k, part.segs == 0 and k < ADA_RING)
                    for v in range(4):
                        s = (u0 + 2 * tiles + v) % 4
                        sp.wait_ge(w_split, n + (2 * tiles + v + 1))
                        sp.dma_start(raw(s, tiles, 256), wd_src[:, bass.ds(i * SEG + f0, tiles), 256 * v:256 * v + 256])\
                            .then_inc(w_here[s], 16)

                for part in parts:
                    if part.reps == 1:
                        seg(part, 0)
                    else:
                        with sp.Fori(0, part.reps) as i:
                            seg(part, i)

            ffn(UNIT["ffn1"], "ffn1", PARTS1, True)

            w_in = a["w_in"][0].rearrange("(k p) c -> p k c", p=P)

            def wide(n, c0):
                for q in range(4):
                    unit(n + q, w_in[:, 2 * q:2 * q + 2, c0:c0 + 512], raw((n + q) % 4, 2, 512))

            def tall(n, count, c0, c=P):
                for q in range(count):
                    unit(n + q, w_in[:, :, c0 + q * P:c0 + q * P + c], raw((n + q) % 4, KD, c))

            wide(UNIT["u"], C_U)
            tall(UNIT["glr"], 1, C_G, 2 * RANK)
            sp.wait_ge(xn_ok, 2 * KD)
            sp.dma_start(x_scr, x[:, :, 0:NL]).then_inc(x_spilled, 16)
            for k in range(KD):
                ada_tile(ADA_LAST, k)
                if k in (1, 3):
                    tall(UNIT["k"] + k // 2, 1, C_K + P * (k // 2))
                if k in (5, 7):
                    tall(UNIT["q"] + k // 2 - 2, 1, C_Q + P * (k // 2 - 2))
            tall(UNIT["r"], 4, C_R)
            sp.wait_ge(b_out, 16 + 16 * 4 * BATCHES)
            is_done(sp, JOB["ada8"])
            for b in range(8):
                if b >= 3:
                    sp.wait_ge(st_used, b - 2)
                sp.dma_start(stream[:, b % 3, :].rearrange("p (g c) -> p g c", g=8),
                             b_scr[8 * b:8 * b + 8].rearrange("g p c -> p g c")).then_inc(st_here[b % 3], 16)
            tall(UNIT["v"], 4, C_V)
            tall(UNIT["ga"], 8, C_GA)
            tall(UNIT["gb"], 8, C_GB)
            is_done(sp, JOB["vt"] + 5)
            for q in range(2):
                sp.wait_ge(c_out[q], 16 + 32 * BATCHES)
            sp.wait_ge(k_out, 16 + 32 * BATCHES)
            for b in range(8):
                if b >= 3:
                    sp.wait_ge(st_used, 8 + b - 2)
                if b == 2:
                    is_done(sp, JOB["gb"] + 7)
                g0 = 4 * b
                for g in range(4):
                    lags = bass.AP(k_scr.tensor, (g0 + g) * 15 * GC, [[GC, CH], [G * 15 * GC, GC], [1, P]])
                    sp.dma_start(stream2[b % 3][:, 0, g, :], lags).then_inc(st_here[b % 3], 16)
                sp.dma_start(stream2[b % 3][:, 1, :, :].rearrange("p g (t c) -> p g t c", c=GC),
                             c_scr[:, g0:g0 + 4, 1:9, :]).then_inc(st_here[b % 3], 16)
                sp.dma_start(stream2[b % 3][:, 2, :, :].rearrange("p g (t c) -> p g t c", c=GC),
                             c_scr[:, G + g0:G + g0 + 4, 0:8, :]).then_inc(st_here[b % 3], 16)
            glu_w = a["s5_glu_w"][0].rearrange("(k p) c -> p k c", p=P)
            for q in range(2):
                unit(UNIT["glu"] + q, glu_w[:, :, 256 * q:256 * q + 256], raw((UNIT["glu"] + q) % 4, 4, 256))
            for name, w in (("ma", "s5_out"), ("mb", "gla_out")):
                src = a[w][0].rearrange("(k p) c -> p k c", p=P)
                for q in range(4):
                    n = UNIT[name] + q
                    unit(n, src[:, :, 256 * q:256 * q + 256], raw(n % 4, 4, 256))
            w_o = a["w_o"][0].rearrange("(k p) c -> p k c", p=P)
            for q in range(8):
                n = UNIT["wo"] + q
                if q == 4:
                    is_done(sp, JOB["mb"] + KD - 1)
                    sp.dma_start(x[:, :, 0:NL], x_scr).then_inc(x_back, 16)
                unit(n, w_o[:, :, P * q:P * q + P], raw(n % 4, KD, P))
            ffn(UNIT["ffn2"], "ffn2", PARTS2, False)
            for t in range(4):
                sp.wait_ge(outc_ok, t + 1)
                sp.dma_start(out[0, P * t:P * t + P, :], out_sb[:, t % 2, :]).then_inc(out_done[t % 2], 16)
            for s in range(2):
                sp.wait_ge(out_done[s], 32)

        @block.gpsimd
        def _(pool):
            pool.sem_inc(w_split, 4)
            pool.memset(ident[:, :], 0.0).then_inc(pool_own, 1)
            pool.memset(ones[:, :], 1.0).then_inc(consts, 1)
            pool.memset(eps[:, :], EPS).then_inc(consts, 1)
            pool.memset(halfpi[:, :], math.pi / 2).then_inc(consts, 1)
            pool.wait_ge(pool_own, 1)
            pool.affine_select(out=ident[:, :], in_=ident[:, :], compare_op=ALU.not_equal, fill=1.0, base=0,
                               pattern=[[-1, P]], channel_multiplier=1).then_inc(consts, 1)

            def parts(s, cols, made):
                pool.tensor_scalar(w_hi[:, s, 0:cols], w_raw[:, s, 0:cols], 1.0, 1.0, ALU.mult, ALU.mult)\
                    .then_inc(hi_made, 1)
                pool.wait_ge(hi_made, made)
                pool.tensor_tensor(w_lo[:, s, 0:cols], w_raw[:, s, 0:cols], w_hi[:, s, 0:cols].bitcast(F32),
                                   ALU.subtract).then_inc(w_split, 1)

            def split(n, cols):
                pool.wait_ge(w_here[n % 4], 16 * (n // 4 + 1))
                is_done(pool, last_user(n - 4))
                parts(n % 4, cols, n + 1)

            def ffn(units, jobs, parts_, fresh):
                def seg(part, i):
                    js = Seg(jobs + part.jobs, part.tiles, part.side)
                    for v in range(part.useg):
                        n = units + part.units + v
                        pool.wait_ge(w_here[n % 4], i * (4 * part.useg) + 16 * (n // 4 + 1))
                        if not (fresh and n < 4):
                            user = js.gu(v - 4) if v >= 4 else js.jobs - KD + 2 * v + 1
                            pool.wait_ge(job_done, i * part.jseg + (user + 1))
                        pool.sem_inc(slot_taken, 1)
                        parts(n % 4, part.tiles * 256 if v >= 2 * part.tiles else 1024, i * part.useg + (n + 1))

                for part in parts_:
                    if part.reps == 1:
                        seg(part, 0)
                    else:
                        with pool.Fori(0, part.reps) as i:
                            seg(part, i)

            ffn(UNIT["ffn1"], JOB["ffn1"], PARTS1, True)
            n = UNIT["u"]
            while n < UNIT["ffn2"]:
                split(n, 8 * 2 * RANK if n == UNIT["glr"] else 1024)
                if n == UNIT["u"] + 3:
                    pool.wait_ge(h_ok, 2 * KD)
                    pool.memset(zmask[:, :], 1.0).then_inc(pool_own, 1)
                    pool.memset(tri[:, :, :], 1.0).then_inc(pool_own, 1)
                    pool.memset(gate_up[:, :, :], 0.0).then_inc(gla_c, 1)
                    pool.wait_ge(pool_own, 3)
                    pool.memset(zmask[:, 0:NT:LC], 0.0).then_inc(masks_ok, 1)
                    pool.affine_select(out=tri[:, 0, :], in_=tri[:, 0, :], compare_op=ALU.is_ge, fill=0.0, base=0,
                                       pattern=[[1, P]], channel_multiplier=-1).then_inc(masks_ok, 1)
                    pool.affine_select(out=tri[:, 1, :], in_=tri[:, 1, :], compare_op=ALU.is_ge, fill=0.0, base=0,
                                       pattern=[[-1, P]], channel_multiplier=1).then_inc(masks_ok, 1)
                n += 1
            is_done(pool, JOB["wo"] + 5)
            ffn(UNIT["ffn2"], JOB["ffn2"], PARTS2, False)

        @block.tensor
        def _(pe):

            def split_mm(terms):
                last = None
                first = True
                for n, term in enumerate(terms):
                    if len(term) == 2:
                        pe.wait_ge(*term)
                        continue
                    sh, sl, moving = term
                    for q, (st, part) in enumerate(((sl, 0), (sh, 1), (sh, 0))):
                        for mv in moving:
                            last = pe.matmul(mv[2], st, mv[part], start=(first and q == 0),
                                             stop=(n == len(terms) - 1 and q == 2))
                    first = False
                return last

            def wv(s, k, c):
                return [w[:, s, 0:k * c].rearrange("p (k c) -> p k c", k=k) for w in (w_hi, w_lo)]

            def transpose(o, i):
                return pe.transpose(o, i, ident[0:i.shape[0], 0:i.shape[0]])

            pe.wait_ge(consts, 8)
            pe.wait_ge(vec_in, 16 * 9)
            transpose(lat(JOB["vec"])[:, 0:P], vecs[:, :]).then_inc(job_done, 1)
            pe.wait_ge(x_landed, 16 * 6)
            for k in range(KD):
                j = JOB["x"] + k
                wait_read(pe, j)
                for t in range(6):
                    o = lat(j)[:, P * t:P * t + P] if t < 4 else ctx_(j)[:, P * (t - 4):P * (t - 3)]
                    last = transpose(o, x_in[:, t, P * k:P * k + P])
                last.then_inc(job_done, 1)

            j = JOB["ada0"]
            pe.wait_ge(silu_c, 1)
            wait_read(pe, j)
            for k in range(KD):
                s = 2 * (k % (ADA_RING0 // 2))
                pe.wait_ge(ada_here0[s], 16 * (k // (ADA_RING0 // 2) + 1))
                for c in range(KD):
                    last = pe.matmul(ada_cols(j)[:, c, :], ada_w0[:, s, P * c:P * c + P], cs[:, k, :],
                                     start=(k == 0 and c == 0), stop=(k == KD - 1), skip_group_check=True)
                last.then_inc(ada_used if k < KD - 1 else job_done, 1)
            j = JOB["lam"]
            pe.wait_ge(small_in, 16 * SMALL)
            wait_read(pe, j)
            transpose(lat(j)[:, 0:DG], lam_in[:, 0, :])
            transpose(lat(j)[:, P:P + 4], gn_in[:, :])
            transpose(lat(j)[:, DG:2 * DG], lam_in[:, 1, :]).then_inc(job_done, 1)

            def s5_side(i, v, j):
                h = v // 2
                pe.wait_ge(bp_ok, i * 8 + (v + 1))
                if v % 2 == 0:
                    if v == 0:
                        pe.wait_ge(s5_in, i * (16 * 14) + 16 * 14)
                        for d in range(NDIR):
                            for q in range(2):
                                c = (2 * d + q) * P
                                transpose(ctx_(j)[:, c:c + P],
                                          c_in[:, d, q:q + 2, :].rearrange("p r s -> p (r s)"))
                    for g in range(4):
                        last = transpose(lat(j)[:, P * g:P * g + P], bp[:, g, :, :].rearrange("p s c -> p (s c)"))
                else:
                    lag0 = h % 2
                    for g in range(4):
                        last = pe.matmul(lat(j)[0:GC, P * g:P * g + P], bb[:, h % 2, 4 * (h // 2) + g, :],
                                         cp[:, h % 2, g, lag0:lag0 + 8, :].rearrange("p s c -> p (s c)"),
                                         start=True, stop=True)
                last.then_inc(job_done, 1)

            def ada_sums(cols):
                for t in range(KD):
                    for v in range(2):
                        last = pe.matmul(cols[:, t, v:v + 1], ada_acc[:, v, P * t:P * t + P], ones[:, 0:1],
                                         start=True, stop=True)
                return last

            def ada_job(g, j):
                pe.wait_ge(acc_ok, 16 * g)
                wait_read(pe, j)
                ada_sums(ada_cols(j)).then_inc(job_done, 1)

            def norm_sum(j, n):
                pe.wait_ge(ssq_ok, norm_count[0] * KD + KD)
                norm_count[0] += 1
                wait_read(pe, j)
                for t in range(n // P):
                    last = pe.matmul(lat(j)[:, t:t + 1], ssq[:, P * t:P * t + P], ones[:, 0:1], start=True, stop=True)
                last.then_inc(job_done, 1)
                wait_read(pe, j + 1)
                pe.wait_ge(rstd_ok, norm_count[0])
                for t in range(n // P):
                    o = lat(j + 1)[:, P * t:P * t + P] if t < 4 else ctx_(j + 1)[:, P * (t - 4):P * (t - 3)]
                    last = pe.matmul(o, rstd_w[:, t, :], ident[:, :], start=True, stop=True)
                last.then_inc(job_done, 1)

            norm_count = [0]

            def ffn(units, jobs, parts, n, norms, act_base):
                two = n == NT

                def seg(part, i):
                    tiles = part.tiles
                    u0 = units + part.units
                    un = i * part.useg + u0
                    js = Seg(jobs + part.jobs, tiles, part.side)

                    def slot_free(j):
                        pe.wait_ge(slot_read[j % 4], j // 4 + i * (part.jseg // 4))

                    for v in range(2 * tiles):
                        s, j = (u0 + v) % 4, js.gu(v)
                        pe.wait_ge(w_split, un + (v + 5))
                        slot_free(j)
                        if two and v == 2 * tiles - 1:
                            pe.wait_ge(acc_ok, i * 16 + 16 * (part.segs + ADA_START))
                            ada_sums(ada_cols(j, ADA_COL))
                        wh, wl = wv(s, KD, P)
                        terms = []
                        for k in range(KD):
                            if v == 0 and part.segs == 0:
                                terms.append((h_ok, KD * norms + k + 1))
                            if two:
                                mv = [(h_hi[:, k, 384 * q:384 * q + 384], h_lo[:, k, 384 * q:384 * q + 384],
                                       (lat, ctx_)[q](j)[:, 0:384]) for q in range(2)]
                            else:
                                mv = [(h_hi[:, k, 0:NL], h_lo[:, k, 0:NL], lat(j))]
                            terms.append((wh[:, k, :], wl[:, k, :], mv))
                        split_mm(terms).then_inc(job_done, 1)
                        if part.side:
                            slot_free(js.side(v))
                            s5_side(i, v, js.side(v))
                    for v in range(4):
                        s = (u0 + 2 * tiles + v) % 4
                        pe.wait_ge(w_split, un + (2 * tiles + v + 5))
                        wh, wl = wv(s, tiles, 256)
                        for q in range(2):
                            j = js.down(2 * v + q)
                            slot_free(j)
                            terms = []
                            for k in range(tiles):
                                if v == 0 and q == 0:
                                    terms.append((act_lo_ok, i * SEG + (act_base + part.segs * SEG + k + 1)))
                                mv = [(act_hi[:, k, 0:NL], act_lo[:, k, 0:NL], lat(j))]
                                if two:
                                    mv.append((act_hi[:, k, NL:NT], act_lo[:, k, NL:NT], ctx_(j)[:, 0:NC]))
                                terms.append((wh[:, k, P * q:P * q + P], wl[:, k, P * q:P * q + P], mv))
                            split_mm(terms).then_inc(job_done, 1)

                for part in parts:
                    if part.reps == 1:
                        seg(part, 0)
                    else:
                        with pe.Fori(0, part.reps) as i:
                            seg(part, i)

            norm_sum(JOB["norm0"], NT)
            ada_job(1, JOB["ada1"])
            ffn(UNIT["ffn1"], JOB["ffn1"], PARTS1, NT, 0, 0)
            norm_sum(JOB["norm1"], NT)

            def wide_jobs(n, j0, count, cols, rows):
                for t in range(count):
                    j = j0 + t
                    if t == 0:
                        pe.wait_ge(w_split, n + 8)
                    wait_read(pe, j)
                    terms = []
                    for k in range(KD):
                        s = (n + k // 2) % 4
                        if t == 0:
                            terms.append((h_ok, KD + k + 1))
                        mv = [(w_hi[:, s, 512 * (k % 2):512 * (k % 2) + 512], w_lo[:, s, 512 * (k % 2):512 * (k % 2) + 512],
                               lat(j)[0:rows, :])]
                        terms.append((cols(h_hi, k, t), cols(h_lo, k, t), mv))
                    split_mm(terms).then_inc(job_done, 1)

            def tall_jobs(n, j0, count, toks, c=P):
                for t in range(count):
                    j = j0 + t
                    pe.wait_ge(w_split, n + t + 5)
                    wait_read(pe, j)
                    wh, wl = wv((n + t) % 4, KD, c)
                    terms = []
                    for k in range(KD):
                        mv = [(h_hi[:, k, 0:NL], h_lo[:, k, 0:NL], lat(j)[0:c, :])]
                        if toks == NT:
                            mv.append((h_hi[:, k, NL:NT], h_lo[:, k, NL:NT], ctx_(j)[0:c, 0:NC]))
                        terms.append((wh[:, k, :], wl[:, k, :], mv))
                    split_mm(terms).then_inc(job_done, 1)

            wide_jobs(UNIT["u"], JOB["u"], CH, lambda h, k, t: h[:, k, t:NT:CH], NCH)
            tall_jobs(UNIT["glr"], JOB["glr"], 1, NT, 2 * RANK)
            tall_jobs(UNIT["k"], JOB["k"], 2, NT)
            tall_jobs(UNIT["q"], JOB["q"], 2, NL)
            ada_job(ADA_LAST, JOB["ada8"])
            def turn_u(b, j):
                if b == 0:
                    for s in range(CH - 4, CH):
                        was_read(pe, JOB["u"] + s)
                wait_read(pe, j)
                for g in range(4):
                    last = transpose(lat(j)[:, NCH * g:NCH * g + NCH],
                                     u_tok[:, 4 * b + g, :, :].rearrange("p s c -> p (s c)"))
                last.then_inc(job_done, 1)

            def state_inputs(b, j):
                if b == 0:
                    for q in range(4, 8):
                        was_read(pe, CJ["ut", q])
                if b % 2 == 0:
                    pe.wait_ge(st_here[b // 2 % 3], 16 * (b // 6 + 1))
                wait_read(pe, j)
                for q in range(4):
                    g = (4 * b + q) % G
                    e = (4 * b + q) % 8
                    last = pe.matmul(lat(j)[:, NCH * q:NCH * q + NCH], stream[:, b // 2 % 3, P * e:P * e + P],
                                     ut[:, g, :], start=True, stop=True)
                last.then_inc(job_done, 1)
                if b % 2:
                    is_done(pe, j)
                    pe.sem_inc(st_used, 1)

            for name, b, j in CHUNK_JOBS:
                if name == "ut":
                    turn_u(b, j)
                elif name == "xs":
                    state_inputs(b, j)
                else:
                    tall_jobs(UNIT["r"] + b, j, 1, NL)

            tall_jobs(UNIT["v"], JOB["v"], 4, NT)
            for t in range(6):
                j = JOB["vt"] + t
                if t == 0:
                    for q in range(4):
                        was_read(pe, JOB["v"] + q)
                wait_read(pe, j)
                for q in range(4):
                    last = transpose(lat(j)[:, P * q:P * q + P], v_t[:, q, P * t:P * t + P])
                last.then_inc(job_done, 1)
            tall_jobs(UNIT["ga"], JOB["ga"], 8, NL)
            tall_jobs(UNIT["gb"], JOB["gb"], 8, NL)
            def gate_logits(p):
                ti, d = p // 2, p % 2
                j = GJ["z", p]
                wait_read(pe, j)
                for q in range(2):
                    last = pe.matmul((lat, ctx_)[q](j)[:, 0:384], gate_up[:, d, P * ti:P * ti + P],
                                     glr[:, 384 * q:384 * q + 384], start=True, stop=True)
                last.then_inc(job_done, 1)

            pe.wait_ge(small_in, 16 * (SMALL + 2))
            gate_logits(0)
            pe.wait_ge(states_ok, 1)
            for b in range(8):
                j = JOB["y"] + b
                pe.wait_ge(st_here[b % 3], 16 * (3, 3, 2)[b % 3] + 96 * (b // 3 + 1))
                wait_read(pe, j)
                for q in range(4):
                    g = 4 * b + q
                    o = lat(j)[0:LCH, P * q:P * q + P]
                    c0 = NC // CH
                    pe.matmul(o, ut[:, g, 0:LCH], stream2[b % 3][:, 0, q, :], start=True, stop=False)
                    pe.matmul(o, xs[:, c0 - 1:c0 - 1 + LCH, g], stream2[b % 3][:, 1, q, :], start=False, stop=False)
                    last = pe.matmul(o, hb[:, :, g], stream2[b % 3][:, 2, q, :],
                                     start=False, stop=True)
                last.then_inc(job_done, 1)
                is_done(pe, j)
                pe.sem_inc(st_used, 1)
            for c in range(4):
                j = JOB["yt"] + c
                if c == 0:
                    for q in range(4, 8):
                        was_read(pe, JOB["y"] + q)
                wait_read(pe, j)
                for t in range(CH):
                    last = transpose(lat(j)[:, LCH * t:LCH * t + LCH], y_tok[:, t, P * c:P * c + P])
                last.then_inc(job_done, 1)
            gate_logits(1)
            pe.wait_ge(yl_ok, 4)
            for q in range(2):
                n = UNIT["glu"] + q
                pe.wait_ge(w_split, n + 5)
                wh, wl = wv(n % 4, 4, 256)
                for h in range(2):
                    j = JOB["glu"] + 2 * q + h
                    wait_read(pe, j)
                    split_mm([(wh[:, k, P * h:P * h + P], wl[:, k, P * h:P * h + P],
                               [(y_hi[:, k, :], y_lo[:, k, :], lat(j))]) for k in range(4)]).then_inc(job_done, 1)
            def out_product(name, t, j, yh, yl):
                n = UNIT[name] + t // 2
                pe.wait_ge(w_split, n + 5)
                wait_read(pe, j)
                wh, wl = wv(n % 4, 4, 256)
                c = slice(P * (t % 2), P * (t % 2) + P)
                terms = []
                for k in range(4):
                    if name == "mb" and t == 0:
                        terms.append((yb_ok, k + 1))
                    terms.append((wh[:, k, c], wl[:, k, c], [(yh[:, k, :], yl[:, k, :], lat(j))]))
                split_mm(terms).then_inc(job_done, 1)

            done_ma = [0]

            def ma_jobs(name, p):
                for _ in range(MA_AFTER.get((name, p), 0)):
                    t = done_ma[0]
                    if t == 0:
                        pe.wait_ge(yal_ok, 4)
                    out_product("ma", t, MA_JOB[t], ya_hi, ya_lo)
                    done_ma[0] += 1

            for p in range(4):
                ti, d = p // 2, p % 2
                if p in (1, 2):
                    gate_logits(p + 1)
                j = GJ["ket", p]
                pe.wait_ge(e_d, p + 1)
                wait_read(pe, j)
                for t in range(6):
                    o = lat(j)[:, P * t:P * t + P] if t < 4 else ctx_(j)[:, P * (t - 4):P * (t - 3)]
                    last = transpose(o, ke[:, P * t:P * t + P])
                last.then_inc(job_done, 1)
                for hp in range(2):
                    j = GJ["sc", p] + hp
                    wait_read(pe, j)
                    for t in range(4):
                        last = pe.matmul(lat(j)[:, P * t:P * t + P], kz[:, hp, P * t:P * t + P],
                                         e1q[:, P * t:P * t + P], start=True, stop=True)
                    last.then_inc(job_done, 1)
                was_read(pe, GJ["ket", p])
                order = (4, 5, 0, 1, 2, 3) if d == 0 else (5, 4, 3, 2, 1, 0)
                for half in range(2):
                    j = GJ["kv", p] + half
                    wait_read(pe, j)
                    for q in range(3):
                        t = order[3 * half + q]
                        for par in range(2):
                            for hp in range(2):
                                hd = 2 * ti + hp
                                last = pe.matmul((lat, ctx_)[par](j)[64 * hp:64 * hp + 64, P * q:P * q + P],
                                                 ket[64 * par:64 * par + 64, t, 64 * hp:64 * hp + 64],
                                                 v_sb[64 * par:64 * par + 64, t, DV * hd:DV * hd + DV],
                                                 start=True, stop=True)
                    last.then_inc(job_done, 1)
                ma_jobs("kv", p)
                if d == 0:
                    continue
                pe.wait_ge(s_ok, p + 1)
                for t in range(4):
                    j = GJ["out", p] + t
                    wait_read(pe, j)
                    for hp in range(2):
                        hd = 2 * ti + hp
                        c = slice(DV * hp, DV * hp + DV)
                        for dd in range(2):
                            pe.matmul(lat(j)[:, c], at_sb[:, dd, hp, t, :], v_sb[:, t, DV * hd:DV * hd + DV],
                                      start=(dd == 0), stop=False, skip_group_check=True)
                        for par in range(2):
                            for dd in range(2):
                                last = pe.matmul(lat(j)[64 * par:64 * par + 64, c],
                                                 qz[:, dd, hp, P * t + 64 * par:P * t + 64 * par + 64],
                                                 s_st[:, dd, 2 * t + par, :], start=False,
                                                 stop=(par == 1 and dd == 1), skip_group_check=True)
                    last.then_inc(job_done, 1)
                ma_jobs("out", p)
            pe.wait_ge(ybtok_ok, 1)
            for c in range(4):
                j = JOB["ybt"] + c
                wait_read(pe, j)
                for t in range(4):
                    last = transpose(lat(j)[:, P * t:P * t + P], o_sb[:, t, P * c:P * c + P])
                last.then_inc(job_done, 1)
            for t in range(KD):
                out_product("mb", t, JOB["mb"] + t, yb_hi, yb_lo)
            for q in range(KD):
                n, j = UNIT["wo"] + q, JOB["wo"] + q
                pe.wait_ge(w_split, n + 5)
                wait_read(pe, j)
                wh, wl = wv(n % 4, KD, P)
                terms = []
                for k in range(KD):
                    if q == 0:
                        terms.append((m_ok, k + 1))
                    terms.append((wh[:, k, :], wl[:, k, :], [(m_hi[:, k, :], m_lo[:, k, :], lat(j))]))
                split_mm(terms).then_inc(job_done, 1)
            norm_sum(JOB["norm2"], NL)
            ffn(UNIT["ffn2"], JOB["ffn2"], PARTS2, NL, 2, FF // P)
            norm_sum(JOB["norm3"], NL)
            pe.wait_ge(fin_ok, KD)
            for t in range(4):
                j = JOB["out"] + t
                wait_read(pe, j)
                for k in range(KD):
                    last = transpose((lat if k < 4 else ctx_)(j)[:, P * (k % 4):P * (k % 4) + P],
                                     x[:, k, P * t:P * t + P])
                last.then_inc(job_done, 1)

        @block.scalar
        def _(act):
            own = [0]

            def link(ins):
                own[0] += 1
                ins.then_inc(act_own, 1)
                act.wait_ge(act_own, own[0])

            rows = [("ada_b", 72), ("ffn1_norm", 8), ("mix_norm", 8), ("ffn2_norm", 8), ("final_norm", 8), ("c", 8),
                    ("c_ctx", 8), ("s5_glu_b", 4), ("gla_gate_b", 4)]
            r0 = 0
            for name, n in rows:
                src = a[name]
                while len(src.shape) > 1:
                    src = src.rearrange("a b -> (a b)") if len(src.shape) == 2 else src.rearrange("a b c -> (a b c)")
                act.dma_start(vecs[r0:r0 + n, :], src.rearrange("(r p) -> r p", p=P)).then_inc(vec_in, 16)
                r0 += n
            for q, name in enumerate(("s5_lambda_re", "s5_lambda_im")):
                for h in range(2):
                    act.dma_start(lam_in[:, q, SP5 * h:SP5 * h + SP5], a[name][0].rearrange("d g p -> (d g) p"))\
                        .then_inc(small_in, 16)
            act.dma_start(s5t[:, 0, :], a["s5_log_dt"][0].rearrange("d g -> (d g)").partition_broadcast(P))\
                .then_inc(small_in, 16)
            act.dma_start(gn_in[:, :], a["gla_norm"][0].rearrange("(r p) -> r p", p=P)).then_inc(small_in, 16)
            act.dma_start(dg5[:, :], a["s5_d"][0].rearrange("(g c) -> c g", c=GC),
                          allow_slow_non_contiguous=True).then_inc(small_in, 16)

            j = JOB["vec"]
            is_done(act, j)
            act.activation(vt[:, :], lat(j)[:, 0:P], ACT.Copy).then_inc(slot_read[j % 4], 1)
            was_read(act, j)
            for v, row in enumerate((104, 112)):
                ins = act.activation(cs[:, :, v], vt[:, row:row + 8], ACT.Silu)
            ins.then_inc(silu_c, 1)
            for k in range(KD):
                j = JOB["x"] + k
                is_done(act, j)
                act.activation(x[:, k, 0:NL], lat(j), ACT.Copy)
                act.activation(x[:, k, NL:NT], ctx_(j)[:, 0:NC], ACT.Copy).then_inc(slot_read[j % 4], 1)

            def s5_trig():
                act.wait_ge(s5_dve, 1)
                act.activation(s5t[:, 8, :], s5t[:, 4, :], ACT.Exp).then_inc(s5_act, 1)
                act.activation(s5t[:, 9, :], s5t[:, 6, :], ACT.Sin).then_inc(s5_act, 1)
                link(act.activation(s5t[:, 10, :], s5t[:, 6, :], ACT.Abs))
                act.activation(s5t[:, 11, :], s5t[:, 10, :], ACT.Sin, bias=halfpi[:, :], scale=-1.0).then_inc(s5_act, 1)

            def s5_side(i, f, j):
                act.wait_ge(b_out, i * 64 + 16 * (f + 1))
                if f == 0:
                    cv = ctx_(j).rearrange("p (d q c) -> p d q c", d=NDIR, q=2)
                    for o, q, sg in ((cm, 0, nsgn), (cms, 1, sgn)):
                        act.activation(o[:, :, :, :].rearrange("p d g c -> p d (g c)"), cv[:, :, q, :], ACT.Copy,
                                       scale=sg[:, 0:1])
                act.activation(bt_sb[:, :, :].rearrange("p g c -> p (g c)"), lat(j), ACT.Copy)\
                    .then_inc(slot_read[j % 4], 1)

            def s5_out(i, f, j_value):
                g0 = bass.ds(i * 8 + (G * (f % 2) + 4 * (f // 2)), 4)
                act.wait_ge(*j_value)
                act.dma_start(b_scr[g0].rearrange("g p c -> p g c"), bt_sb[:, :, :]).then_inc(b_out, 16)
                act.wait_ge(bp_ok, i * 8 + (2 * f + 2))
                act.dma_start(c_scr[:, g0, :, :], cp[:, f % 2, :, :, :]).then_inc(c_out[f % 2], 16)

            def norm(q, j, n):
                for k in range(KD):
                    if q == 0:
                        was_read(act, JOB["x"] + k)
                    else:
                        was_read(act, (JOB["norm1"] - KD, JOB["wo"], JOB["norm3"] - KD)[q - 1] + k)
                    if k >= 2 or q:
                        act.wait_ge(ssq_ok, KD * q + k - 1)
                    act.activation(silu[:, k % 2, 0:n], x[:, k, 0:n], ACT.Square).then_inc(sq_ok, 1)
                is_done(act, j)
                if q == 1:
                    act.wait_ge(k_out, 16 + 32 * BATCHES)
                act.activation(root[:, 0:n // P], lat(j)[:, 0:n // P], ACT.Sqrt, bias=eps[:, :], scale=1.0 / D)\
                    .then_inc(slot_read[j % 4], 1)
                if q == 3:
                    return
                act.wait_ge(cols_ok, q + 1)
                for k in range(KD):
                    act.wait_ge(xn_ok, KD * q + k + 1)
                    parts = [(slice(0, NL), 0)] + ([(slice(NL, NT), 1)] if n == NT else [])
                    for c, v in parts:
                        ins = act.activation(h_hi[:, k, c], gu[:, k % 2, c], ACT.Identity,
                                             bias=mod[:, 24 * q + k, v:v + 1])
                    ins.then_inc(h_hi_ok, 1)

            def ffn(jobs, parts, n):
                def seg(part, i):
                    js = Seg(jobs + part.jobs, part.tiles, part.side)
                    for f in range(part.tiles):
                        jg, ju = js.gu(2 * f), js.gu(2 * f + 1)
                        dst, src = silu[:, f % 2, 0:n], lat(jg)
                        if n == NT:
                            dst, src = dst.rearrange("p (b c) -> p b c", b=2), both(jg, 384)
                        act.wait_ge(job_done, (jg + 1) + i * part.jseg)
                        act.activation(dst, src, ACT.Silu).then_inc(slot_read[jg % 4], 1)
                        if part.side:
                            j = js.side(2 * f)
                            act.wait_ge(job_done, (j + 1) + i * part.jseg)
                            s5_side(i, f, j)
                            s5_out(i, f, (slot_read[j % 4], (j // 4 + 1) + i * (part.jseg // 4)))
                        act.wait_ge(slot_read[ju % 4], (ju // 4 + 1) + i * (part.jseg // 4))
                        act.activation(act_hi[:, f, 0:n], gu[:, f % 2, 0:n], ACT.Copy).then_inc(act_hi_ok, 1)
                        if n == NT and part.segs == 0 and f == 0:
                            act.wait_ge(small_in, 16 * SMALL)
                            act.activation(s5t[:, 1, :], s5t[:, 0, :], ACT.Exp).then_inc(s5_act, 1)
                        if n == NT and part.segs == 0 and f == 1:
                            s5_trig()
                        if part.side and f % 2:
                            act.wait_ge(k_ok, i * 2 + (f // 2 + 1))
                            act.dma_start(k_scr[:, bass.ds(i * 8 + 4 * (f // 2), 4), :, :], kf[:, :, :, :])\
                                .then_inc(k_out, 16)

                for part in parts:
                    if part.reps == 1:
                        seg(part, 0)
                    else:
                        with act.Fori(0, part.reps) as i:
                            seg(part, i)

            norm(0, JOB["norm0"], NT)
            ffn(JOB["ffn1"], PARTS1, NT)
            norm(1, JOB["norm1"], NT)

            act.wait_ge(h_ok, 2 * KD)
            for s in range(CH):
                j = JOB["u"] + s
                is_done(act, j)
                act.activation(u_tok[:, :, CH - 1 - s, :], lat(j)[0:NCH, :].rearrange("p (g c) -> p g c", c=GC), ACT.Copy)\
                    .then_inc(slot_read[j % 4], 1)
            act.wait_ge(gla_c, 1)
            for d in range(2):
                act.dma_start(gate_up[RANK * d:RANK * d + RANK, d, :], a["gla_gate_up"][0, d]).then_inc(small_in, 16)

            def w_major(t):
                return t.rearrange("p (w r) -> p r w", r=ROWS)

            def row_major(t):
                return t.rearrange("p (r w) -> p r w", w=GRID_W)

            def evac_tokens(j, dst, n, rows, scale=1.0):
                is_done(act, j)
                ins = act.activation(w_major(dst[:, 0:NL]), row_major(lat(j)[0:rows, :]), ACT.Copy, scale=scale)
                if n == NT:
                    ins = act.activation(dst[:, NL:NT], ctx_(j)[0:rows, 0:NC], ACT.Copy)
                ins.then_inc(slot_read[j % 4], 1)

            evac_tokens(JOB["glr"], glr[:, :], NT, 2 * RANK)
            for q in range(2):
                evac_tokens(JOB["k"] + q, kt[:, q, :], NT, P)
            for q in range(2):
                evac_tokens(JOB["q"] + q, qt[:, q, :], NL, P, DK ** -0.5)
            act.wait_ge(x_spilled, 16)
            nctx = NC // CH
            for name, b, j in CHUNK_JOBS:
                is_done(act, j)
                if name == "ut":
                    act.activation(ut[:, 4 * b:4 * b + 4, :], lat(j)[:, 0:4 * NCH].rearrange("p (g c) -> p g c", g=4),
                                   ACT.Copy).then_inc(slot_read[j % 4], 1)
                elif name == "r":
                    act.activation(r_sb[:, b, :], lat(j), ACT.Silu).then_inc(slot_read[j % 4], 1)
                else:
                    src = lat(j)[:, 0:4 * NCH].rearrange("p (g c) -> p c g", g=4)
                    dgs = slice(4 * b, 4 * b + 4)
                    lats, ctxs = src[:, 0:LCH, :], src[:, LCH:NCH, :]
                    if b >= 8:
                        lats, ctxs = lats[:, ::-1, :], ctxs[:, ::-1, :]
                    act.activation(xs[:, nctx:NCH, dgs], lats, ACT.Copy)
                    act.activation(xs[:, 0:nctx, dgs], ctxs, ACT.Copy).then_inc(slot_read[j % 4], 1)
            for q in range(4):
                evac_tokens(JOB["v"] + q, v_t[:, q, :], NT, P)
            for t in range(6):
                j = JOB["vt"] + t
                is_done(act, j)
                act.activation(v_sb[:, t, :], lat(j), ACT.Copy).then_inc(slot_read[j % 4], 1)
            for t in range(16):
                j = JOB["ga"] + t
                is_done(act, j)
                if t >= 2:
                    act.wait_ge(gate_out[t % 2], 16 * (t // 2))
                act.activation(gate_buf[:, t % 2, :], lat(j), ACT.Sigmoid).then_inc(slot_read[j % 4], 1)
                was_read(act, j)
                act.dma_start(g_scr[:, t, :], gate_buf[:, t % 2, :]).then_inc(gate_out[t % 2], 16)
            def softplus(p):
                g = g_a[p % 2]
                if p >= 2:
                    act.wait_ge(e_d, p - 1)
                is_done(act, GJ["z", p])
                link(act.activation(g[:, :].rearrange("p (b c) -> p b c", b=2), both(GJ["z", p], 384), ACT.Abs,
                                    bias=vt[:, 124 + 2 * (p % 2) + p // 2:125 + 2 * (p % 2) + p // 2]))
                link(act.activation(g[:, :], g[:, :], ACT.Exp, scale=-1.0))
                act.activation(g[:, :], g[:, :], ACT.Ln, bias=ones[:, 0:1]).then_inc(z_a, 1)

            def decays(p):
                act.wait_ge(z_d, p + 1)
                gv = g_c[:, :].rearrange("p (c t) -> p c t", t=LC)
                act.activation(g_a[p % 2][:, 0:NL], g_b[:, 0:NL], ACT.Exp, scale=1.0 / 16)
                link(act.activation(decay[:, p % 2, :], gv[:, :, (LC - 1 if p % 2 == 0 else 0)], ACT.Exp, scale=1.0 / 16))
                act.activation(g_b[:, 0:NL], g_b[:, 0:NL], ACT.Exp, scale=-1.0 / 16)
                act.activation(g_d[:, :], g_d[:, :], ACT.Exp, scale=1.0 / 16)
                act.activation(g_c[:, 0:NL], g_c[:, 0:NL], ACT.Exp, scale=1.0 / 16).then_inc(e_a, 1)

            softplus(0)
            for b in range(8):
                j = JOB["y"] + b
                if b == 2:
                    decays(0)
                is_done(act, j)
                act.activation(y_tok[:, :, 64 * b:64 * b + 64].rearrange("p t (g c) -> p t g c", c=GC),
                               lat(j)[0:LCH, :].rearrange("p (g t c) -> p t g c", g=4, c=GC), ACT.Gelu_apprx_tanh)\
                    .then_inc(slot_read[j % 4], 1)


            def token_order(t):
                return t.rearrange("p (k t) -> p t k", t=CH)

            for c in range(4):
                j = JOB["yt"] + c
                is_done(act, j)
                src = lat(j).rearrange("p (t k) -> p t k", t=CH)
                act.activation(token_order(y32[:, c, :]), src, ACT.Copy)
                act.activation(token_order(y_hi[:, c, :]), src, ACT.Copy).then_inc(yh_ok, 1)
            softplus(1)
            for c in range(4):
                j = JOB["glu"] + c
                is_done(act, j)
                if c < 2:
                    act.wait_ge(gate_out[c], 128)
                act.activation(gate_buf[:, c % 2, :], lat(j), ACT.Sigmoid, bias=vt[:, 120 + c:121 + c])\
                    .then_inc(slot_read[j % 4], 1)
                act.wait_ge(ya_ok, c + 1)
                if c == 3:
                    for e in range(4):
                        act.activation(ya_hi[:, e, :], y32[:, e, :], ACT.Copy).then_inc(glu_sig, 1)
            taken_ma = [0]

            def take_ma(name, p):
                for _ in range(MA_AFTER.get((name, p), 0)):
                    t = taken_ma[0]
                    j = MA_JOB[t]
                    is_done(act, j)
                    act.activation(ma[:, t, :], lat(j), ACT.Copy).then_inc(slot_read[j % 4], 1)
                    taken_ma[0] += 1

            for p in range(4):
                if p in (1, 2):
                    softplus(p + 1)
                j = GJ["ket", p]
                is_done(act, j)
                act.activation(ket[:, 0:4, :].rearrange("p t c -> p (t c)"), lat(j), ACT.Copy)
                act.activation(ket[:, 4:6, :].rearrange("p t c -> p (t c)"), ctx_(j)[:, 0:2 * P], ACT.Copy)\
                    .then_inc(slot_read[j % 4], 1)
                if p < 3:
                    decays(p + 1)
                take_ma("kv", p)
                if p % 2 == 0:
                    continue
                for t in range(4):
                    j = GJ["out", p] + t
                    is_done(act, j)
                    act.activation(o_sb[:, t, DV * (p - 1):DV * (p - 1) + 2 * DV], lat(j)[:, 0:2 * DV], ACT.Copy)\
                        .then_inc(slot_read[j % 4], 1)
                    was_read(act, j)
                    act.sem_inc(o_ok, 1)
                take_ma("out", p)
            def load_gates(t):
                for br in range(2):
                    act.dma_start(gates[:, t % 2, br, :], g_scr[:, KD * br + t, :]).then_inc(gate_in[t % 2], 16)

            for t in range(2):
                load_gates(t)
            act.wait_ge(o_rs, 1)
            act.activation(oms[:, :], oms[:, :], ACT.Sqrt, bias=eps[:, :], scale=1.0 / DV).then_inc(o_rs, 1)
            for c in range(4):
                j = JOB["ybt"] + c
                was_read(act, j)
                act.activation(yb_hi[:, c, :], r_sb[:, c, :], ACT.Copy).then_inc(ybh_ok, 1)
            for t in range(KD):
                act.wait_ge(m32_ok, t + 1)
                act.activation(m_hi[:, t, :], mt[:, t % 2, 2, :], ACT.Copy).then_inc(mh_ok, 1)
                if t + 2 < KD:
                    load_gates(t + 2)
            norm(2, JOB["norm2"], NL)
            ffn(JOB["ffn2"], PARTS2, NL)
            norm(3, JOB["norm3"], NL)
            for t in range(4):
                j = JOB["out"] + t
                is_done(act, j)
                if t >= 2:
                    act.wait_ge(out_done[t % 2], 16)
                act.activation(out_sb[:, t % 2, :].rearrange("p (b c) -> p b c", b=2), both(j, 512), ACT.Copy)\
                    .then_inc(slot_read[j % 4], 1)
                was_read(act, j)
                act.sem_inc(outc_ok, 1)

        @block.vector
        def _(dve):
            own = [0]

            def link(ins):
                own[0] += 1
                ins.then_inc(dve_own, 1)
                dve.wait_ge(dve_own, own[0])

            TT, TS, STT = dve.tensor_tensor, dve.tensor_scalar, dve.scalar_tensor_tensor
            dve.memset(sgn[0:64, :], -1.0).then_inc(consts, 1)
            dve.memset(sgn[64:128, :], 1.0).then_inc(consts, 1)
            dve.memset(nsgn[0:64, :], 1.0).then_inc(consts, 1)
            dve.memset(nsgn[64:128, :], -1.0).then_inc(consts, 1)
            dve.sem_inc(s5_in_used, 1)
            dve.sem_inc(b_out, 16)
            dve.sem_inc(k_out, 16)
            for q in range(2):
                dve.sem_inc(c_out[q], 16)

            f = [s5t[:, q, :] for q in range(16)]
            dt, lr, li, th = f[1], f[2], f[3], f[6]

            def s5_lambda():
                j = JOB["lam"]
                is_done(dve, j)
                dve.tensor_copy(li, lat(j)[:, DG:2 * DG])
                dve.tensor_copy(gn[:, :], lat(j)[:, P:P + 4])
                TS(lr, lat(j)[:, 0:DG], -1e-4, None, ALU.min).then_inc(slot_read[j % 4], 1)

            def s5_angle():
                was_read(dve, JOB["lam"])
                dve.wait_ge(s5_act, 1)
                TT(f[4], lr, dt, ALU.mult)
                link(TT(f[5], li, dt, ALU.mult))
                link(TS(f[7], f[5], 1.0 / TWO_PI, ROUND, ALU.mult, ALU.add))
                link(TS(f[7], f[7], -ROUND, None, ALU.add))
                link(STT(f[6], f[7], -PI_1, f[5], ALU.mult, ALU.add))
                link(STT(f[6], f[7], -PI_2, f[6], ALU.mult, ALU.add))
                link(STT(f[6], f[7], -PI_3, f[6], ALU.mult, ALU.add))
                TS(th, f[6], PI_MAX, -PI_MAX, ALU.min, ALU.max).then_inc(s5_dve, 1)
                link(TT(f[12], lr, lr, ALU.mult))
                link(TT(f[13], li, li, ALU.mult))
                link(TT(f[12], f[12], f[13], ALU.add))
                link(dve.reciprocal(f[12], f[12]))

            def s5_powers():
                dve.wait_ge(s5_act, 4)
                dve.memset(pr[:, 0, :], 1.0)
                dve.memset(pis[:, 0, :], 0.0)
                TT(pr[:, 1, :], f[8], f[11], ALU.mult)
                link(TT(f[9], f[8], f[9], ALU.mult))
                link(TS(f[13], pr[:, 1, :], -1.0, None, ALU.add))
                link(TT(f[14], f[13], lr, ALU.mult))
                link(TT(f[15], f[9], li, ALU.mult))
                link(TT(f[14], f[14], f[15], ALU.add))
                TT(coef[:, 0, :], f[14], f[12], ALU.mult)
                link(TT(f[15], f[13], li, ALU.mult))
                link(TT(f[13], f[9], lr, ALU.mult))
                link(TT(f[15], f[13], f[15], ALU.subtract))
                link(TT(f[15], f[15], f[12], ALU.mult))
                TS(coef[:, 1, :], f[15], sgn[:, 0:1], None, ALU.mult)
                link(dve.tensor_copy(pis[:, 1, :], f[9]))
                for q in range(2, 9):
                    TT(f[0], pr[:, q - 1, :], pr[:, 1, :], ALU.mult)
                    TT(f[10], pis[:, q - 1, :], f[9], ALU.mult)
                    TT(f[13], pr[:, q - 1, :], f[9], ALU.mult)
                    link(TT(f[14], pis[:, q - 1, :], pr[:, 1, :], ALU.mult))
                    TT(pr[:, q, :], f[0], f[10], ALU.subtract)
                    link(TT(pis[:, q, :], f[13], f[14], ALU.add))
                link(TS(pis[:, :, :], pis[:, :, :], sgn[:, 0:1], None, ALU.mult))
                dve.tensor_copy(lam8[:, 0, :], pr[:, 8, :])
                link(TS(lam8[:, 1, :], pis[:, 8, :], -1.0, None, ALU.mult))

            s5_n = [0]

            def s5_link(i, ins):
                s5_n[0] += 1
                ins.then_inc(s5_own, 1)
                dve.wait_ge(s5_own, i * S5_LINKS + s5_n[0])

            def s5_input(i):
                dve.wait_ge(s5_in, i * (16 * 14) + 16 * 14)

                def c(q):
                    return coef[:, q, :].rearrange("p (d g) -> p d g", d=NDIR)[:, :, bass.ds(i * 8, 8)]\
                        .unsqueeze(3).to_broadcast([P, NDIR, 8, GC])

                s_bb, s_bbs, s_bm, s_bms, tmp = (t[:, :, :, :] for t in (bb, bbs, bm, bms, bb_t))
                TT(s_bb, s_bm, c(0), ALU.mult)
                TT(s_bbs, s_bms, c(0), ALU.mult)
                s5_link(i, TT(tmp, s_bms, c(1), ALU.mult))
                s5_link(i, TT(s_bb, s_bb, tmp, ALU.add))
                s5_link(i, TT(tmp, s_bm, c(1), ALU.mult))
                s5_link(i, TT(s_bbs, s_bbs, tmp, ALU.subtract))

            def half_power(q, n, rev):
                w = pw[:, q, 0:n, :]
                if rev:
                    w = w[:, ::-1, :]
                return w.rearrange("p s g -> p g s").unsqueeze(3).to_broadcast([P, 4, n, GC])

            def half_matrix(t, h, n):
                return t[:, h % 2, 4 * (h // 2):4 * (h // 2) + 4, :].unsqueeze(2).to_broadcast([P, 4, n, GC])

            def s5_b(i, h):
                if h:
                    dve.wait_ge(bp_ok, i * 8 + 2 * h)
                tmp, rev = ptmp[:, :, 0:CH, :], h % 2 == 1
                s5_link(i, dve.tensor_copy(pw[:, :, :, :],
                                           powers[:, :, :, bass.ds(i * 8 + (G * (h % 2) + 4 * (h // 2)), 4)]))
                TT(bp[:, :, :, :], half_power(0, CH, rev), half_matrix(bb, h, CH), ALU.mult)
                s5_link(i, TT(tmp, half_power(1, CH, rev), half_matrix(bbs, h, CH), ALU.mult))
                TT(bp[:, :, :, :], bp[:, :, :, :], tmp, ALU.add).then_inc(bp_ok, 1)

            def s5_c(i, h):
                dve.wait_ge(bp_ok, i * 8 + (2 * h + 1))
                dve.wait_ge(c_out[h % 2], i * 32 + (16 * (h // 2) + 16))
                o, rev = cp[:, h % 2, :, :, :], h % 2 == 1
                TT(o, half_power(0, 9, rev), half_matrix(cm, h, 9), ALU.mult)
                s5_link(i, TT(ptmp[:, :, :, :], half_power(1, 9, rev), half_matrix(cms, h, 9), ALU.mult))
                TT(o, o, ptmp[:, :, :, :], ALU.subtract).then_inc(bp_ok, 1)

            def s5_lags(i, h, j, read):
                src = lat(j)[0:GC, :].rearrange("p (g t c) -> p g t c", g=4, c=GC)
                if h % 2 == 0:
                    dve.wait_ge(k_out, i * 32 + (16 * (h // 2) + 16))
                    dve.tensor_copy(kf[:, :, 7:15, :], src).then_inc(slot_read[j % 4], 1)
                    read()
                    return
                dve.tensor_copy(kf[:, :, 0:7, :], src[:, :, 0:7, :])
                TT(kf[:, :, 7, :], src[:, :, 7, :], kf[:, :, 7, :], ALU.add).then_inc(slot_read[j % 4], 1)
                dve.wait_ge(bp_ok, i * 8 + min(2 * h + 3, 8))
                tmp = ptmp[0:GC, :, 0, :]
                s5_link(i, TT(tmp, dg5[:, bass.ds(i * 8 + 4 * (h // 2), 4)].unsqueeze(2).to_broadcast([GC, 4, GC]),
                              ident[0:GC, 0:GC].unsqueeze(1).to_broadcast([GC, 4, GC]), ALU.mult))
                TT(kf[:, :, 7, :], kf[:, :, 7, :], tmp, ALU.add).then_inc(k_ok, 1)

            def ada_add(g, k):
                s = k % ADA_RING
                tile = ada_w[:, s, :]
                if isinstance(g, int) and g == 1:
                    s = 2 * (k % (ADA_RING0 // 2)) + 1
                    tile = ada_w0[:, s, :]
                    dve.wait_ge(ada_here0[s], 16 * (k // (ADA_RING0 // 2) + 1))
                else:
                    dve.wait_ge(ada_here[s], (g - ADA_START) * (16 * KD // ADA_RING) + 16 * (k // ADA_RING + 1))
                for v in range(2):
                    if k == 0:
                        TS(ada_acc[:, v, :], tile, cs[:, k, v:v + 1], None, ALU.mult).then_inc(acc_ok, 1)
                    else:
                        dve.wait_ge(acc_ok, (g - 1) * 16 + (2 * k + v - 1))
                        STT(ada_acc[:, v, :], tile, cs[:, k, v:v + 1], ada_acc[:, v, :],
                            ALU.mult, ALU.add).then_inc(acc_ok, 1)

            def ada_bias(cols, t):
                return TT(mod[:, t, :], cols, vt[:, t].unsqueeze(2).to_broadcast([P, KD, 2]), ALU.add)

            def scale_cols(q, g_row):
                STT(amul[:, q, :, :], mod[:, 24 * q + 8:24 * q + 16, :], 1.0,
                    vt[:, g_row:g_row + 8].unsqueeze(2).to_broadcast([P, 8, 2]), ALU.add, ALU.mult).then_inc(cols_ok, 1)

            def add_square(q, k, n):
                dve.wait_ge(sq_ok, KD * q + k + 1)
                if k == 0:
                    dve.tensor_copy(ssq[:, 0:n], silu[:, 0, 0:n]).then_inc(ssq_ok, 1)
                else:
                    dve.wait_ge(ssq_ok, KD * q + k)
                    TT(ssq[:, 0:n], ssq[:, 0:n], silu[:, k % 2, 0:n], ALU.add).then_inc(ssq_ok, 1)

            def norm_root(j, n):
                was_read(dve, j)
                link(dve.reciprocal(root[:, 0:n // P], root[:, 0:n // P]))
                dve.tensor_copy(rstd_w[:, 0:n // P, :], root[:, 0:n // P].unsqueeze(2).to_broadcast([P, n // P, P]))\
                    .then_inc(rstd_ok, 1)

            def rstd(j, c):
                return (ctx_(j + 1)[:, c.start - NL:c.stop - NL] if c.start >= NL else lat(j + 1)[:, c])

            def norm(q, n):
                j = JOB[f"norm{q}"]
                is_done(dve, j + 1)
                if q == 3:
                    for k in range(KD):
                        STT(x[:, k, 0:n], x[:, k, 0:n], vt[:, 96 + k:97 + k], rstd(j, slice(0, n)), ALU.mult, ALU.mult)\
                            .then_inc(fin_ok, 1)
                    dve.wait_ge(fin_ok, KD)
                    dve.sem_inc(slot_read[(j + 1) % 4], 1)
                    return
                parts = [(slice(0, NL), 0)] + ([(slice(NL, NT), 1)] if n == NT else [])

                def xn(k):
                    if k >= 2:
                        dve.wait_ge(h_ok, KD * q + k - 1)
                    for c, v in parts:
                        ins = STT(gu[:, k % 2, c], x[:, k, c], amul[:, q, k, v:v + 1], rstd(j, c), ALU.mult, ALU.mult)
                    ins.then_inc(xn_ok, 1)
                    if k == KD - 1:
                        dve.wait_ge(xn_ok, KD * q + KD)
                        dve.sem_inc(slot_read[(j + 1) % 4], 1)

                dve.wait_ge(cols_ok, q + 1)
                xn(0)
                for k in range(KD):
                    if k + 1 < KD:
                        xn(k + 1)
                    dve.wait_ge(xn_ok, KD * q + k + 1)
                    dve.wait_ge(h_hi_ok, KD * q + k + 1)
                    for c, v in parts:
                        ins = STT(h_lo[:, k, c], gu[:, k % 2, c], mod[:, 24 * q + k, v:v + 1],
                                  h_hi[:, k, c].bitcast(F32), ALU.add, ALU.subtract)
                    ins.then_inc(h_ok, 1)

            def ffn(jobs, parts, n, q, act_base):
                def seg(part, i):
                    tiles = part.tiles
                    js = Seg(jobs + part.jobs, tiles, part.side)
                    a0 = act_base + part.segs * SEG
                    s5_n[0] = 0

                    def done(j):
                        dve.wait_ge(job_done, (j + 1) + i * part.jseg)

                    def read(j):
                        dve.wait_ge(slot_read[j % 4], (j // 4 + 1) + i * (part.jseg // 4))

                    ada = ((0, 3), (3, 6), (6, 8), (8, 8)) if tiles == SEG else ((0, 5), (5, 8))
                    for f_ in range(tiles):
                        jg, ju = js.gu(2 * f_), js.gu(2 * f_ + 1)
                        if part.side and f_ == 0:
                            s5_input(i)
                            s5_b(i, 0)
                        if q == 0:
                            for k in range(*ada[f_]):
                                ada_add(i + (ADA_START + part.segs), k)
                        if part.side:
                            if f_ == 0:
                                read(js.side(0))
                                dve.sem_inc(s5_in_used, 1)
                            s5_c(i, f_)
                        read(jg)
                        done(ju)
                        if n == NT:
                            dst, sl = (t[:, f_ % 2, :].rearrange("p (b c) -> p b c", b=2) for t in (gu, silu))
                            src = both(ju, 384)
                        else:
                            dst, src, sl = gu[:, f_ % 2, 0:n], lat(ju), silu[:, f_ % 2, 0:n]
                        if q == 0 and f_ == tiles - 1:
                            ada_bias(ada_cols(ju, ADA_COL), bass.ds(i * KD + KD * (ADA_START + part.segs), KD))
                        STT(dst, src, 0.5, sl, ALU.mult, ALU.mult).then_inc(slot_read[ju % 4], 1)
                        read(ju)
                        dve.wait_ge(act_hi_ok, i * SEG + (a0 + f_ + 1))
                        TT(act_lo[:, f_, 0:n], gu[:, f_ % 2, 0:n], act_hi[:, f_, 0:n].bitcast(F32), ALU.subtract)\
                            .then_inc(act_lo_ok, 1)
                        if q == 0 and part.segs == 0:
                            if f_ == 0:
                                s5_angle()
                            if f_ == 2:
                                s5_powers()
                        if part.side:
                            j = js.side(2 * f_ + 1)
                            if f_ + 1 < SEG:
                                s5_b(i, f_ + 1)
                            done(j)
                            s5_lags(i, f_, j, lambda: read(j))
                    for k in range(KD):
                        j = js.down(k)
                        done(j)
                        g = 24 * q + 16 + k
                        ins = STT(x[:, k, 0:NL], lat(j), mod[:, g, 0:1], x[:, k, 0:NL], ALU.mult, ALU.add)
                        if n == NT:
                            ins = STT(x[:, k, NL:NT], ctx_(j)[:, 0:NC], mod[:, g, 1:2], x[:, k, NL:NT],
                                      ALU.mult, ALU.add)
                        ins.then_inc(slot_read[j % 4], 1)
                        if tiles == TAIL and k:
                            add_square(q + 1, k - 1, n)
                    if tiles == TAIL:
                        add_square(q + 1, KD - 1, n)
                    read(js.down(KD - 1))
                    assert not part.side or s5_n[0] == S5_LINKS

                for part in parts:
                    if part.reps == 1:
                        seg(part, 0)
                    else:
                        with dve.Fori(0, part.reps) as i:
                            seg(part, i)

            dve.wait_ge(silu_c, 1)
            for k in range(KD):
                ada_add(1, k)
                if k >= 2:
                    add_square(0, k - 2, NT)
            for k in range(KD - 2, KD):
                add_square(0, k, NT)
            s5_lambda()
            norm_root(JOB["norm0"], NT)
            for g in range(ADA_START):
                j = JOB[f"ada{g}"]
                is_done(dve, j)
                ada_bias(ada_cols(j), slice(KD * g, KD * g + KD)).then_inc(slot_read[j % 4], 1)
            was_read(dve, j)
            scale_cols(0, 72)
            norm(0, NT)
            ffn(JOB["ffn1"], PARTS1, NT, 0, 0)
            scale_cols(1, 80)
            scale_cols(2, 88)
            norm_root(JOB["norm1"], NT)
            norm(1, NT)
            for k in range(KD):
                ada_add(ADA_LAST, k)
            is_done(dve, JOB["ada8"])
            ada_bias(ada_cols(JOB["ada8"]), slice(KD * ADA_LAST, KD * ADA_LAST + KD)).then_inc(slot_read[JOB["ada8"] % 4], 1)

            for b in range(12, 16):
                was_read(dve, CJ["xs", b])

            def step(prev, cur, count, first=False):
                if not first:
                    dve.wait_ge(scan_step, count)
                TT(st1[:, :], prev, lam8[:, 0, :], ALU.mult).then_inc(scan_step, 1)
                TT(st2[0:64, :], prev[64:128, :], lam8[64:128, 1, :], ALU.mult).then_inc(scan_step, 1)
                TT(st2[64:128, :], prev[0:64, :], lam8[0:64, 1, :], ALU.mult).then_inc(scan_step, 1)
                dve.wait_ge(scan_step, count + 1)
                TT(cur, cur, st1[:, :], ALU.add).then_inc(scan_step, 1)
                dve.wait_ge(scan_step, count + 4)
                TT(cur, cur, st2[:, :], ALU.add).then_inc(scan_step, 1)

            def state(jj):
                return xs[:, bass.ds(jj, 1), :].rearrange("p a g -> p (a g)")

            step(xs[:, 0, :], xs[:, 1, :], 0, first=True)
            with dve.Fori(0, (NCH - 3) // 3) as i:
                for q in range(3):
                    step(state(i * 3 + (1 + q)), state(i * 3 + (2 + q)), i * 15 + (5 + 5 * q))
            dve.wait_ge(scan_step, 5 * (NCH - 2))
            is_done(dve, JOB["gb"] + 7)
            dve.tensor_copy(hb[:, :, :], xs[:, NC // CH - 1:NC // CH - 1 + LCH, G:DG][:, ::-1, :]).then_inc(states_ok, 1)
            dve.wait_ge(masks_ok, 3)
            for t in (tri[0:64, 0, 64:128], tri[64:128, 1, 0:64], kz[:, :, :], qz[:, :, :, :]):
                link(dve.memset(t, 0.0))

            def cumulate(p):
                ti, d = p // 2, p % 2
                j = GJ["z", p]
                gb_col = vt[:, 124 + 2 * d + ti:125 + 2 * d + ti]
                is_done(dve, j)
                dve.wait_ge(z_a, p + 1)
                link(TS(g_b[:, :].rearrange("p (b c) -> p b c", b=2), both(j, 384), gb_col, 0.0, ALU.add, ALU.min))
                dve.sem_inc(slot_read[j % 4], 1)
                link(TT(g_b[:, :], g_b[:, :], g_a[p % 2][:, :], ALU.subtract))
                step = 1 if d == 0 else -1
                link(dve.tensor_tensor_scan(g_c[:, ::step], zmask[:, :], g_b[:, ::step], 0.0, ALU.mult, ALU.add))
                gv = g_c[:, :].rearrange("p (c t) -> p c t", t=LC)
                ref, last = (LC // 2, LC - 1) if d == 0 else (LC // 2 - 1, 0)
                TT(g_b[:, 0:NL].rearrange("p (c t) -> p c t", t=LC), gv[:, 0:8, :],
                   gv[:, 0:8, ref:ref + 1].to_broadcast([P, 8, LC]), ALU.subtract)
                TT(g_d[:, :].rearrange("p (c t) -> p c t", t=LC), gv[:, :, last:last + 1].to_broadcast([P, 12, LC]),
                   gv, ALU.subtract).then_inc(z_d, 1)

            def decayed(p):
                ti, d = p // 2, p % 2
                dve.wait_ge(e_a, p + 1)
                TT(e1q[:, :], qt[:, ti, :], g_a[p % 2][:, 0:NL], ALU.mult)
                for hp in range(2):
                    r = slice(64 * hp, 64 * hp + 64)
                    TT(kz[r, hp, :], kt[r, ti, 0:NL], g_b[r, 0:NL], ALU.mult)
                TT(ke[:, :], kt[:, ti, :], g_d[:, :], ALU.mult).then_inc(e_d, 1)
                if p == 2:
                    is_done(dve, GJ["out", 1] + 3)
                for hp in range(2):
                    r = slice(64 * hp, 64 * hp + 64)
                    ins = TT(qz[r, d, hp, :], qt[r, ti, :], g_c[r, 0:NL], ALU.mult)
                link(ins)

            cumulate(0)
            decayed(0)
            is_done(dve, JOB["y"] + 7)
            link(dve.memset(at_sb[:, :, :, :, :], 0.0))
            for c in range(4):
                j = JOB["yt"] + c
                dve.wait_ge(yh_ok, c + 1)
                TT(y_lo[:, c, :], y32[:, c, :], y_hi[:, c, :].bitcast(F32), ALU.subtract).then_inc(yl_ok, 1)
                dve.sem_inc(slot_read[j % 4], 1)
            cumulate(1)
            for c in range(4):
                was_read(dve, JOB["glu"] + c)
                TT(y32[:, c, :], y32[:, c, :], gate_buf[:, c % 2, :], ALU.mult).then_inc(ya_ok, 1)
            for c in range(4):
                dve.wait_ge(glu_sig, c + 1)
                dve.wait_ge(ya_ok, 4)
                TT(ya_lo[:, c, :], y32[:, c, :], ya_hi[:, c, :].bitcast(F32), ALU.subtract).then_inc(yal_ok, 1)

            for p in range(4):
                d = p % 2
                if p:
                    decayed(p)
                if p in (1, 2):
                    cumulate(p + 1)
                for hp in range(2):
                    j = GJ["sc", p] + hp
                    is_done(dve, j)
                    dve.copy_predicated(at_sb[:, d, hp, :, :],
                                        tri[:, d, :].unsqueeze(1).to_broadcast([P, 4, P]).bitcast(I32),
                                        lat(j).rearrange("p (t c) -> p t c", t=4)).then_inc(slot_read[j % 4], 1)
                order = (4, 5, 0, 1, 2, 3) if d == 0 else (5, 4, 3, 2, 1, 0)
                nth = 0
                prev = None
                for half in range(2):
                    j = GJ["kv", p] + half
                    is_done(dve, j)
                    for q in range(3):
                        t = order[3 * half + q]
                        for par in ((0, 1) if d == 0 else (1, 0)):
                            c = 2 * t + par
                            kv = (lat, ctx_)[par](j)[:, P * q:P * q + P]
                            if nth < 3:
                                nxt = s_cur[:, d, nth % 2, :]
                            elif nth < 11:
                                nc_ = nth - 3
                                nxt = s_st[:, d, nc_ if d == 0 else 7 - nc_, :]
                            else:
                                nxt = None
                            if nth == 0:
                                link(dve.tensor_copy(nxt, kv))
                            elif nxt is not None:
                                link(STT(nxt, prev, decay[:, p % 2, c:c + 1], kv, ALU.mult, ALU.add))
                            prev = nxt
                            nth += 1
                    dve.sem_inc(slot_read[j % 4], 1)
                dve.sem_inc(s_ok, 1)
            dve.wait_ge(o_ok, 8)
            ov = o_sb[:, :, :].rearrange("p t (h e) -> p (t h) e", h=HEADS)
            link(TT(osq[:, :, :], o_sb[:, :, :], o_sb[:, :, :], ALU.mult))
            dve.tensor_reduce(oms[:, :], osq[:, :, :].rearrange("p t (h e) -> p (t h) e", h=HEADS), AX.X, ALU.add)\
                .then_inc(o_rs, 1)
            dve.wait_ge(o_rs, 2)
            link(dve.reciprocal(oms[:, :], oms[:, :]))
            TT(ov, ov, oms[:, :].unsqueeze(2).to_broadcast([P, 16, DV]), ALU.mult).then_inc(ybtok_ok, 1)
            def yb_low(c):
                dve.wait_ge(ybh_ok, c + 1)
                TT(yb_lo[:, c, :], r_sb[:, c, :], yb_hi[:, c, :].bitcast(F32), ALU.subtract).then_inc(yb_ok, 1)

            for c in range(4):
                j = JOB["ybt"] + c
                is_done(dve, j)
                STT(r_sb[:, c, :].rearrange("p (r w) -> p r w", w=GRID_W), lat(j).rearrange("p (w r) -> p r w", r=ROWS),
                    gn[:, c:c + 1], r_sb[:, c, :].rearrange("p (r w) -> p r w", w=GRID_W), ALU.mult, ALU.mult)\
                    .then_inc(slot_read[j % 4], 1)
                if c:
                    yb_low(c - 1)
            yb_low(3)

            def m_low(t):
                dve.wait_ge(mh_ok, t + 1)
                TT(m_lo[:, t, :], mt[:, t % 2, 2, :], m_hi[:, t, :].bitcast(F32), ALU.subtract).then_inc(m_ok, 1)

            for t in range(KD):
                jb = JOB["mb"] + t
                dve.wait_ge(gate_in[t % 2], 32 * (t // 2 + 1))
                was_read(dve, MA_JOB[t])
                if t >= 2:
                    dve.wait_ge(m_ok, t - 1)
                TT(mt[:, t % 2, 0, :], ma[:, t, :], gates[:, t % 2, 0, :], ALU.mult)
                is_done(dve, jb)
                TT(mt[:, t % 2, 1, :], lat(jb), gates[:, t % 2, 1, :], ALU.mult).then_inc(slot_read[jb % 4], 1)
                was_read(dve, jb)
                TT(mt[:, t % 2, 2, :], mt[:, t % 2, 0, :], mt[:, t % 2, 1, :], ALU.add).then_inc(m32_ok, 1)
                if t:
                    m_low(t - 1)
            m_low(KD - 1)
            dve.wait_ge(x_back, 16)
            for k in range(KD):
                j = JOB["wo"] + k
                is_done(dve, j)
                STT(x[:, k, 0:NL], lat(j), mod[:, 40 + k, 0:1], x[:, k, 0:NL], ALU.mult, ALU.add)\
                    .then_inc(slot_read[j % 4], 1)
                if k:
                    add_square(2, k - 1, NL)
            add_square(2, KD - 1, NL)
            norm_root(JOB["norm2"], NL)
            norm(2, NL)
            ffn(JOB["ffn2"], PARTS2, NL, 2, FF // P)
            norm_root(JOB["norm3"], NL)
            norm(3, NL)


_INS = ['x', 'c', 'ctx', 'c_ctx', 'ada_w', 'ada_b', 'ffn1_norm', 'ffn1_w_gate', 'ffn1_w_up', 'ffn1_w_down', 'mix_norm',
        'w_in', 's5_lambda_re', 's5_lambda_im', 's5_log_dt', 's5_b_re', 's5_b_im', 's5_c_re', 's5_c_im', 's5_d',
        's5_glu_w', 's5_glu_b', 's5_out', 'gla_gate_up', 'gla_gate_b', 'gla_norm', 'gla_out', 'w_o', 'ffn2_norm',
        'ffn2_w_gate', 'ffn2_w_up', 'ffn2_w_down', 'final_norm']


def kernel(**inputs):
    import numpy as _np
    import concourse.bacc as _bacc
    from concourse import mybir as _mybir
    from concourse.bass_utils import run_bass_kernel_spmd as _run

    nc = _bacc.Bacc("TRN2", target_bir_lowering=False, num_devices=1)
    arrays, args = {}, {}
    for name in _INS:
        v = _np.ascontiguousarray(inputs[name])
        arrays[f"in_{name}_dram"] = v
        args[name] = nc.dram_tensor(f"in_{name}_dram", v.shape, _mybir.dt.from_np(v.dtype), kind="ExternalInput").ap()
    out = nc.dram_tensor("out_0_dram", (1, NL, D), _mybir.dt.float32, kind="ExternalOutput").ap()
    build(nc, args, out)
    r = _run(nc, [arrays], core_ids=[0])
    return r.results[0]["out_0_dram"]
```
